# Optimizing a Trainium2 kernel written in Bass

```python
import math
import jax, jax.numpy as jnp
from jax import lax
import numpy as np
import jax
import jax.numpy as jnp

D_MODEL = 2048
BATCH = 1
SEQ = 256
DEPTH = 1

D_MIX = D_MODEL
D_POOL = D_MIX // 4
D_HYENA = 3 * D_MIX // 8
D_GMLP = D_MIX - D_POOL - D_HYENA
POOL_WINDOWS = (2, 4, 8, 16)
N_POOL_GROUPS = len(POOL_WINDOWS)
POOL_GROUP_DIM = D_POOL // N_POOL_GROUPS
HYENA_GROUP_DIM = 128
N_HYENA_GROUPS = D_HYENA // HYENA_GROUP_DIM
FILTER_BANDS = 16
FILTER_EMB = 1 + 2 * FILTER_BANDS
FILTER_HIDDEN = 64
DECAY_TARGET = 1e-2
FAST_DECAY_PCT = 0.3
SLOW_DECAY_PCT = 1.5
CHUNK = 128
GMLP_HEAD_DIM = 128
N_GMLP_HEADS = D_GMLP // GMLP_HEAD_DIM
D_IN_PROJ = D_POOL + 3 * D_HYENA + 2 * D_GMLP
D_FF = 5632
CONV_WIDTH = 3
RMS_EPS = 1e-6
LN_EPS = 1e-5


def rmsnorm(x, g):
    xf = x.astype(jnp.float32)
    y = xf * lax.rsqrt(jnp.mean(xf * xf, axis=-1, keepdims=True) + RMS_EPS)
    return (y * g.astype(jnp.float32)).astype(x.dtype)

def layernorm(x, g, b):
    xf = x.astype(jnp.float32)
    mu = jnp.mean(xf, axis=-1, keepdims=True)
    var = jnp.mean(jnp.square(xf - mu), axis=-1, keepdims=True)
    y = (xf - mu) * lax.rsqrt(var + LN_EPS)
    return (y * g.astype(jnp.float32) + b.astype(jnp.float32)).astype(x.dtype)

def dwconv3(x, w, b):
    L = x.shape[1]
    xp = jnp.pad(x, ((0, 0), (1, 1), (0, 0)))
    return xp[:, :L] * w[0] + xp[:, 1:L + 1] * w[1] + xp[:, 2:] * w[2] + b

def multiscale_pool_mixer(xa, w_pool, b_pool, scale):
    B, L, _ = xa.shape
    xf = xa.reshape(B, L, N_POOL_GROUPS, POOL_GROUP_DIM).astype(jnp.float32)
    csum = jnp.concatenate([jnp.zeros_like(xf[:, :1]), jnp.cumsum(xf, axis=1)], axis=1)
    t = np.arange(L)
    pooled = []
    for g, w in enumerate(POOL_WINDOWS):
        lo = np.maximum(t - w // 2, 0)
        hi = np.minimum(t + w // 2 - 1, L - 1)
        cnt = (hi - lo + 1).astype(np.float32)
        s = csum[:, hi + 1, g] - csum[:, lo, g]
        pooled.append(s / cnt[None, :, None])
    pooled = jnp.stack(pooled, axis=2)
    diff = (pooled - xf).astype(xa.dtype)
    y = jnp.einsum('blgc,gcd->blgd', diff, w_pool) + b_pool
    return y.reshape(B, L, D_POOL) * scale

def filter_features(L):
    t = jnp.linspace(0.0, 1.0, L, dtype=jnp.float32)[:, None]
    w = 2.0 * math.pi * jnp.arange(L, dtype=jnp.float32)[:, None] / L
    f = jnp.linspace(1e-4, FILTER_BANDS - 1, FILTER_BANDS, dtype=jnp.float32)[None, :]
    return jnp.concatenate([t, jnp.cos(f * w), -jnp.sin(f * w)], axis=-1), t

def implicit_filters(feat, t, w1, b1, fr1, w2, b2, fr2, w3):
    f32 = lambda a: a.astype(jnp.float32)
    h = jnp.sin(f32(fr1) * (feat @ f32(w1) + f32(b1)))
    h = jnp.sin(f32(fr2) * (h @ f32(w2) + f32(b2)))
    h = h @ f32(w3)
    deltas = jnp.linspace(math.log(DECAY_TARGET) / SLOW_DECAY_PCT,
                          math.log(DECAY_TARGET) / FAST_DECAY_PCT, D_HYENA, dtype=jnp.float32)
    decay = jnp.exp(-t * jnp.abs(deltas)[None, :])
    return h[:, :D_HYENA] * decay, h[:, D_HYENA:] * decay

def bidirectional_fftconv(z, h_fwd, h_bwd):
    B, L, C = z.shape
    k = jnp.concatenate([h_fwd, jnp.zeros((1, C), h_fwd.dtype), h_bwd[:0:-1]], axis=0)
    k_f = jnp.fft.rfft(k, n=2 * L, axis=0)
    z_f = jnp.fft.rfft(z.astype(jnp.float32), n=2 * L, axis=1)
    return jnp.fft.irfft(z_f * k_f[None], n=2 * L, axis=1)[:, :L]

def hyena_mixer(xb, short_w, short_b, h_fwd, h_bwd, d_skip):
    xs = dwconv3(xb, short_w, short_b)
    x0, x1, v = jnp.split(xs, 3, axis=-1)
    z = x1 * v
    y = bidirectional_fftconv(z, h_fwd, h_bwd).astype(z.dtype) + d_skip * z
    return x0 * y

def chunked_spatial_gating(xc, ln_g, ln_b, w_s, b_s):
    B, L, _ = xc.shape
    z = jax.nn.gelu(xc)
    u, v = jnp.split(z, 2, axis=-1)
    v = layernorm(v, ln_g, ln_b).reshape(B, L // CHUNK, CHUNK, N_GMLP_HEADS, GMLP_HEAD_DIM)
    g = jnp.einsum('bnpec,eqp->bnqec', v, w_s) + b_s.T[:, :, None]
    return u * g.reshape(B, L, D_GMLP)

def first_inputs(seed: int = 0) -> dict:
    key = jax.random.key(seed)
    ks = jax.random.split(key, 27)
    nrm = lambda k, shape, s: s * jax.random.normal(k, shape, jnp.float32)
    c = POOL_GROUP_DIM
    return {
        "x": nrm(ks[0], (BATCH, SEQ, D_MODEL), 1.0),
        "norm_mix": 1.0 + nrm(ks[1], (DEPTH, D_MODEL), 0.05),
        "w_in": nrm(ks[2], (DEPTH, D_MODEL, D_IN_PROJ), D_MODEL ** -0.5),
        "pool_w": nrm(ks[3], (DEPTH, N_POOL_GROUPS, c, c), c ** -0.5),
        "pool_b": nrm(ks[4], (DEPTH, N_POOL_GROUPS, c), 0.02),
        "pool_scale": 1.0 + nrm(ks[5], (DEPTH, D_POOL), 0.1),
        "hy_short_w": nrm(ks[6], (DEPTH, CONV_WIDTH, 3 * D_HYENA), 0.5),
        "hy_short_b": nrm(ks[7], (DEPTH, 3 * D_HYENA), 0.02),
        "hy_filt_w1": nrm(ks[8], (DEPTH, FILTER_EMB, FILTER_HIDDEN), FILTER_EMB ** -0.5),
        "hy_filt_b1": nrm(ks[9], (DEPTH, FILTER_HIDDEN), 0.5),
        "hy_filt_freq1": 1.0 + nrm(ks[10], (DEPTH, FILTER_HIDDEN), 0.1),
        "hy_filt_w2": nrm(ks[11], (DEPTH, FILTER_HIDDEN, FILTER_HIDDEN), FILTER_HIDDEN ** -0.5),
        "hy_filt_b2": nrm(ks[12], (DEPTH, FILTER_HIDDEN), 0.5),
        "hy_filt_freq2": 1.0 + nrm(ks[13], (DEPTH, FILTER_HIDDEN), 0.1),
        "hy_filt_w3": nrm(ks[14], (DEPTH, FILTER_HIDDEN, 2 * D_HYENA), 0.005),
        "hy_skip": nrm(ks[15], (DEPTH, D_HYENA), 0.5),
        "gm_ln_g": 1.0 + nrm(ks[16], (DEPTH, D_GMLP), 0.05),
        "gm_ln_b": nrm(ks[17], (DEPTH, D_GMLP), 0.02),
        "gm_w_s": nrm(ks[18], (DEPTH, N_GMLP_HEADS, CHUNK, CHUNK), CHUNK ** -0.5),
        "gm_b_s": 1.0 + nrm(ks[19], (DEPTH, N_GMLP_HEADS, CHUNK), 0.1),
        "w_out": nrm(ks[20], (DEPTH, D_MIX, D_MODEL), D_MIX ** -0.5),
        "norm_ffn": 1.0 + nrm(ks[21], (DEPTH, D_MODEL), 0.05),
        "ffn_w_up": nrm(ks[22], (DEPTH, D_MODEL, 2 * D_FF), D_MODEL ** -0.5),
        "ffn_conv_w": nrm(ks[23], (DEPTH, CONV_WIDTH, 2 * D_FF), 0.5),
        "ffn_conv_b": nrm(ks[24], (DEPTH, 2 * D_FF), 0.02),
        "ffn_w_down": nrm(ks[25], (DEPTH, D_FF, D_MODEL), D_FF ** -0.5),
        "norm_final": 1.0 + nrm(ks[26], (D_MODEL,), 0.05),
    }

def first_block(x, norm_mix, w_in, pool_w, pool_b, pool_scale, hy_short_w, hy_short_b,
              hy_filt_w1, hy_filt_b1, hy_filt_freq1, hy_filt_w2, hy_filt_b2, hy_filt_freq2,
              hy_filt_w3, hy_skip, gm_ln_g, gm_ln_b, gm_w_s, gm_b_s, w_out, norm_ffn,
              ffn_w_up, ffn_conv_w, ffn_conv_b, ffn_w_down, norm_final):
    L = x.shape[1]
    feat, t = filter_features(L)
    a_end = D_POOL
    b_end = D_POOL + 3 * D_HYENA
    for i in range(DEPTH):
        h = rmsnorm(x, norm_mix[i])
        p = h @ w_in[i]
        y_a = multiscale_pool_mixer(p[..., :a_end], pool_w[i], pool_b[i], pool_scale[i])
        h_fwd, h_bwd = implicit_filters(feat, t, hy_filt_w1[i], hy_filt_b1[i], hy_filt_freq1[i],
                                        hy_filt_w2[i], hy_filt_b2[i], hy_filt_freq2[i], hy_filt_w3[i])
        y_b = hyena_mixer(p[..., a_end:b_end], hy_short_w[i], hy_short_b[i], h_fwd, h_bwd, hy_skip[i])
        y_c = chunked_spatial_gating(p[..., b_end:], gm_ln_g[i], gm_ln_b[i], gm_w_s[i], gm_b_s[i])
        x = x + jnp.concatenate([y_a, y_b, y_c], axis=-1) @ w_out[i]
        h = rmsnorm(x, norm_ffn[i])
        up = dwconv3(h @ ffn_w_up[i], ffn_conv_w[i], ffn_conv_b[i])
        gate, val = jnp.split(up, 2, axis=-1)
        x = x + (jax.nn.silu(gate) * val) @ ffn_w_down[i]
    return rmsnorm(x, norm_final)


CHUNK_2 = 64
N_MEM = 256
NORM_EPS = 1e-6
NEG_INF = -1e30

A_HEADS = 8
A_HEAD_DIM = 128
A_WIDTH = A_HEADS * A_HEAD_DIM
A_LEFT_CHUNKS = 8
A_BAND = (A_LEFT_CHUNKS + 1) * CHUNK_2
REL_CLIP = 128

B_HEADS = 16
B_HEAD_DIM = 64
B_WIDTH = B_HEADS * B_HEAD_DIM
DECAY_LORA = 64
ICLR_LORA = 64
GN_EPS = 64e-5

C_HEADS = 4
C_HEAD_DIM = 256
C_WIDTH = C_HEADS * C_HEAD_DIM

IN_SPLITS = (A_WIDTH,) * 4 + (B_WIDTH,) * 4 + (DECAY_LORA, ICLR_LORA) + (C_WIDTH,) * 2 + (D_MODEL,) * 3
IN_COLS = sum(IN_SPLITS)


def rms_norm(x, g):
    xf = x.astype(jnp.float32)
    y = xf * lax.rsqrt(jnp.mean(xf * xf, axis=-1, keepdims=True) + NORM_EPS)
    return (y * g.astype(jnp.float32)).astype(x.dtype)

def _rel_index():
    r = np.arange(CHUNK_2)[:, None]
    m = np.arange(A_BAND)[None, :]
    dist = r + A_LEFT_CHUNKS * CHUNK_2 - m
    return np.clip(dist, -REL_CLIP, REL_CLIP) + REL_CLIP

def chunked_band_attention(q, k, v, rel_bias):
    bsz, s, h, dh = q.shape
    n_chunks = s // CHUNK_2
    pad = A_LEFT_CHUNKS * CHUNK_2
    kp = jnp.pad(k, ((0, 0), (pad, 0), (0, 0), (0, 0)))
    vp = jnp.pad(v, ((0, 0), (pad, 0), (0, 0), (0, 0)))
    bias = rel_bias[:, _rel_index()].astype(jnp.float32)
    band_pos = jnp.arange(A_BAND) - pad
    scale = dh ** -0.5

    def one_chunk(c):
        start = c * CHUNK_2
        qc = lax.dynamic_slice_in_dim(q, start, CHUNK_2, axis=1)
        kc = lax.dynamic_slice_in_dim(kp, start, A_BAND, axis=1)
        vc = lax.dynamic_slice_in_dim(vp, start, A_BAND, axis=1)
        sc = jnp.einsum('bqhd,bkhd->bhqk', qc, kc, preferred_element_type=jnp.float32) * scale + bias
        valid = (start + band_pos) >= 0
        sc = jnp.where(valid[None, None, None, :], sc, NEG_INF)
        p = jax.nn.softmax(sc, axis=-1)
        return jnp.einsum('bhqk,bkhd->bqhd', p.astype(vc.dtype), vc)

    out = lax.map(one_chunk, jnp.arange(n_chunks))
    return jnp.transpose(out, (1, 0, 2, 3, 4)).reshape(bsz, s, h * dh)

def token_shift_lerp(p, mu):
    prev = jnp.pad(p, ((0, 0), (1, 0), (0, 0)))[:, :-1]
    return p + mu * (prev - p)

def rwkv7_scan(r, decay, k, v, a_vec, b_vec):
    bsz, _, h, n = r.shape

    def step(state, inp):
        r_t, w_t, k_t, v_t, a_t, b_t = inp
        sa = jnp.einsum('bhij,bhj->bhi', state, a_t)
        state = state * w_t[:, :, None, :] + sa[..., None] * b_t[:, :, None, :] + v_t[..., None] * k_t[:, :, None, :]
        return state, jnp.einsum('bhij,bhj->bhi', state, r_t)

    xs = tuple(jnp.moveaxis(t, 1, 0) for t in (r, decay, k, v, a_vec, b_vec))
    s0 = jnp.zeros((bsz, h, n, n), jnp.float32)
    _, out = lax.scan(step, s0, xs)
    return jnp.moveaxis(out, 0, 1)

def rwkv7_time_mix(p_r, p_k, p_v, p_wd, p_ad, mu_rkv, mu_w, mu_a, w0, w2, a0, a2, k_k, k_a, r_k, ln_w, ln_b):
    f = lambda t: t.astype(jnp.float32)
    p_r, p_k, p_v, p_wd, p_ad = f(p_r), f(p_k), f(p_v), f(p_wd), f(p_ad)
    bsz, s, _ = p_r.shape
    r = token_shift_lerp(p_r, f(mu_rkv[0]))
    k = token_shift_lerp(p_k, f(mu_rkv[1]))
    v = token_shift_lerp(p_v, f(mu_rkv[2]))
    wd = token_shift_lerp(p_wd, f(mu_w))
    ad = token_shift_lerp(p_ad, f(mu_a))
    w = -jax.nn.softplus(-(f(w0) + jnp.tanh(wd) @ f(w2))) - 0.5
    decay = jnp.exp(-jnp.exp(w))
    a = jax.nn.sigmoid(f(a0) + ad @ f(a2))
    heads = lambda t: t.reshape(bsz, s, B_HEADS, B_HEAD_DIM)
    kk = heads(k * f(k_k))
    kk = kk * lax.rsqrt(jnp.maximum(jnp.sum(kk * kk, axis=-1, keepdims=True), 1e-24))
    k = k * (1.0 + (a - 1.0) * f(k_a))
    rh, kh, vh, ah, dh = heads(r), heads(k), heads(v), heads(a), heads(decay)
    o = rwkv7_scan(rh, dh, kh, vh, -kk, kk * ah)
    mean = jnp.mean(o, axis=-1, keepdims=True)
    var = jnp.mean(jnp.square(o - mean), axis=-1, keepdims=True)
    o = ((o - mean) * lax.rsqrt(var + GN_EPS)).reshape(bsz, s, B_WIDTH) * f(ln_w) + f(ln_b)
    bonus = jnp.sum(rh * kh * f(r_k), axis=-1, keepdims=True) * vh
    return o + bonus.reshape(bsz, s, B_WIDTH)

def memory_cross_attention(q, mk, mv):
    bsz, s, h, dh = q.shape
    sc = jnp.einsum('bshd,bmhd->bhsm', q, mk, preferred_element_type=jnp.float32) * (dh ** -0.5)
    p = jax.nn.softmax(sc, axis=-1)
    out = jnp.einsum('bhsm,bmhd->bshd', p.astype(mv.dtype), mv)
    return out.reshape(bsz, s, h * dh)

def hybrid_layer(x, mem, norm_g, w_in, a_q_g, a_k_g, a_rel_bias, w_up_a,
                 b_mu_rkv, b_mu_w, b_mu_a, b_w0, b_w2, b_a0, b_a2, b_k_k, b_k_a, b_r_k,
                 b_ln_w, b_ln_b, w_up_b, mem_norm_g, w_mem_kv, c_q_g, c_k_g, w_up_c, w_o):
    bsz, s, _ = x.shape
    h = rms_norm(x, norm_g)
    proj = h @ w_in
    offsets = np.cumsum(np.array(IN_SPLITS))[:-1].tolist()
    (aq, ak, av, az, br, bk, bv, bz, bwd, bad, cq, cz, ga, gb, gc) = jnp.split(proj, offsets, axis=-1)

    aq = rms_norm(aq.reshape(bsz, s, A_HEADS, A_HEAD_DIM), a_q_g)
    ak = rms_norm(ak.reshape(bsz, s, A_HEADS, A_HEAD_DIM), a_k_g)
    av = av.reshape(bsz, s, A_HEADS, A_HEAD_DIM)
    ya = chunked_band_attention(aq, ak, av, a_rel_bias) * jax.nn.silu(az)

    yb = rwkv7_time_mix(br, bk, bv, bwd, bad, b_mu_rkv, b_mu_w, b_mu_a, b_w0, b_w2, b_a0, b_a2,
                        b_k_k, b_k_a, b_r_k, b_ln_w, b_ln_b).astype(x.dtype) * jax.nn.silu(bz)

    m = rms_norm(mem, mem_norm_g)
    mk, mv = jnp.split(m @ w_mem_kv, 2, axis=-1)
    mk = rms_norm(mk.reshape(bsz, N_MEM, C_HEADS, C_HEAD_DIM), c_k_g)
    mv = mv.reshape(bsz, N_MEM, C_HEADS, C_HEAD_DIM)
    cq = rms_norm(cq.reshape(bsz, s, C_HEADS, C_HEAD_DIM), c_q_g)
    yc = memory_cross_attention(cq, mk, mv) * jax.nn.silu(cz)

    merged = (jax.nn.sigmoid(ga) * (ya @ w_up_a)
              + jax.nn.sigmoid(gb) * (yb @ w_up_b)
              + jax.nn.sigmoid(gc) * (yc @ w_up_c))
    return x + merged @ w_o

def second_inputs(seed: int = 0) -> dict:
    key = jax.random.key(seed)
    ks = jax.random.split(key, 32)
    nrm = lambda k, shape, sc: jax.random.normal(k, shape, jnp.float32) * sc
    L = DEPTH
    return {
        "x": nrm(ks[0], (BATCH, SEQ, D_MODEL), 1.0),
        "mem": nrm(ks[1], (BATCH, N_MEM, D_MODEL), 1.0),
        "norm_g": 1.0 + nrm(ks[2], (L, D_MODEL), 0.1),
        "w_in": nrm(ks[3], (L, D_MODEL, IN_COLS), D_MODEL ** -0.5),
        "a_q_g": 1.0 + nrm(ks[4], (L, A_HEAD_DIM), 0.1),
        "a_k_g": 1.0 + nrm(ks[5], (L, A_HEAD_DIM), 0.1),
        "a_rel_bias": nrm(ks[6], (L, A_HEADS, 2 * REL_CLIP + 1), 0.5),
        "w_up_a": nrm(ks[7], (L, A_WIDTH, D_MODEL), A_WIDTH ** -0.5),
        "b_mu_rkv": jax.random.uniform(ks[8], (L, 3, B_WIDTH), jnp.float32),
        "b_mu_w": jax.random.uniform(ks[9], (L, DECAY_LORA), jnp.float32),
        "b_mu_a": jax.random.uniform(ks[10], (L, ICLR_LORA), jnp.float32),
        "b_w0": jax.random.uniform(ks[11], (L, B_WIDTH), jnp.float32, minval=-3.0, maxval=0.5),
        "b_w2": nrm(ks[12], (L, DECAY_LORA, B_WIDTH), 0.1),
        "b_a0": nrm(ks[13], (L, B_WIDTH), 0.5),
        "b_a2": nrm(ks[14], (L, ICLR_LORA, B_WIDTH), 0.1),
        "b_k_k": 0.85 + nrm(ks[15], (L, B_WIDTH), 0.05),
        "b_k_a": 1.0 + nrm(ks[16], (L, B_WIDTH), 0.05),
        "b_r_k": nrm(ks[17], (L, B_HEADS, B_HEAD_DIM), 0.1),
        "b_ln_w": 1.0 + nrm(ks[18], (L, B_WIDTH), 0.1),
        "b_ln_b": nrm(ks[19], (L, B_WIDTH), 0.02),
        "w_up_b": nrm(ks[20], (L, B_WIDTH, D_MODEL), B_WIDTH ** -0.5),
        "mem_norm_g": 1.0 + nrm(ks[21], (L, D_MODEL), 0.1),
        "w_mem_kv": nrm(ks[22], (L, D_MODEL, 2 * C_WIDTH), D_MODEL ** -0.5),
        "c_q_g": 1.0 + nrm(ks[23], (L, C_HEAD_DIM), 0.1),
        "c_k_g": 1.0 + nrm(ks[24], (L, C_HEAD_DIM), 0.1),
        "w_up_c": nrm(ks[25], (L, C_WIDTH, D_MODEL), C_WIDTH ** -0.5),
        "w_o": nrm(ks[26], (L, D_MODEL, D_MODEL), D_MODEL ** -0.5),
    }

def second_block(x, mem, norm_g, w_in, a_q_g, a_k_g, a_rel_bias, w_up_a,
              b_mu_rkv, b_mu_w, b_mu_a, b_w0, b_w2, b_a0, b_a2, b_k_k, b_k_a, b_r_k,
              b_ln_w, b_ln_b, w_up_b, mem_norm_g, w_mem_kv, c_q_g, c_k_g, w_up_c, w_o):
    for l in range(DEPTH):
        x = hybrid_layer(x, mem, norm_g[l], w_in[l], a_q_g[l], a_k_g[l], a_rel_bias[l], w_up_a[l],
                         b_mu_rkv[l], b_mu_w[l], b_mu_a[l], b_w0[l], b_w2[l], b_a0[l], b_a2[l],
                         b_k_k[l], b_k_a[l], b_r_k[l], b_ln_w[l], b_ln_b[l], w_up_b[l],
                         mem_norm_g[l], w_mem_kv[l], c_q_g[l], c_k_g[l], w_up_c[l], w_o[l])
    return x


def setup_inputs(seed=0):
    out = dict(first_inputs(seed))
    for name, value in second_inputs(seed + 1).items():
        if name != "x":
            out[name + "_2"] = value
    return out


def reference(
    x, norm_mix, w_in, pool_w, pool_b, pool_scale, hy_short_w, hy_short_b, hy_filt_w1,
    hy_filt_b1, hy_filt_freq1, hy_filt_w2, hy_filt_b2, hy_filt_freq2, hy_filt_w3, hy_skip,
    gm_ln_g, gm_ln_b, gm_w_s, gm_b_s, w_out, norm_ffn, ffn_w_up, ffn_conv_w, ffn_conv_b,
    ffn_w_down, norm_final, mem_2, norm_g_2, w_in_2, a_q_g_2, a_k_g_2, a_rel_bias_2, w_up_a_2,
    b_mu_rkv_2, b_mu_w_2, b_mu_a_2, b_w0_2, b_w2_2, b_a0_2, b_a2_2, b_k_k_2, b_k_a_2, b_r_k_2,
    b_ln_w_2, b_ln_b_2, w_up_b_2, mem_norm_g_2, w_mem_kv_2, c_q_g_2, c_k_g_2, w_up_c_2, w_o_2,
):
    x = first_block(
        x, norm_mix, w_in, pool_w, pool_b, pool_scale, hy_short_w, hy_short_b, hy_filt_w1,
        hy_filt_b1, hy_filt_freq1, hy_filt_w2, hy_filt_b2, hy_filt_freq2, hy_filt_w3, hy_skip,
        gm_ln_g, gm_ln_b, gm_w_s, gm_b_s, w_out, norm_ffn, ffn_w_up, ffn_conv_w, ffn_conv_b,
        ffn_w_down, norm_final,
    )
    return second_block(
        x, mem_2, norm_g_2, w_in_2, a_q_g_2, a_k_g_2, a_rel_bias_2, w_up_a_2, b_mu_rkv_2,
        b_mu_w_2, b_mu_a_2, b_w0_2, b_w2_2, b_a0_2, b_a2_2, b_k_k_2, b_k_a_2, b_r_k_2, b_ln_w_2,
        b_ln_b_2, w_up_b_2, mem_norm_g_2, w_mem_kv_2, c_q_g_2, c_k_g_2, w_up_c_2, w_o_2,
    )


_drawn_inputs = setup_inputs


def setup_inputs(seed=0):
    import zlib

    import numpy as np

    out = dict(_drawn_inputs(seed))
    spreads = {}
    factors = {'pool_b': 5.084,
     'hy_short_b': 6.621,
     'hy_filt_freq1': 8.0,
     'hy_filt_freq2': 8.0,
     'gm_ln_g': 2.891,
     'gm_ln_b': 7.042,
     'ffn_conv_b': 4.235,
     'a_q_g_2': 8.0,
     'a_k_g_2': 8.0,
     'b_mu_w_2': 64.0,
     'b_k_k_2': 64.0,
     'b_k_a_2': 12.271,
     'b_ln_b_2': 22.113,
     'mem_norm_g_2': 8.0,
     'c_q_g_2': 8.0,
     'c_k_g_2': 8.0,
     'a_rel_bias_2': 8.0,
     'b_w2_2': 5.691,
     'b_ln_w_2': 4.678}
    for name, (base, spread) in spreads.items():
        noise = np.random.default_rng([zlib.crc32(name.encode()), seed]).standard_normal(out[name].shape)
        drawn = base * np.exp(spread * noise) if base else spread * noise
        out[name] = jnp.asarray(drawn.astype(out[name].dtype))
    for name, factor in factors.items():
        out[name] = (out[name] * factor).astype(out[name].dtype)
    return out
```

```python
from contextlib import ExitStack, contextmanager
from itertools import count

import numpy as np

import concourse.bass as bass
from concourse import mybir

ALU = mybir.AluOpType
ACT = mybir.ActivationFunctionType
F32 = mybir.dt.float32
F32R = mybir.dt.float32r
AX_X = mybir.AxisListType.X

P = 128
T = 256
D = 2048
KT = D // P
HY = 6
D_HY = HY * P
FF_TILES = 5632 // P
FF_HALF = FF_TILES // 2
CHUNK = 64
NCH = T // CHUNK
HEADS_A = 8
HEADS_C = 4
SUB = 8
NEG = -1e30
TWO_PI = 2.0 * np.pi
ROUND = float(1.5 * 2 ** 23)
PI_HI = 6.28125
PI_LO = float(np.float32(TWO_PI - PI_HI))
PI_CUT = 3.1415925

RING = 4
UK = 4
UN = 256

U_IN = 17 * 4
U_OUT = 8 * 4
U_UP = FF_HALF * 4
U_DOWN = 4 * 11
U_LORA = 4
U_RA = HEADS_A * 16
U_MEM = 8 * 4
U_C = HEADS_C * 8
U_MERGE = 8 * 18
UNITS = U_IN + U_OUT + 2 * (U_UP + U_DOWN) + U_LORA + U_RA + U_MEM + U_C + U_MERGE + U_OUT

PARAMS = [("norm_mix", 16), ("pool_b", 4), ("pool_scale", 4), ("hy_w", 54), ("hy_b", 18), ("hy_skip", 6),
          ("gm_g", 6), ("gm_b", 6), ("norm_ffn", 16), ("ffn", 8 * FF_TILES), ("norm_final", 16),
          ("norm_g", 16), ("mem_g", 16), ("rwkv", 80), ("mu_wa", 1), ("w0", 8), ("a0", 8), ("aq_g", 1),
          ("ak_g", 1), ("cq_g", 2), ("ck_g", 2), ("f_b1", 1), ("f_fr1", 1), ("f_b2", 1), ("f_fr2", 1)]
COL = {}
_at = 0
for _name, _n in PARAMS:
    COL[_name] = _at
    _at += _n
NPAR = _at
MU_R, MU_K, MU_V, K_K, K_A, R_K, LN_W, LN_B, RW_COLS = 0, 1, 2, 3, 4, 5, 6, 7, 10

CONSTS = [("ident", 128), ("upper", 128), ("upper_in", 128), ("lower_in", 128), ("lower_out", 128),
          ("upper_eq", 64), ("ones", 128), ("head_ones", 128), ("center", 128), ("eps6", 1), ("eps5", 1),
          ("eps_gn", 1)]
CC = {}
_at = 0
for _name, _n in CONSTS:
    CC[_name] = (_at, _n)
    _at += _n
NCONST = _at


def const_tables():
    r = np.arange(P)[:, None]
    c = np.arange(P)[None, :]
    same = (r // 64) == (c // 64)
    block = (r // SUB) == (c // SUB)
    eye = (r == c)
    parts = {
        "ident": eye, "upper": same & (r < c), "upper_in": block & (r < c), "lower_in": block & (r > c),
        "lower_out": same & (r > c) & ~block, "upper_eq": (r % 64) <= np.arange(64)[None, :],
        "ones": np.ones((P, P)), "head_ones": same, "center": eye - same / 64.0,
        "eps6": np.full((P, 1), 1e-6), "eps5": np.full((P, 1), 1e-5), "eps_gn": np.full((P, 1), 64e-5),
    }
    return np.concatenate([parts[n].astype(np.float32) for n, _ in CONSTS], axis=1)


def hyena_tables():
    f32 = np.float32
    t = np.arange(T)
    theta = 2.0 * np.pi / (2 * T) * (np.arange(T) + 0.5)
    ang = t[:, None] * theta[None, :]
    cos, sin = np.cos(ang), np.sin(ang)
    tables = np.stack([cos, sin, cos.T / T, sin.T / T]).astype(f32)
    tables = tables.reshape(4, 2, P, T).transpose(2, 0, 1, 3)
    tt = np.linspace(0.0, 1.0, T, dtype=f32)[:, None]
    w = (2.0 * np.pi * np.arange(T)[:, None] / T).astype(f32)
    f = np.linspace(1e-4, 15, 16, dtype=f32)[None, :]
    fw = (f * w).astype(np.float64)
    feat = np.concatenate([tt, np.cos(fw), -np.sin(fw)], axis=-1).astype(f32)
    lo = np.log(1e-2)
    deltas = np.linspace(lo / 1.5, lo / 0.3, D_HY, dtype=f32)
    decay = np.exp(-(tt * np.abs(deltas)[None, :]).astype(np.float64)).astype(f32)
    decay = decay.reshape(2, P, D_HY).transpose(1, 0, 2)
    inv = np.zeros((4, T), f32)
    for g, win in enumerate((2, 4, 8, 16)):
        a = np.maximum(t - win // 2, 0)
        b = np.minimum(t + win // 2 - 1, T - 1)
        inv[g] = 1.0 / (b - a + 1)
    return tables, feat.T, decay, np.broadcast_to(inv, (P, 4, T))


class Counts:

    def __init__(self, eng):
        self.eng = eng
        self.base = {}
        self.extra = {}

    def next(self, key, by=1):
        self.extra[key] = self.extra.get(key, 0) + by
        return self.now(key)

    def now(self, key):
        return self.base.get(key, 0) + self.extra.get(key, 0)

    @contextmanager
    def loop(self, n, per):
        base, extra = self.base, self.extra
        keys = set(base) | set(extra) | set(per)
        before = {k: base.get(k, 0) + extra.get(k, 0) for k in keys}
        self.base, self.extra = {}, {}
        with self.eng.Fori(0, n) as i:
            for k in keys:
                self.base[k] = before[k] + i * per[k] if k in per else before[k]
            yield i
            moved = {k: v for k, v in self.extra.items() if v}
            assert moved == per, f"one iteration moves {moved}"
        self.base = base
        self.extra = {k: extra.get(k, 0) + n * per.get(k, 0) for k in keys}


def build(nc, a):
    out_ap = a["out"]
    with ExitStack() as ctx:
        def sb(name, shape, dt=F32):
            return ctx.enter_context(nc.sbuf_tensor(name, shape, dt))

        def sem(name):
            return ctx.enter_context(nc.semaphore(name))

        banks = [ctx.enter_context(nc.psum_tensor(f"bank{i}", [P, 512], F32)) for i in range(8)]

        raw = [sb(f"raw{i}", [P, UK, UN]) for i in range(RING)]
        w_hi = [sb(f"w_hi{i}", [P, UK, UN], F32R) for i in range(RING)]
        w_lo = [sb(f"w_lo{i}", [P, UK, UN], F32R) for i in range(RING)]
        x = sb("x", [P, KT, T])
        h_hi = sb("h_hi", [P, KT, T], F32R)
        h_lo = sb("h_lo", [P, KT, T], F32R)
        par = sb("par", [P, NPAR])
        con = sb("con", [P, NCONST])
        arena_at = nc.sbuf_base
        arena_at = (arena_at + 31) // 32 * 32
        usable = nc.sbuf_usable_end - arena_at

        placed = {}

        def place(name, shape, at, dt=F32):
            size = 4 * int(np.prod(shape[1:]))
            assert at + size <= usable, (name, at + size, usable)
            placed[name] = at + size
            return nc.alloc_sbuf_tensor_at(name, shape, dt, offset=arena_at + at)

        K = 1024
        y_hi = place("y_hi", [P, KT, T], 0, F32R)
        y_lo = place("y_lo", [P, KT, T], 16 * K, F32R)
        scratch = place("scratch", [P, KT, T], 0)
        root = place("root", [P, T], 103 * K)
        x0 = place("x0", [P, HY, T], 32 * K)
        z1 = place("z1", [P, HY, T], 38 * K)
        zv = place("zv", [P, HY, T], 44 * K)
        k_re = place("k_re", [P, 2, D_HY], 50 * K)
        k_im = place("k_im", [P, 2, D_HY], 56 * K)
        dft = place("dft", [P, 4, 2, T], 62 * K)
        decay = place("decay", [P, 2, D_HY], 70 * K)
        f_fwd = place("f_fwd", [P, 2, D_HY], 76 * K)
        f_bwd = place("f_bwd", [P, 2, D_HY], 82 * K)
        f_sum = place("f_sum", [P, 2, D_HY], 88 * K)
        feat = place("feat", [33, T], 94 * K)
        fw1 = place("fw1", [33, 64], 95 * K)
        fw2 = place("fw2", [64, 64], 95 * K + 256)
        fh = [place(f"fh{i}", [64, T], (96 + i) * K) for i in range(4)]
        fw3 = place("fw3", [64, 2 * D_HY], 16 * K)
        gv = place("gv", [P, HY, T], 70 * K)
        gu = place("gu", [P, HY, T], 76 * K)
        gsq = place("gsq", [P, HY, T], 82 * K)
        gvt = place("gvt", [P, 2, D_HY], 82 * K)
        zt = place("zt", [P, 2, D_HY], 88 * K)
        ws = place("ws", [P, HY, P], 94 * K)
        pw = place("pw", [P, 4, P], 97 * K)
        bs = place("bs", [1, HY * P], 99 * K)
        prod = [place(f"prod{i}", [P, 384], (38 + 6) * K + 1536 * i) for i in range(4)]
        mix = place("mix", [P, 2, T], 44 * K)
        PW = 272
        pool_x = place("pool_x", [P, 4, PW], 50 * K)
        pool_a = place("pool_a", [P, 4, PW], 50 * K + 4352)
        pool_b = place("pool_b", [P, 4, PW], 50 * K + 2 * 4352)
        inv = place("inv", [P, 4, T], 64 * K)
        pool_d = place("pool_d", [P, 4, T], 32 * K)
        y_part = place("y_part", [P, 4, T], 88 * K)
        m_hi = place("m_hi", [P, FF_HALF, T], 0, F32R)
        m_lo = place("m_lo", [P, FF_HALF, T], 22 * K, F32R)
        scratch2 = place("scratch2", [P, KT, T], 46 * K)
        conv_o = place("conv_o", [P, 2, 2, T], 62 * K)
        conv_m = place("conv_m", [P, 2, T], 66 * K)
        root2 = place("root2", [P, T], 70 * K)
        yall = place("yall", [P, 24, T], 0)
        cum = place("cum", [P, 8, T], 24 * K)
        icl = place("icl", [P, 8, T], 32 * K)
        bd = {}
        at = 40 * K
        for n in ("a", "b", "k", "v", "Nt", "N", "No", "Kt", "Q", "F", "Vt", "At", "Bt", "Kk", "b1", "b2",
                  "b3", "AkV", "Y"):
            bd[n] = place("m_" + n, [P, NCH, P], at)
            at += 2 * K
        BK = place("m_BK", [P, 2, NCH, CHUNK], at)
        at += 2 * K
        small = {}
        small_at = {}
        for n, w in (("pr", 257), ("pk", 257), ("pv", 257), ("t0", 256), ("r", 256), ("k0", 256), ("v", 256),
                     ("k2", 256), ("kk", 256), ("sq", 256), ("rk", 256), ("bz", 256), ("ep", 260), ("en", 256),
                     ("rt", 256), ("bon", 256)):
            small[n] = place("s_" + n, [P, w], at)
            small_at[n] = at
            at += (4 * w + 31) // 32 * 32
        S = place("S", [P, 2, P], at)
        SA = place("SA", [P, P], at + 1024)
        S_dec = place("S_dec", [P, P], at + 1536)
        at += 2048
        qk = place("qk", [P, 2, T], at)
        qr = place("qr", [P, 2, T], at + 2048)
        az = place("az", [P, T], at + 4096)
        bias_t = place("bias_t", [P, 384], at + 5120)
        stat = place("stat", [P, 16], at + 6656)
        prt = place("prt", [P, 384], at + 2048)
        av_t = place("av_t", [P, 2, P], small_at["rk"])
        prb = place("prb", [P, 384], small_at["k2"])
        lora = place("lora", [P, 1024], 40 * K)
        lx = place("lx", [P, 257], 44 * K)
        lt = place("lt", [P, T], 46 * K)
        ping = place("ping", [P, 8, T], 48 * K)
        memx = place("memx", [P, KT, T], 24 * K)
        scratch3 = place("scratch3", [P, KT, T], 72 * K)
        mh_hi = place("mh_hi", [P, KT, T], 40 * K, F32R)
        mh_lo = place("mh_lo", [P, KT, T], 56 * K, F32R)
        mk = place("mk", [P, 8, T], 72 * K)
        mvt = place("mvt", [P, 2, 8 * P], 80 * K)
        cpair = place("cpair", [P, 2, T], 88 * K)
        csq = place("csq", [P, 2, T], 90 * K)
        cg = place("cg", [P, 2, T], 92 * K)
        cp = place("cp", [P, 2, T], 94 * K)
        cpt = place("cpt", [P, 2, T], 96 * K)
        mvh = place("mvh", [P, 2, T], 98 * K)
        cstat = place("cstat", [P, 16], 100 * K)
        croot = place("croot", [P, T], 101 * K)
        ya_hi = place("ya_hi", [P, 24, T], 24 * K, F32R)
        ya_lo = place("ya_lo", [P, 24, T], 48 * K, F32R)
        gate = place("gate", [P, 2, T], 72 * K)
        macc = place("macc", [P, 2, T], 74 * K)
        mtmp = place("mtmp", [P, 2, T], 76 * K)
        mg_hi = place("mg_hi", [P, KT, T], 78 * K, F32R)
        mg_lo = place("mg_lo", [P, KT, T], 0, F32R)
        obuf = place("obuf", [P, KT, T], 24 * K)

        landed = [sem(f"unit_landed{i}") for i in range(RING)]
        hi_done = sem("hi_done")
        split_done = sem("split_done")
        unit_used = sem("unit_used")
        bank_read = [sem(f"bank_read{i}") for i in range(4)]
        psum_for_dve = sem("psum_for_dve")
        psum_for_act = sem("psum_for_act")
        dve_for_pe = sem("dve_for_pe")
        act_for_pe = sem("act_for_pe")
        dve_for_act = sem("dve_for_act")
        act_for_dve = sem("act_for_dve")
        dve_step = sem("dve_step")
        x_in = sem("x_in")
        tab_in = sem("tab_in")
        filt_in = sem("filt_in")
        mixer_in = sem("mixer_in")
        inv_in = sem("inv_in")
        mem_in = sem("mem_in")
        lora_in = sem("lora_in")
        mem2_in = sem("mem2_in")
        free_early = sem("free_early")
        free_inv = sem("free_inv")
        free_lora = sem("free_lora")
        free_mem = sem("free_mem")
        bias_in = sem("bias_in")
        bias_used = sem("bias_used")
        hidden_ready = sem("hidden_ready")
        head_written = sem("head_written")
        merged_ready = sem("merged_ready")
        stored = sem("stored")

        PROJ = [banks[0], banks[1], banks[3], banks[4]]

        def p2(b):
            return PROJ[b][:, :].rearrange("p (s t) -> p s t", s=2)

        def col(name, i=0):
            return par[:, bass.ds(COL[name] + i, 1)]

        def con_(name):
            s, n = CC[name]
            return con[:, s:s + n]

        def b4(bank):
            return banks[bank][:, :].rearrange("p (c t) -> p c t", c=4)

        def bcast(ap2d, n):
            return ap2d.unsqueeze(1).broadcast_to([P, n, ap2d.shape[1]])

        final_fill = {}
        block = ctx.enter_context(nc.Block())

        @block.gpsimd
        def _(pool):
            for dst, src in ((feat[:, :], "feat"), (fw1[:, :], "fw1"), (fw2[:, :], "fw2"), (fw3[:, :], "fw3"),
                             (dft[:, :, :, :], "dft"), (decay[:, :, :], "decay")):
                pool.dma_start(dst, a[src]).then_inc(filt_in, 16)
            pool.wait_ge(free_early, 1)
            for dst, src in ((ws[:, :, :], "ws"), (pw[:, :, :], "pw"), (bs[:, :], "bs")):
                pool.dma_start(dst, a[src]).then_inc(mixer_in, 16)
            pool.wait_ge(free_inv, 1)
            pool.dma_start(inv[:, :, :], a["inv"]).then_inc(inv_in, 16)
            pool.wait_ge(free_lora, 1)
            pool.dma_start(lora[:, :], a["lora"]).then_inc(lora_in, 16)
            with pool.Fori(0, HEADS_A) as g:
                pool.wait_ge(bias_used, g + 1)
                pool.dma_start(bias_t[:, :], a["bias"][g]).then_inc(bias_in, 16)
            pool.wait_ge(free_mem, 1)
            pool.dma_start(memx[:, :, :], a["memT"]).then_inc(mem_in, 16)

        @block.tensor
        def _(pe):
            n = Counts(pe)
            slots = count()

            def mm(out, lhsT, rhs, start=True, stop=True):
                return pe.matmul(out, lhsT, rhs, start=start, stop=stop, skip_group_check=True)

            def unit(bank, k0, hi, lo, first, last, tiles=2, fresh=True):
                slot = next(slots) % RING
                pe.wait_ge(split_done, n.next("split"))
                o = p2(bank)
                for kk in range(UK):
                    for t in range(tiles):
                        wh = w_hi[slot][:, kk, t * P:(t + 1) * P]
                        wl = w_lo[slot][:, kk, t * P:(t + 1) * P]
                        rh, rl = hi[:, k0 + kk, :], lo[:, k0 + kk, :]
                        mm(o[:, t, :], wh, rh, first and kk == 0 and t == 0, False)
                        mm(o[:, t, :], wh, rl, False, False)
                        m = mm(o[:, t, :], wl, rh, False, last and kk == UK - 1 and t == tiles - 1)
                m.then_inc(unit_used, 1)

            def group(bank, hi, lo, k0=0, units=4, tiles=2, filled=True):
                if filled:
                    pe.wait_ge(bank_read[bank], n.now(("fill", bank)))
                n.next(("fill", bank))
                for u in range(units):
                    unit(bank, k0 + UK * u, hi, lo, u == 0, u == units - 1, tiles)

            def from_dve(k=1):
                pe.wait_ge(dve_for_pe, n.next("dve", k))

            def from_act(k=1):
                pe.wait_ge(act_for_pe, n.next("act", k))

            def norm_sums(src):
                for c in range(4):
                    from_act()
                    for t in range(4 * c, 4 * c + 4):
                        m = mm(banks[2][:, 0:T], con_("ones"), src[:, t, :], t == 0, t == KT - 1)
                m.then_inc(psum_for_act, 1)

            pe.wait_ge(tab_in, 32)
            norm_sums(scratch)
            from_dve()
            group(0, h_hi, h_lo, filled=False)
            pe.wait_ge(filt_in, 6 * 16)
            mm(banks[3][0:64, 0:T], fw1[:, :], feat[:, :]).then_inc(psum_for_dve, 1)
            group(1, h_hi, h_lo, filled=False)
            from_act()
            mm(banks[3][0:64, 0:T], fw2[:, :], fh[3][:, :]).then_inc(psum_for_dve, 1)
            group(0, h_hi, h_lo)
            from_act()
            for c in range(2):
                for q in range(4):
                    if c == 1:
                        from_dve()
                    mm(banks[3 + q][:, 0:384], fh[3][:, c * P:(c + 1) * P], fw3[:, q * 384:(q + 1) * 384])\
                        .then_inc(psum_for_dve, 1)
            group(1, h_hi, h_lo)
            from_dve(4)
            from_dve()
            for q, (tab, src) in enumerate(((0, f_sum), (1, f_bwd))):
                for f in range(2):
                    for c in range(2):
                        b = 3 + (4 * q + 2 * f + c) % 4
                        if q == 1:
                            from_act()
                        for k in range(2):
                            m = mm(banks[b][:, 0:384], dft[:, tab, k, f * P:(f + 1) * P],
                                   src[:, k, c * 384:(c + 1) * 384], k == 0, k == 1)
                        m.then_inc(psum_for_act, 1)
            from_act(4)
            for p in range(4, 9):
                group(p % 2, h_hi, h_lo)
            group(1, h_hi, h_lo)
            from_dve()
            for c in range(2):
                for half in range(2):
                    b = 3 + 2 * c + half
                    for j in range(3):
                        m = pe.transpose(banks[b][:, j * P:(j + 1) * P], z1[:, 3 * half + j, c * P:(c + 1) * P],
                                         con_("ident"))
                    m.then_inc(psum_for_act, 1)
            group(0, h_hi, h_lo)
            group(1, h_hi, h_lo)
            from_act(4)
            for i, (f, c) in enumerate(((0, 0), (0, 1), (1, 0), (1, 1))):
                if i >= 2:
                    from_dve()
                for part in range(2):
                    b = 3 + 2 * (i % 2) + part
                    for k in range(2):
                        m = mm(banks[b][:, 0:384], dft[:, part, k, f * P:(f + 1) * P],
                               zt[:, k, c * 384:(c + 1) * 384], k == 0, k == 1)
                m.then_inc(psum_for_dve, 1)
            group(0, h_hi, h_lo)
            from_dve(3)
            for j in range(HY):
                o = banks[3 + j // 2][:, (j % 2) * T:(j % 2 + 1) * T]
                for i, (src, tab, k) in enumerate(((k_re, 2, 0), (k_re, 2, 1), (k_im, 3, 0), (k_im, 3, 1))):
                    m = mm(o, src[:, k, j * P:(j + 1) * P], dft[:, tab, k, :], i == 0, i == 3)
                if j % 2:
                    m.then_inc(psum_for_dve, 1)
            from_act()
            for j in range(HY):
                m = mm(banks[6][:, 0:T], con_("ones"), gv[:, j, :], j == 0, j == HY - 1)
            m.then_inc(psum_for_dve, 1)
            group(1, h_hi, h_lo)
            from_act()
            for j in range(HY):
                m = mm(banks[7][:, 0:T], con_("ones"), gsq[:, j, :], j == 0, j == HY - 1)
            m.then_inc(psum_for_act, 1)
            group(0, h_hi, h_lo)
            from_dve()
            for e in range(HY):
                for c in range(2):
                    i = 2 * c + e % 2
                    m = pe.transpose(banks[3 + e // 2][:, i * P:(i + 1) * P], gv[:, e, c * P:(c + 1) * P],
                                     con_("ident"))
                if e % 2:
                    m.then_inc(psum_for_act, 1)
            group(1, h_hi, h_lo)
            pe.wait_ge(mixer_in, 3 * 16)
            from_act(3)
            for e in range(HY):
                for c in range(2):
                    o = banks[3 + e // 2][:, (e % 2) * T + c * P:(e % 2) * T + (c + 1) * P]
                    mm(o, gvt[:, c, e * P:(e + 1) * P], ws[:, e, :], True, False)
                    m = mm(o, con[0:1, CC["ones"][0]:CC["ones"][0] + P], bs[0:1, e * P:(e + 1) * P], False, True)
                if e % 2:
                    m.then_inc(psum_for_dve, 1)
            group(0, h_hi, h_lo)
            from_dve()
            for g in range(4):
                m = mm(banks[6 + g // 2][:, (g % 2) * T:(g % 2 + 1) * T], pw[:, g, :], pool_d[:, g, :])
            m.then_inc(psum_for_dve, 1)
            from_dve()
            with n.loop(4, {("fill", 0): 1, ("fill", 1): 1, "split": 8}):
                group(1, y_hi, y_lo)
                group(0, y_hi, y_lo)
            norm_sums(scratch2)
            from_dve()
            n.next(("fill", 2))
            n.next(("fill", 3))
            with n.loop(2, {("fill", 0): 13, ("fill", 1): 13, ("fill", 2): 2, ("fill", 3): 2,
                            "split": U_UP + U_DOWN, "hidden": FF_HALF}):
                with n.loop(FF_HALF // 2, {("fill", 0): 1, ("fill", 1): 1, "split": 8}):
                    group(1, h_hi, h_lo)
                    group(0, h_hi, h_lo)
                pe.wait_ge(hidden_ready, n.next("hidden", FF_HALF))
                for q in range(4):
                    pair = (0, 1) if q % 2 == 0 else (2, 3)
                    for b in pair:
                        pe.wait_ge(bank_read[b], n.now(("fill", b)))
                        n.next(("fill", b))
                    for u in range(11):
                        slot = next(slots) % RING
                        pe.wait_ge(split_done, n.next("split"))
                        wh4 = w_hi[slot][:, :, :].rearrange("p k n -> p (k n)").rearrange("p (k n) -> p k n", k=2)
                        wl4 = w_lo[slot][:, :, :].rearrange("p k n -> p (k n)").rearrange("p (k n) -> p k n", k=2)
                        for kk in range(2):
                            for t in range(4):
                                o = p2(pair[t // 2])[:, t % 2, :]
                                wh, wl = wh4[:, kk, t * P:(t + 1) * P], wl4[:, kk, t * P:(t + 1) * P]
                                rh, rl = m_hi[:, 2 * u + kk, :], m_lo[:, 2 * u + kk, :]
                                mm(o, wh, rh, u == 0 and kk == 0 and t % 2 == 0, False)
                                mm(o, wh, rl, False, False)
                                m = mm(o, wl, rh, False, u == 10 and kk == 1 and t % 2 == 1)
                        m.then_inc(unit_used, 1)
            norm_sums(scratch2)
            norm_sums(scratch2)
            from_dve()
            group(1, h_hi, h_lo, tiles=1)
            from_act()
            pe.wait_ge(lora_in, 16)
            for j in range(8):
                if j >= 2:
                    from_act()
                mm(banks[3 + j % 2][:, 0:T], lora[0:64, j * P:(j + 1) * P], lt[0:64, :])
                mm(banks[5 + j % 2][:, 0:T], lora[64:128, j * P:(j + 1) * P], lt[64:128, :])\
                    .then_inc(psum_for_act, 1)
            from_act(2)

            ident = con_("ident")

            def per_chunk(bank, lhs, rhs):
                o = b4(bank)
                for c in range(NCH):
                    m = mm(o[:, c, :], lhs[:, c, :], rhs if rhs is ident else rhs[:, c, :])
                return m

            with n.loop(HEADS_A, {("fill", 0): 2, ("fill", 1): 2, "split": 16, "dve": 19, "act": 22}):
                group(0, h_hi, h_lo)
                group(1, h_hi, h_lo)
                from_dve(2)
                mm(banks[2][:, 0:T], con_("head_ones"), small["sq"][:, :])
                mm(banks[2][:, T:2 * T], con_("head_ones"), small["rk"][:, :]).then_inc(psum_for_dve, 1)
                group(0, h_hi, h_lo)
                from_act()
                mm(banks[7][:, :], con_("ones"), qr[:, :, :].rearrange("p s t -> p (s t)"))\
                    .then_inc(psum_for_act, 1)
                pe.wait_ge(bank_read[1], n.now(("fill", 1)))
                n.next(("fill", 1))
                unit(1, 0, h_hi, h_lo, True, False)
                from_dve()
                a_, b_, k_, v_ = bd["a"], bd["b"], bd["k"], bd["v"]
                per_chunk(3, b_, a_).then_inc(psum_for_dve, 1)
                per_chunk(4, a_, b_).then_inc(psum_for_dve, 1)
                per_chunk(5, k_, a_).then_inc(psum_for_dve, 1)
                o6 = banks[6][:, :].rearrange("p (q c t) -> p q c t", q=2, c=NCH)
                for q, lhs in enumerate((b_, k_)):
                    for c in range(NCH):
                        m = mm(o6[:, q, c, :], lhs[:, c, :], small["rt"][:, c * CHUNK:(c + 1) * CHUNK])
                m.then_inc(psum_for_dve, 1)
                per_chunk(2, v_, ident).then_inc(psum_for_act, 1)
                unit(1, 4, h_hi, h_lo, False, False)
                from_dve()
                per_chunk(3, bd["Nt"], bd["N"]).then_inc(psum_for_act, 1)
                per_chunk(4, bd["N"], bd["Nt"]).then_inc(psum_for_act, 1)
                from_dve()
                from_act()
                per_chunk(5, bd["Kt"], bd["Vt"]).then_inc(psum_for_act, 1)
                per_chunk(6, a_, ident).then_inc(psum_for_act, 1)
                per_chunk(2, b_, ident).then_inc(psum_for_act, 1)
                unit(1, 8, h_hi, h_lo, False, False)
                from_act(2)
                per_chunk(3, bd["b1"], bd["Q"]).then_inc(psum_for_dve, 1)
                per_chunk(4, bd["b2"], bd["b1"]).then_inc(psum_for_act, 1)
                from_act(3)
                per_chunk(5, k_, ident).then_inc(psum_for_act, 1)
                unit(1, 12, h_hi, h_lo, False, True)
                from_dve()
                from_act()
                per_chunk(3, bd["b3"], bd["Q"]).then_inc(psum_for_dve, 1)
                from_dve()
                from_act()
                per_chunk(3, bd["No"], bd["Q"]).then_inc(psum_for_dve, 1)
                per_chunk(4, bd["Q"], bd["No"]).then_inc(psum_for_act, 1)
                per_chunk(5, bd["Q"], bd["At"]).then_inc(psum_for_act, 1)
                per_chunk(6, bd["Q"], bd["AkV"]).then_inc(psum_for_act, 1)
                from_dve()
                mm(banks[7][:, 0:P], qk[:, 0, 0:P], qk[:, 1, 0:P])
                mm(banks[7][:, P:P + T], qk[:, 0, P:T], qk[:, 1, :]).then_inc(psum_for_dve, 1)
                from_dve()
                from_act(1)
                per_chunk(3, bd["b2"], bd["b1"]).then_inc(psum_for_act, 1)
                per_chunk(4, bd["b1"], bd["b2"]).then_inc(psum_for_act, 1)
                from_act(2)
                from_act(1)
                for c in range(2):
                    m = pe.transpose(banks[2][:, c * P:(c + 1) * P], small["t0"][:, c * P:(c + 1) * P], ident)
                m.then_inc(psum_for_act, 1)
                from_act(2)
                per_chunk(3, bd["N"], bd["F"]).then_inc(psum_for_dve, 1)
                per_chunk(4, bd["Nt"], bd["N"]).then_inc(psum_for_act, 1)
                from_act(1)
                from_act(1)
                from_dve()
                per_chunk(3, bd["b3"], bd["F"]).then_inc(psum_for_dve, 1)
                from_dve(2)
                per_chunk(5, bd["Y"], bd["F"]).then_inc(psum_for_act, 1)
                per_chunk(6, bd["F"], bd["Kt"]).then_inc(psum_for_act, 1)
                for i, o in enumerate((0, P, 2 * P)):
                    m = pe.transpose(banks[7][:, i * P:(i + 1) * P], prb[:, o:o + P], ident)
                m.then_inc(psum_for_act, 1)
                from_act(3)
                o3 = banks[3]
                for c in range(NCH):
                    cs = slice(c * CHUNK, (c + 1) * CHUNK)
                    if c:
                        from_dve()
                        mm(banks[2][:, 0:P], bd["b2"][:, c, :], S[:, c % 2, :]).then_inc(psum_for_dve, 1)
                        from_dve()
                    if c == 0:
                        mm(banks[5][:, 0:P], av_t[:, 0, :], prt[:, 0:P])
                        mm(banks[5][:, P:T], av_t[:, 0, :], prt[:, P:T], True, False)
                        mm(banks[5][:, P:T], av_t[:, 1, :], prt[:, T:T + P], False, True)\
                            .then_inc(psum_for_dve, 1)
                    sa = SA[:, :] if c else bd["b1"][:, 0, :]
                    if c < NCH - 1:
                        mm(banks[4][:, 0:P], bd["Bt"][:, c, :], sa, True, False)
                        mm(banks[4][:, 0:P], bd["Kk"][:, c, :], bd["Vt"][:, c, :], False, True)\
                            .then_inc(psum_for_dve, 1)
                    mm(o3[:, cs], sa, BK[:, 0, c, :], True, False)
                    if c:
                        mm(o3[:, cs], S[:, c % 2, :], small["rt"][:, cs], False, False)
                    m = mm(o3[:, cs], bd["Vt"][:, c, :], BK[:, 1, c, :], False, True)
                m.then_inc(psum_for_act, 1)
                from_act()
                mm(banks[4][:, 0:T], con_("center"), small["t0"][:, :]).then_inc(psum_for_act, 1)
                from_act()
                mm(banks[6][:, 0:T], con_("head_ones"), small["sq"][:, :]).then_inc(psum_for_act, 1)
                from_dve()
            norm_sums(scratch3)
            from_dve()
            with n.loop(2, {("fill", 0): 1, ("fill", 1): 1, "split": 8, "dve": 2, "act": 2}):
                for b in (0, 1):
                    group(b, mh_hi, mh_lo)
                    from_act()
                    for s in range(2):
                        m = mm(banks[7][:, 0:T], con_("ones"), csq[:, s, :], s == 0, s == 1)
                    m.then_inc(psum_for_act, 1)
                    from_dve()
            with n.loop(2, {("fill", 0): 1, ("fill", 1): 1, "split": 8, "act": 2}):
                for b in (0, 1):
                    group(b, mh_hi, mh_lo)
                    pe.wait_ge(bank_read[b], n.now(("fill", b)))
                    for c in range(2):
                        for s in range(2):
                            m = pe.transpose(banks[7][:, (2 * c + s) * P:(2 * c + s + 1) * P],
                                             cpair[:, s, c * P:(c + 1) * P], ident)
                    m.then_inc(psum_for_act, 1)
                    from_act()
            with n.loop(HEADS_C, {("fill", 0): 1, ("fill", 1): 1, "split": 8, "dve": 2, "act": 2, "head": 1}) as hd:
                group(0, h_hi, h_lo)
                from_act()
                for s in range(2):
                    m = mm(banks[7][:, 0:T], con_("ones"), csq[:, s, :], s == 0, s == 1)
                m.then_inc(psum_for_act, 1)
                group(1, h_hi, h_lo)
                from_dve()
                for q in range(2):
                    for s in range(2):
                        m = mm(banks[3][:, q * T:(q + 1) * T], cpair[:, s, q * P:(q + 1) * P],
                               mk[:, hd * 2 + s, :], s == 0, s == 1)
                m.then_inc(psum_for_dve, 1)
                from_dve()
                for c in range(2):
                    for q in range(2):
                        m = pe.transpose(banks[4][:, (2 * c + q) * P:(2 * c + q + 1) * P],
                                         cp[:, q, c * P:(c + 1) * P], ident)
                m.then_inc(psum_for_act, 1)
                from_act()
                for s in range(2):
                    for c in range(2):
                        m = mm(banks[5][:, s * T:(s + 1) * T], mvh[:, c, s * P:(s + 1) * P], cpt[:, c, :],
                               c == 0, c == 1)
                m.then_inc(psum_for_dve, 1)
                pe.wait_ge(head_written, n.next("head"))
            from_dve()
            with n.loop(4, {("fill", 0): 6, ("fill", 1): 6, "split": 36}):
                for j in range(2):
                    for m3 in range(3):
                        group(0, h_hi, h_lo)
                        group(1, ya_hi, ya_lo, k0=8 * m3, units=2)
            pe.wait_ge(merged_ready, 8)
            final_fill.update({b: n.now(("fill", b)) for b in (0, 1)})
            with n.loop(4, {("fill", 0): 1, ("fill", 1): 1, "split": 8}):
                group(0, mg_hi, mg_lo)
                group(1, mg_hi, mg_lo)
        @block.sync
        def _(sp):
            sp.dma_start(x[:, :, :], a["xT"]).then_inc(x_in, 16)
            sp.dma_start(par[:, :], a["par"]).then_inc(tab_in, 16)
            sp.dma_start(con[:, :], a["con"]).then_inc(tab_in, 16)
            for s in range(RING):
                sp.dma_start(raw[s][:, :, :], a["units"][s].rearrange("p (k n) -> p k n", k=UK))\
                    .then_inc(landed[s], 16)
            with sp.Fori(1, UNITS // RING) as i:
                for s in range(RING):
                    sp.wait_ge(split_done, i * RING + (s - RING + 1))
                    sp.dma_start(raw[s][:, :, :], a["units"][i * RING + s].rearrange("p (k n) -> p k n", k=UK))\
                        .then_inc(landed[s], 16)
            for j in range(8):
                sp.wait_ge(bank_read[j % 2], final_fill[j % 2] + j // 2 + 1)
                sp.dma_start(out_ap[:, 2 * j:2 * j + 2, :], obuf[:, 2 * j:2 * j + 2, :]).then_inc(stored, 16)
            sp.wait_ge(stored, 16 * 8)


        @block.scalar
        def _(act):
            n = Counts(act)
            slots = count()

            def send(ins, to):
                ins.then_inc(to, 1)

            def copy(out, in_, scale=1.0):
                return act.activation(out, in_, ACT.Copy, scale=scale)

            def split():
                slot = next(slots) % RING
                u = n.next("unit")
                act.wait_ge(landed[slot], n.next(("landed", slot), 16))
                if not isinstance(u, int) or u > RING:
                    act.wait_ge(unit_used, u - RING)
                copy(w_hi[slot][:, :, :], raw[slot][:, :, :]).then_inc(hi_done, 1)

            def split4(k=4):
                for _ in range(k):
                    split()

            def group_done():
                act.wait_ge(unit_used, n.now("unit") - RING)

            def psum(k=1):
                act.wait_ge(psum_for_act, n.next("psum", k))

            def from_dve(k=1):
                act.wait_ge(dve_for_act, n.next("dve", k))

            def to_pe(ins):
                ins.then_inc(act_for_pe, 1)

            def to_dve(ins):
                ins.then_inc(act_for_dve, 1)

            def norm(src, sq, hi, rt, split_it=True):
                for c in range(4):
                    cs = slice(4 * c, 4 * c + 4)
                    to_pe(act.activation(sq[:, cs, :], src[:, cs, :], ACT.Square))
                psum()
                to_dve(act.activation(rt[:, :], banks[2][:, 0:T], ACT.Sqrt, bias=con_("eps6"), scale=1.0 / D))
                if split_it:
                    for c in range(4):
                        cs = slice(4 * c, 4 * c + 4)
                        from_dve()
                        to_dve(copy(hi[:, cs, :], sq[:, cs, :]))

            act.wait_ge(x_in, 16)
            act.wait_ge(tab_in, 32)
            norm(x, scratch, h_hi, root)
            split4()

            def hyena(p):
                dst = (x0, z1, zv)[p // 3]
                j = 2 * (p % 3)
                b = p % 2
                group_done()
                n.next(("fill", b))
                for s in range(2):
                    m = act.activation(dst[:, j + s, :], p2(b)[:, s, :], ACT.Identity,
                                       bias=col("hy_b", 2 * p + s), scale=col("hy_w", 18 + 2 * p + s))
                to_dve(m)

            def sine():
                from_dve()
                to_pe(act.activation(fh[3][:, :], fh[2][:, :], ACT.Sin))

            split4()
            hyena(0)
            sine()
            split4()
            hyena(1)
            sine()
            split4()
            hyena(2)
            split4()
            hyena(3)
            for q, dst in enumerate((k_re, k_im)):
                for f in range(2):
                    for c in range(2):
                        psum()
                        to_pe(copy(dst[:, f, c * 384:(c + 1) * 384], banks[3 + (4 * q + 2 * f + c) % 4][:, 0:384]))
            for p in range(4, 9):
                split4()
                hyena(p)

            def gelu(p):
                dst = gv if p < 12 else gu
                j = 2 * (p % 3)
                group_done()
                n.next(("fill", p % 2))
                act.activation(dst[:, j:j + 2, :], p2(p % 2), ACT.Gelu_apprx_tanh).then_inc(bank_read[p % 2], 1)

            def y_half(tile, k, s):
                from_dve()
                to_dve(copy(y_hi[:, tile:tile + k, :], y_part[:, s:s + k, :]))

            split4()
            gelu(9)
            for c in range(2):
                for half in range(2):
                    psum()
                    to_pe(copy(zt[:, c, half * 384:(half + 1) * 384], banks[3 + 2 * c + half][:, 0:384]))
            split4()
            gelu(10)
            split4()
            group_done()
            n.next(("fill", 1))
            g11 = act.activation(gv[:, 4:6, :], p2(1), ACT.Gelu_apprx_tanh)
            g11.then_inc(bank_read[1], 1)
            split4()
            gelu(12)
            act.wait_ge(bank_read[0], n.now(("fill", 0)))
            act.activation(root[:, 0:1], gv[:, 5, 0:1], ACT.Copy).then_inc(act_for_pe, 1)
            for k in range(3):
                y_half(4 + 2 * k, 2, 2 * (k % 2))
            from_dve()
            to_pe(act.activation(gsq[:, :, :], gv[:, :, :], ACT.Square))
            split4()
            gelu(13)
            psum()
            to_dve(act.activation(root[:, :], banks[7][:, 0:T], ACT.Sqrt, bias=con_("eps5"), scale=1.0 / D_HY))
            split4()
            gelu(14)
            for k in range(3):
                psum()
                to_pe(copy(gvt[:, :, 2 * k * P:(2 * k + 2) * P],
                           banks[3 + k][:, :].rearrange("p (c t) -> p c t", c=2)))

            def pool_in(p, b):
                group_done()
                n.next(("fill", b))
                copy(pool_x[:, 2 * (p - 15):2 * (p - 15) + 2, 8:8 + T], p2(b)).then_inc(bank_read[b], 1)

            split4()
            pool_in(15, 1)
            for k in range(3):
                y_half(10 + 2 * k, 2, 2 * (k % 2))
            split4()
            pool_in(16, 0)
            y_half(0, 4, 0)

            with n.loop(4, dict({("landed", s): 32 for s in range(RING)}, unit=8, **{})) as i:
                split4(8)
            for b in (0, 1):
                n.next(("fill", b), 4)
                act.wait_ge(bank_read[b], n.now(("fill", b)))
            norm(x, scratch2, h_hi, root2)

            def land(k):
                return {("landed", s): 16 * k // RING for s in range(RING)}

            with n.loop(2, land(U_UP + U_DOWN) | {"unit": U_UP + U_DOWN, "dve": 2 * FF_HALF,
                                                  ("fill", 0): 13, ("fill", 1): 13}) as half:
                with n.loop(FF_HALF // 2, land(8) | {"unit": 8, "dve": 4, ("fill", 0): 1, ("fill", 1): 1}) as j:
                    for q, b in enumerate((1, 0)):
                        base = half * (8 * FF_HALF) + j * 16 + 8 * q
                        o = conv_o[:, q, :, :]
                        split4()
                        group_done()
                        n.next(("fill", b))
                        for s in range(2):
                            m = act.activation(o[:, s, :], p2(b)[:, s, :], ACT.Identity,
                                               bias=col("ffn", base + (4 * s + 3)),
                                               scale=col("ffn", base + (4 * s + 1)))
                        to_dve(m)
                        from_dve()
                        to_dve(act.activation(o[:, 0, :], o[:, 0, :], ACT.Silu))
                        from_dve()
                        to_dve(copy(m_hi[:, j * 2 + q, :], conv_m[:, q, :]))
                for q in range(4):
                    split4(11)
                    if q % 2 == 0:
                        n.next(("fill", 0))
                        n.next(("fill", 1))
            from_dve()
            norm(x, scratch2, None, root2, split_it=False)
            from_dve()
            norm(x, scratch2, h_hi, root2)
            split4()
            group_done()
            n.next(("fill", 1))
            copy(lx[:, 1:257], p2(1)[:, 0, :]).then_inc(bank_read[1], 1)
            from_dve()
            to_pe(act.activation(lt[0:64, :], lt[0:64, :], ACT.Tanh))
            for j in range(8):
                psum()
                act.activation(cum[:, j, :], banks[3 + j % 2][:, 0:T], ACT.Sigmoid, bias=col("w0", j))
                to_pe(act.activation(icl[:, j, :], banks[5 + j % 2][:, 0:T], ACT.Sigmoid, bias=col("a0", j)))
            act.activation(root2[:, 0:1], icl[:, 0, 0:1], ACT.Copy).then_inc(act_for_dve, 1)
            from_dve()

            def flat(t):
                return t[:, :, :].rearrange("p c t -> p (c t)")

            def keep(name, bank):
                psum()
                to_pe(copy(flat(bd[name]), banks[bank][:, :]))

            ep4 = small["ep"][:, :].rearrange("p (c t) -> p c t", c=NCH)
            with n.loop(HEADS_A, land(16) | {"unit": 16, "psum": 22, "dve": 2, ("fill", 0): 2, ("fill", 1): 2}) as g:
                cg_ = cum[:, bass.ds(g, 1), :].rearrange("p o t -> p (o t)")
                act.activation(ep4[:, :, 1:65], cg_.rearrange("p (c t) -> p c t", c=NCH), ACT.Exp)
                act.activation(small["en"][:, :], cg_, ACT.Exp, scale=-1.0)
                split4()
                group_done()
                n.next(("fill", 0))
                copy(small["pr"][:, 1:257], p2(0)[:, 0, :])
                copy(small["pk"][:, 1:257], p2(0)[:, 1, :]).then_inc(bank_read[0], 1)
                split4()
                group_done()
                n.next(("fill", 1))
                copy(small["pv"][:, 1:257], p2(1)[:, 0, :])
                to_dve(act.activation(small["bz"][:, :], p2(1)[:, 1, :], ACT.Tanh, scale=0.5))
                from_dve()
                to_dve(act.activation(small["sq"][:, :], small["sq"][:, :], ACT.Sqrt))
                split4()
                group_done()
                n.next(("fill", 0))
                to_pe(act.activation(qr[:, :, :], p2(0), ACT.Square))
                copy(qk[:, :, :], p2(0)).then_inc(bank_read[0], 1)
                psum()
                to_dve(act.activation(flat(qr), banks[7][:, :], ACT.Sqrt, bias=con_("eps6"), scale=1.0 / P))
                split()
                keep("Vt", 2)
                split()
                keep("b1", 3)
                keep("b2", 4)
                keep("AkV", 5)
                keep("At", 6)
                keep("Bt", 2)
                split()
                keep("b3", 4)
                keep("Kk", 5)
                split()
                keep("b1", 4)
                keep("Y", 5)
                keep("Kt", 6)
                group_done()
                n.next(("fill", 1))
                to_pe(copy(small["t0"][:, :], p2(1)[:, 0, :]))
                to_dve(act.activation(az[:, :], p2(1)[:, 1, :], ACT.Tanh, scale=0.5))
                keep("N", 3)
                keep("Nt", 4)
                psum()
                to_pe(copy(flat(av_t), banks[2][:, 0:T]))
                keep("b3", 4)
                from_dve()
                act.activation(prb[:, 0:P], prb[:, 0:P], ACT.Exp, bias=stat[:, 2:3], accum_out=stat[:, 4:5])
                to_dve(act.activation(prb[:, P:3 * P], prb[:, P:3 * P], ACT.Exp, bias=stat[:, 3:4],
                                      accum_out=stat[:, 5:6]))
                keep("b2", 5)
                keep("b1", 6)
                psum()
                to_pe(copy(prt[:, :], banks[7][:, 0:3 * P]))
                psum()
                to_pe(copy(small["t0"][:, :], banks[3][:, 0:T]))
                psum()
                to_pe(act.activation(small["sq"][:, :], banks[4][:, 0:T], ACT.Square))
                psum()
                to_dve(act.activation(small["kk"][:, :], banks[6][:, 0:T], ACT.Sqrt, bias=con_("eps_gn"),
                                      scale=1.0 / 64))
            act.wait_ge(mem_in, 16)
            norm(memx, scratch3, mh_hi, croot)

            def root_of(n_ch):
                psum()
                to_dve(act.activation(croot[:, :], banks[7][:, 0:T], ACT.Sqrt, bias=con_("eps6"), scale=1.0 / n_ch))

            with n.loop(2, land(8) | {"unit": 8, "psum": 2, ("fill", 0): 1, ("fill", 1): 1}):
                for b in (0, 1):
                    split4()
                    group_done()
                    n.next(("fill", b))
                    to_pe(act.activation(csq[:, :, :], p2(b), ACT.Square))
                    copy(cpair[:, :, :], p2(b)).then_inc(bank_read[b], 1)
                    root_of(2 * P)
            with n.loop(2, land(8) | {"unit": 8, "psum": 2, ("fill", 0): 1, ("fill", 1): 1}) as i:
                for b in (0, 1):
                    split4()
                    group_done()
                    n.next(("fill", b))
                    copy(cpair[:, :, :], p2(b)).then_inc(bank_read[b], 1)
                    psum()
                    to_pe(copy(mvt[:, :, bass.ds(i * (4 * P) + 2 * b * P, 2 * P)],
                               banks[7][:, :].rearrange("p (c t) -> p c t", c=2)))
            with n.loop(HEADS_C, land(8) | {"unit": 8, "psum": 2, "dve": 1, ("fill", 0): 1, ("fill", 1): 1}):
                split4()
                group_done()
                n.next(("fill", 0))
                to_pe(act.activation(csq[:, :, :], p2(0), ACT.Square))
                copy(cpair[:, :, :], p2(0)).then_inc(bank_read[0], 1)
                root_of(2 * P)
                split4()
                group_done()
                n.next(("fill", 1))
                to_dve(act.activation(cg[:, :, :], p2(1), ACT.Tanh, scale=0.5))
                from_dve()
                for q in range(2):
                    m = act.activation(cp[:, q, :], banks[3][:, q * T:(q + 1) * T], ACT.Exp, scale=1.0 / 16,
                                       bias=cstat[:, 2 + q:3 + q], accum_out=cstat[:, 4 + q:5 + q])
                to_dve(m)
                psum()
                to_pe(copy(flat(cpt), banks[4][:, :]))
            act.wait_ge(head_written, HEADS_C)
            for c in range(6):
                to_dve(copy(ya_hi[:, 4 * c:4 * c + 4, :], yall[:, 4 * c:4 * c + 4, :]))
            with n.loop(4, land(36) | {"unit": 36, "dve": 2, ("fill", 0): 6, ("fill", 1): 6}) as i:
                for j in range(2):
                    for m3 in range(3):
                        split4()
                        group_done()
                        act.wait_ge(bank_read[1], n.now(("fill", 1)))
                        n.next(("fill", 0))
                        act.activation(gate[:, :, :], p2(0), ACT.Tanh, scale=0.5).then_inc(bank_read[0], 1)
                        split4(2)
                        n.next(("fill", 1))
                    from_dve()
                    to_dve(copy(mg_hi[:, bass.ds(i * 4 + 2 * j, 2), :], macc[:, :, :], 0.5))
            with n.loop(7, land(4) | {"unit": 4}):
                split4()

        @block.vector
        def _(dve):
            n = Counts(dve)
            slots = count()

            def split():
                slot = next(slots) % RING
                dve.wait_ge(hi_done, n.next("unit"))
                dve.tensor_tensor(w_lo[slot][:, :, :], raw[slot][:, :, :], w_hi[slot][:, :, :].bitcast(F32),
                                  ALU.subtract).then_inc(split_done, 1)

            def split4(k=4):
                for _ in range(k):
                    split()

            def group_done():
                dve.wait_ge(unit_used, n.now("unit") - RING)

            def psum(k=1):
                dve.wait_ge(psum_for_dve, n.next("psum", k))

            def from_act(k=1):
                dve.wait_ge(act_for_dve, n.next("act", k))

            def step(ins):
                ins.then_inc(dve_step, 1)
                n.next("step")

            def settle():
                dve.wait_ge(dve_step, n.now("step"))

            def to_pe(ins):
                ins.then_inc(dve_for_pe, 1)
                n.next("to_pe")

            def settle_pe():
                dve.wait_ge(dve_for_pe, n.now("to_pe"))

            def to_act(ins):
                ins.then_inc(dve_for_act, 1)
                n.next("to_act")

            def settle_act():
                dve.wait_ge(dve_for_act, n.now("to_act"))

            def read(ins, b):
                ins.then_inc(bank_read[b], 1)

            def own_bank(b):
                dve.wait_ge(bank_read[b], n.now(("fill", b)))

            def tt(out, x_, y_, op):
                return dve.tensor_tensor(out, x_, y_, op)

            def stt(out, x_, s, y_, op0, op1):
                return dve.scalar_tensor_tensor(out, x_, s, y_, op0, op1)

            def ts(out, x_, s0, s1=None, op0=ALU.mult, op1=None):
                return dve.tensor_scalar(out, x_, s0, s1, op0) if op1 is None else \
                    dve.tensor_scalar(out, x_, s0, s1, op0, op1)

            def low(lo, f, hi):
                return tt(lo, f, hi.bitcast(F32), ALU.subtract)

            def norm(src, g, f, hi, lo, rt):
                from_act()
                step(dve.reciprocal(rt[:, :], rt[:, :]))
                settle()
                for t in range(KT):
                    m = stt(f[:, t, :], src[:, t, :], col(g, t), rt[:, :], ALU.mult, ALU.mult)
                    if hi is not None and t % 4 == 3:
                        to_act(m)
                if hi is None:
                    to_act(m)
                    settle_act()
                    return
                for c in range(4):
                    cs = slice(4 * c, 4 * c + 4)
                    from_act()
                    m = low(lo[:, cs, :], f[:, cs, :], hi[:, cs, :])
                to_pe(m)

            dve.wait_ge(x_in, 16)
            dve.wait_ge(tab_in, 32)
            norm(x, "norm_mix", scratch, h_hi, h_lo, root)
            split4()

            def taps(dst, b, w0, w2):
                o = p2(b)
                for s in range(2):
                    step(stt(dst[s][:, 1:T], o[:, s, 0:T - 1], w0[s], dst[s][:, 1:T], ALU.mult, ALU.add))
                settle()
                return [lambda s=s: stt(dst[s][:, 0:T - 1], o[:, s, 1:T], w2[s], dst[s][:, 0:T - 1], ALU.mult,
                                        ALU.add) for s in range(2)]

            def hyena(p):
                dst = (x0, z1, zv)[p // 3]
                j = 2 * (p % 3)
                b = p % 2
                from_act()
                n.next(("fill", b))
                last = taps([dst[:, j + s, :] for s in range(2)], b, [col("hy_w", 2 * p + s) for s in range(2)],
                            [col("hy_w", 36 + 2 * p + s) for s in range(2)])
                step(last[0]())
                read(last[1](), b)

            def sine(b_, fr):
                u, k, r = fh[0][:, :], fh[1][:, :], fh[2][:, :]
                psum()
                step(ts(u, banks[3][0:64, 0:T], col(b_)[0:64, :], col(fr)[0:64, :], ALU.add, ALU.mult))
                settle()
                step(ts(k, u, float(1.0 / TWO_PI), ROUND, ALU.mult, ALU.add))
                settle()
                step(ts(k, k, ROUND, None, ALU.subtract))
                settle()
                step(stt(r, k, -PI_HI, u, ALU.mult, ALU.add))
                settle()
                step(stt(r, k, -PI_LO, r, ALU.mult, ALU.add))
                settle()
                to_act(ts(r, r, PI_CUT, -PI_CUT, ALU.min, ALU.max))

            split4()
            hyena(0)
            dve.wait_ge(filt_in, 6 * 16)
            sine("f_b1", "f_fr1")
            split4()
            hyena(1)
            sine("f_b2", "f_fr2")
            split4()
            hyena(2)
            for c in range(2):
                for q in range(4):
                    psum()
                    dst = f_fwd if q < 2 else f_bwd
                    qs = slice((q % 2) * 384, (q % 2 + 1) * 384)
                    to_pe(tt(dst[:, c, qs], banks[3 + q][:, 0:384], decay[:, c, qs], ALU.mult))
            settle_pe()
            dve.memset(f_bwd[0:1, 0, :], 0.0).then_inc(free_early, 1)
            dve.wait_ge(free_early, 1)
            step(tt(f_sum[:, :, :], f_fwd[:, :, :], f_bwd[:, :, :], ALU.add))
            settle()
            to_pe(tt(f_bwd[:, :, :], f_fwd[:, :, :], f_bwd[:, :, :], ALU.subtract))
            for p in range(3, 9):
                split4()
                hyena(p)
            own_bank(0)
            own_bank(1)
            settle()
            to_pe(tt(z1[:, :, :], z1[:, :, :], zv[:, :, :], ALU.mult))
            for p in (9, 10, 11):
                split4()
                n.next(("fill", p % 2))
            for i, (f, c) in enumerate(((0, 0), (0, 1), (1, 0), (1, 1))):
                psum()
                zr, zi = (banks[3 + 2 * (i % 2) + k][:, 0:384] for k in range(2))
                cs = slice(c * 384, (c + 1) * 384)
                kr, ki = k_re[:, f, cs], k_im[:, f, cs]
                if i == 0:
                    settle_pe()
                step(tt(prod[0][:, :], zr, kr, ALU.mult))
                step(tt(prod[1][:, :], zi, ki, ALU.mult))
                step(tt(prod[2][:, :], zr, ki, ALU.mult))
                to_pe(tt(prod[3][:, :], zi, kr, ALU.mult))
                settle()
                settle_pe()
                step(tt(kr, prod[0][:, :], prod[1][:, :], ALU.subtract))
                if i < 3:
                    step(tt(ki, prod[2][:, :], prod[3][:, :], ALU.add))
                else:
                    to_pe(tt(ki, prod[2][:, :], prod[3][:, :], ALU.add))
                settle()
            settle_pe()
            split4()
            n.next(("fill", 0))

            def y_low(tile, k, s, last=None):
                from_act()
                m = low(y_lo[:, tile:tile + k, :], y_part[:, s:s + k, :], y_hi[:, tile:tile + k, :])
                (to_pe if last else step)(m)

            for k in range(3):
                psum()
                for s in range(2):
                    step(stt(mix[:, s, :], z1[:, 2 * k + s, :], col("hy_skip", 2 * k + s),
                             banks[3 + k][:, s * T:(s + 1) * T], ALU.mult, ALU.add))
                settle()
                s = 2 * (k % 2)
                to_act(tt(y_part[:, s:s + 2, :], mix[:, :, :], x0[:, 2 * k:2 * k + 2, :], ALU.mult))
                settle_act()
                y_low(4 + 2 * k, 2, s)
                settle()
            dve.memset(pool_x[:, :, 0:8], 0.0)
            dve.memset(pool_x[:, :, 8 + T:PW], 0.0).then_inc(free_inv, 1)
            psum()
            for j in range(HY):
                m = stt(gv[:, j, :], banks[6][:, 0:T], -1.0 / D_HY, gv[:, j, :], ALU.mult, ALU.add)
            to_act(m)
            settle_act()
            split4()
            n.next(("fill", 1))
            from_act()
            step(dve.reciprocal(root[:, :], root[:, :]))
            settle()
            step(tt(gv[:, :, :], gv[:, :, :], bcast(root[:, :], HY), ALU.mult))
            settle()
            for j in range(HY):
                m = ts(gv[:, j, :], gv[:, j, :], col("gm_g", j), col("gm_b", j), ALU.mult, ALU.add)
            to_pe(m)
            split4()
            n.next(("fill", 0))
            split4()
            n.next(("fill", 1))
            for k in range(3):
                psum()
                s = 2 * (k % 2)
                to_act(tt(y_part[:, s:s + 2, :], gu[:, 2 * k:2 * k + 2, :],
                          banks[3 + k][:, :].rearrange("p (s t) -> p s t", s=2), ALU.mult))
                settle_act()
                y_low(10 + 2 * k, 2, s)
                settle()
            split4()
            n.next(("fill", 0))
            own_bank(1)
            own_bank(0)
            dve.wait_ge(free_inv, 1)
            step(tt(pool_a[:, :, 1:PW], pool_x[:, :, 0:PW - 1], pool_x[:, :, 1:PW], ALU.add))
            settle()
            step(tt(pool_b[:, 1:4, 2:PW - 1], pool_a[:, 1:4, 1:PW - 2], pool_a[:, 1:4, 3:PW], ALU.add))
            settle()
            step(tt(pool_a[:, 2:4, 4:PW - 3], pool_b[:, 2:4, 2:PW - 5], pool_b[:, 2:4, 6:PW - 1], ALU.add))
            settle()
            step(tt(pool_b[:, 3:4, 8:PW - 7], pool_a[:, 3:4, 4:PW - 11], pool_a[:, 3:4, 12:PW - 3], ALU.add))
            settle()
            dve.wait_ge(inv_in, 16)
            for g in range(4):
                src = (pool_a, pool_b, pool_a, pool_b)[g]
                step(tt(pool_d[:, g, :], src[:, g, 8:8 + T], inv[:, g, :], ALU.mult))
            settle()
            to_pe(tt(pool_d[:, :, :], pool_d[:, :, :], pool_x[:, :, 8:8 + T], ALU.subtract))
            psum()
            for g in range(4):
                m = ts(y_part[:, g, :], banks[6 + g // 2][:, (g % 2) * T:(g % 2 + 1) * T], col("pool_b", g),
                       col("pool_scale", g), ALU.add, ALU.mult)
            to_act(m)
            settle_act()
            y_low(0, 4, 0, last=True)

            def residual(tile, b, out=None):
                group_done()
                n.next(("fill", b))
                t = x[:, bass.ds(tile, 2), :]
                dst = t if out is None else out[:, bass.ds(tile, 2), :]
                read(tt(dst, t, p2(b), ALU.add), b)

            with n.loop(4, {"unit": 8, ("fill", 0): 1, ("fill", 1): 1}) as i:
                for q, b in enumerate((1, 0)):
                    split4()
                    residual(i * 4 + 2 * q, b)
            own_bank(0)
            own_bank(1)
            norm(x, "norm_ffn", scratch2, h_hi, h_lo, root2)
            for b in (2, 3):
                n.next(("fill", b))
                dve.memset(conv_m[:, 0, 0:1], 0.0).then_inc(bank_read[b], 1)
                own_bank(b)
            with n.loop(2, {"unit": U_UP + U_DOWN, "act": 3 * FF_HALF, "to_act": 2 * FF_HALF, "step": 3 * FF_HALF // 1 - FF_HALF,
                            ("fill", 0): 13, ("fill", 1): 13, ("fill", 2): 2, ("fill", 3): 2}) as half:
                with n.loop(FF_HALF // 2, {"unit": 8, "act": 6, "to_act": 4, "step": 4, ("fill", 0): 1,
                                           ("fill", 1): 1}) as j:
                    for q, b in enumerate((1, 0)):
                        base = half * (8 * FF_HALF) + j * 16 + 8 * q
                        o = conv_o[:, q, :, :]
                        split4()
                        from_act()
                        n.next(("fill", b))
                        last = taps([o[:, s, :] for s in range(2)], b, [col("ffn", base + 4 * s) for s in range(2)],
                                    [col("ffn", base + (4 * s + 2)) for s in range(2)])
                        to_act(last[0]())
                        read(last[1](), b)
                        from_act()
                        own_bank(b)
                        to_act(tt(conv_m[:, q, :], o[:, 0, :], o[:, 1, :], ALU.mult))
                        settle_act()
                        from_act()
                        low(m_lo[:, j * 2 + q, :], conv_m[:, q, :], m_hi[:, j * 2 + q, :])\
                            .then_inc(hidden_ready, 1)
                for q in range(4):
                    split4(11)
                    group_done()
                    for s, b in enumerate((0, 1) if q % 2 == 0 else (2, 3)):
                        n.next(("fill", b))
                        t = x[:, 4 * q + 2 * s:4 * q + 2 * s + 2, :]
                        read(tt(t, t, p2(b), ALU.add), b)
                for b in range(4):
                    own_bank(b)
            to_act(dve.memset(lx[:, 0:1], 0.0))
            norm(x, "norm_final", x, None, None, root2)
            norm(x, "norm_g", scratch2, h_hi, h_lo, root2)
            dve.memset(lx[:, 0:1], 0.0).then_inc(free_lora, 1)
            dve.wait_ge(free_lora, 1)
            split4()
            n.next(("fill", 1))
            own_bank(1)
            step(tt(lt[:, :], lx[:, 0:T], lx[:, 1:T + 1], ALU.subtract))
            settle()
            to_act(stt(lt[:, :], lt[:, :], col("mu_wa"), lx[:, 1:T + 1], ALU.mult, ALU.add))
            from_act()
            step(ts(cum[:, :, :], cum[:, :, :], -float(np.exp(-0.5))))
            settle()
            a4, b4_ = (t[:, :, :].rearrange("p g (c t) -> p (g c) t", t=CHUNK) for t in (cum, ping))
            for k in range(6):
                s = 1 << k
                step(tt(b4_[:, :, s:CHUNK], a4[:, :, s:CHUNK], a4[:, :, 0:CHUNK - s], ALU.add))
                step(dve.tensor_copy(b4_[:, :, 0:s], a4[:, :, 0:s]))
                settle()
                a4, b4_ = b4_, a4
            for t in ("a", "b", "k", "v"):
                step(dve.memset(bd[t][:, :, :], 0.0))
            ep4 = small["ep"][:, :].rearrange("p (c t) -> p c t", c=NCH)
            step(dve.memset(ep4[:, :, 0:1], 1.0))
            for t in ("pr", "pk", "pv"):
                step(dve.memset(small[t][:, 0:1], 0.0))
            dve.memset(stat[:, 0:1], 0.0).then_inc(bias_used, 1)
            dve.wait_ge(bias_used, 1)
            settle()
            to_act(dve.memset(stat[:, 1:2], 0.0))
            settle_act()

            def c4(t):
                return t.rearrange("p (c t) -> p c t", c=NCH)

            def flat(t):
                return t[:, :, :].rearrange("p c t -> p (c t)")

            sm = small
            shift = lambda t: (sm[t][:, 0:T], sm[t][:, 1:T + 1])
            ident4 = bcast(con_("ident"), NCH)
            with n.loop(HEADS_A, {"unit": 16, "psum": 18, "act": 6, "step": 41, "to_pe": 19, "to_act": 2,
                                  ("fill", 0): 2, ("fill", 1): 2, "bias": 1}) as g:
                rw = lambda k: col("rwkv", g * RW_COLS + k)
                icl_g = icl[:, bass.ds(g, 1), :].rearrange("p o t -> p (o t)")
                split4()
                n.next(("fill", 0))
                own_bank(0)
                prev, now = shift("pr")
                step(tt(sm["t0"][:, :], prev, now, ALU.subtract))
                prevk, nowk = shift("pk")
                step(tt(sm["k2"][:, :], prevk, nowk, ALU.subtract))
                settle()
                step(stt(sm["r"][:, :], sm["t0"][:, :], rw(MU_R), now, ALU.mult, ALU.add))
                step(stt(sm["k0"][:, :], sm["k2"][:, :], rw(MU_K), nowk, ALU.mult, ALU.add))
                settle()
                step(ts(sm["kk"][:, :], sm["k0"][:, :], rw(K_K)))
                step(ts(sm["t0"][:, :], icl_g, 1.0, rw(K_A), ALU.subtract, ALU.mult))
                settle()
                to_pe(tt(sm["sq"][:, :], sm["kk"][:, :], sm["kk"][:, :], ALU.mult))
                step(stt(sm["k2"][:, :], sm["t0"][:, :], 1.0, sm["k0"][:, :], ALU.add, ALU.mult))
                settle()
                to_pe(stt(sm["rk"][:, :], sm["r"][:, :], rw(R_K), sm["k2"][:, :], ALU.mult, ALU.mult))
                split4()
                n.next(("fill", 1))
                from_act()
                prev, now = shift("pv")
                step(tt(sm["t0"][:, :], prev, now, ALU.subtract))
                read(stt(sm["bz"][:, :], sm["bz"][:, :], 1.0, p2(1)[:, 1, :], ALU.add, ALU.mult), 1)
                settle()
                step(stt(sm["v"][:, :], sm["t0"][:, :], rw(MU_V), now, ALU.mult, ALU.add))
                psum()
                to_act(ts(sm["sq"][:, :], banks[2][:, 0:T], 1e-24, None, ALU.max))
                settle()
                step(tt(sm["bon"][:, :], banks[2][:, T:2 * T], sm["v"][:, :], ALU.mult))
                split()
                from_act()
                step(dve.reciprocal(sm["sq"][:, :], sm["sq"][:, :]))
                settle()
                step(tt(sm["kk"][:, :], sm["kk"][:, :], sm["sq"][:, :], ALU.mult))
                settle()
                step(tt(sm["t0"][:, :], sm["kk"][:, :], icl_g, ALU.mult))
                settle()
                for h in range(2):
                    hp, hc = slice(64 * h, 64 * h + 64), slice(64 * h, 64 * h + 64)
                    step(stt(bd["a"][hp, :, hc], c4(sm["kk"][hp, :]), -1.0, ep4[hp, :, 0:CHUNK], ALU.mult,
                             ALU.mult))
                    step(tt(bd["b"][hp, :, hc], c4(sm["t0"][hp, :]), c4(sm["en"][hp, :]), ALU.mult))
                    step(tt(bd["k"][hp, :, hc], c4(sm["k2"][hp, :]), c4(sm["en"][hp, :]), ALU.mult))
                    step(dve.tensor_copy(bd["v"][hp, :, hc], c4(sm["v"][hp, :])))
                to_pe(tt(c4(sm["rt"][:, :]), c4(sm["r"][:, :]), ep4[:, :, 1:CHUNK + 1], ALU.mult))
                split4(3)
                n.next(("fill", 0))
                from_act()
                step(dve.reciprocal(flat(qr), flat(qr)))
                split()
                psum()
                step(tt(bd["Nt"][:, :, :], b4(3), bcast(con_("upper_in"), NCH), ALU.mult))
                psum()
                step(tt(bd["N"][:, :, :], b4(4), bcast(con_("lower_in"), NCH), ALU.mult))
                to_pe(tt(bd["No"][:, :, :], b4(4), bcast(con_("lower_out"), NCH), ALU.mult))
                psum()
                step(tt(bd["Kt"][:, :, :], b4(5), bcast(con_("upper"), NCH), ALU.mult))
                settle()
                step(tt(bd["Q"][:, :, :], bd["Nt"][:, :, :], ident4, ALU.add))
                psum()
                to_pe(tt(BK[:, :, :, :].rearrange("p q c t -> p (q c) t"),
                         banks[6][:, :].rearrange("p (q t) -> p q t", t=CHUNK), bcast(con_("upper_eq"), 8), ALU.mult))
                settle()
                split()
                split()
                psum()
                to_pe(tt(bd["Q"][:, :, :], bd["Q"][:, :, :], b4(3), ALU.add))
                split()
                settle_pe()
                psum()
                to_pe(tt(bd["Q"][:, :, :], bd["Q"][:, :, :], b4(3), ALU.add))
                step(stt(qk[:, 0, :], qk[:, 0, :], col("aq_g"), qr[:, 0, :], ALU.mult, ALU.mult))
                to_pe(stt(qk[:, 1, :], qk[:, 1, :], col("ak_g"), qr[:, 1, :], ALU.mult, ALU.mult))
                psum()
                step(dve.tensor_copy(bd["b2"][:, :, :], b4(3)))
                to_pe(tt(bd["F"][:, :, :], b4(3), ident4, ALU.add))
                settle_pe()
                n.next(("fill", 1))
                from_act()
                read(stt(az[:, :], az[:, :], 1.0, p2(1)[:, 1, :], ALU.add, ALU.mult), 1)
                psum()
                dve.wait_ge(bias_in, 16 * n.next("bias"))
                dve_bias = stt(prb[:, :], banks[7][:, 0:3 * P], float(P) ** -0.5, bias_t[:, :], ALU.mult, ALU.add)
                dve_bias.then_inc(bias_used, 1)
                dve.wait_ge(bias_used, n.now("bias") + 1)
                step(dve.memset(prb[0:64, 64:P], NEG))
                step(dve.memset(prb[0:64, P + 192:3 * P], NEG))
                settle()
                step(dve.tensor_reduce(stat[:, 0:1], prb[:, 0:P], AX_X, ALU.max))
                step(dve.tensor_reduce(stat[:, 1:2], prb[:, P:3 * P], AX_X, ALU.max))
                settle()
                to_act(ts(stat[:, 2:4], stat[:, 0:2], -1.0))
                psum()
                to_pe(tt(bd["F"][:, :, :], bd["F"][:, :, :], b4(3), ALU.add))
                from_act()
                step(dve.reciprocal(stat[:, 6:8], stat[:, 4:6]))
                settle()
                step(ts(prb[:, 0:P], prb[:, 0:P], stat[:, 6:7]))
                to_pe(ts(prb[:, P:3 * P], prb[:, P:3 * P], stat[:, 7:8]))
                settle_pe()
                psum()
                to_pe(tt(bd["F"][:, :, :], bd["F"][:, :, :], b4(3), ALU.add))
                own_bank(1)
                psum()
                y_g = yall[:, bass.ds(g, 1), :].rearrange("p o t -> p (o t)")
                step(stt(y_g, banks[5][:, 0:T], 0.5, az[:, :], ALU.mult, ALU.mult))
                for c in range(NCH):
                    decay_c = ep4[:, c, CHUNK:CHUNK + 1]
                    if c:
                        if c < NCH - 1:
                            step(ts(S_dec[:, :], S[:, c % 2, :], decay_c))
                        psum()
                        to_pe(tt(SA[:, :], banks[2][:, 0:P], bd["b1"][:, c, :], ALU.add))
                        settle()
                    if c < NCH - 1:
                        psum()
                        if c == 0:
                            to_pe(ts(S[:, 1, :], banks[4][:, 0:P], decay_c))
                        else:
                            to_pe(stt(S[:, (c + 1) % 2, :], banks[4][:, 0:P], decay_c, S_dec[:, :], ALU.mult,
                                      ALU.add))
                        settle_pe()
                from_act()
                step(dve.reciprocal(sm["kk"][:, :], sm["kk"][:, :]))
                settle()
                step(tt(sm["k0"][:, :], banks[4][:, 0:T], sm["kk"][:, :], ALU.mult))
                settle()
                step(ts(sm["k0"][:, :], sm["k0"][:, :], rw(LN_W), rw(LN_B), ALU.mult, ALU.add))
                settle()
                step(tt(sm["k0"][:, :], sm["k0"][:, :], sm["bon"][:, :], ALU.add))
                settle()
                y_g = yall[:, bass.ds(g + 8, 1), :].rearrange("p o t -> p (o t)")
                to_pe(stt(y_g, sm["k0"][:, :], 0.5, sm["bz"][:, :], ALU.mult, ALU.mult))
                settle_pe()
            dve.memset(stat[:, 0:1], 0.0).then_inc(free_mem, 1)
            dve.wait_ge(free_mem, 1)
            dve.wait_ge(mem_in, 16)
            norm(memx, "mem_g", scratch3, mh_hi, mh_lo, croot)

            def head_norm(dst, g):
                from_act()
                step(dve.reciprocal(croot[:, :], croot[:, :]))
                settle()
                for s in range(2):
                    m = stt(dst(s), cpair[:, s, :], col(g, s), croot[:, :], ALU.mult, ALU.mult)
                to_pe(m)

            with n.loop(2, {"unit": 8, "act": 2, "step": 2, "to_pe": 2, ("fill", 0): 1, ("fill", 1): 1}) as i:
                for b in (0, 1):
                    split4()
                    n.next(("fill", b))
                    own_bank(b)
                    head_norm(lambda s: mk[:, bass.ds(i * 4 + (2 * b + s), 1), :].rearrange("p o t -> p (o t)"),
                              "ck_g")
            with n.loop(2, {"unit": 8, ("fill", 0): 1, ("fill", 1): 1}):
                split4(8)
                n.next(("fill", 0))
                n.next(("fill", 1))
            with n.loop(HEADS_C, {"unit": 8, "psum": 2, "act": 3, "step": 5, "to_pe": 2, "to_act": 1,
                                  ("fill", 0): 1, ("fill", 1): 1}) as h:
                split4()
                n.next(("fill", 0))
                own_bank(0)
                head_norm(lambda s: cpair[:, s, :], "cq_g")
                split4()
                n.next(("fill", 1))
                from_act()
                read(stt(cg[:, :, :], cg[:, :, :], 1.0, p2(1), ALU.add, ALU.mult), 1)
                step(dve.tensor_copy(mvh[:, :, :], mvt[:, :, bass.ds(h * (2 * P), 2 * P)]))
                psum()
                step(dve.tensor_reduce(cstat[:, 0:2], banks[3][:, :].rearrange("p (q t) -> p q t", q=2), AX_X,
                                       ALU.max))
                settle()
                to_act(ts(cstat[:, 2:4], cstat[:, 0:2], -1.0 / 16))
                from_act()
                step(dve.reciprocal(cstat[:, 6:8], cstat[:, 4:6]))
                settle()
                step(ts(cp[:, 0, :], cp[:, 0, :], cstat[:, 6:7]))
                to_pe(ts(cp[:, 1, :], cp[:, 1, :], cstat[:, 7:8]))
                psum()
                own_bank(1)
                stt(yall[:, bass.ds(h * 2 + 16, 2), :], banks[5][:, :].rearrange("p (s t) -> p s t", s=2), 0.5,
                    cg[:, :, :], ALU.mult, ALU.mult).then_inc(head_written, 1)
            for c in range(6):
                from_act()
                cs = slice(4 * c, 4 * c + 4)
                m = low(ya_lo[:, cs, :], yall[:, cs, :], ya_hi[:, cs, :])
            to_pe(m)
            settle_pe()
            with n.loop(4, {"unit": 36, "act": 2, "to_act": 2, "step": 2, ("fill", 0): 6, ("fill", 1): 6,
                            "merged": 2}) as i:
                for j in range(2):
                    for m3 in range(3):
                        split4()
                        n.next(("fill", 0))
                        split4(2)
                        own_bank(0)
                        group_done()
                        n.next(("fill", 1))
                        dst = mtmp if m3 else macc
                        read(stt(dst[:, :, :], gate[:, :, :], 1.0, p2(1), ALU.add, ALU.mult), 1)
                        own_bank(1)
                        if m3:
                            (to_act if m3 == 2 else step)(tt(macc[:, :, :], macc[:, :, :], mtmp[:, :, :], ALU.add))
                            settle()
                    settle_act()
                    from_act()
                    hi = mg_hi[:, bass.ds(i * 4 + 2 * j, 2), :].bitcast(F32)
                    stt(mg_lo[:, bass.ds(i * 4 + 2 * j, 2), :], macc[:, :, :], 0.5, hi, ALU.mult, ALU.subtract)\
                        .then_inc(merged_ready, 1)
                    dve.wait_ge(merged_ready, n.next("merged"))
            with n.loop(3, {"unit": 8, ("fill", 0): 1, ("fill", 1): 1}) as i:
                for b in (0, 1):
                    split4()
                    residual(i * 4 + 2 * b, b, obuf)
            split4()
            residual(12, 0, obuf)
            dve.wait_ge(unit_used, UNITS)
            read(tt(obuf[:, 14:16, :], x[:, 14:16, :], p2(1), ALU.add), 1)


SHAPES = {"units": (UNITS, P, UK * UN), "xT": (P, KT, T), "memT": (P, KT, T), "par": (P, NPAR),
          "con": (P, NCONST), "feat": (33, T), "fw1": (33, 64), "fw2": (64, 64), "fw3": (64, 2 * D_HY),
          "dft": (P, 4, 2, T), "decay": (P, 2, D_HY), "ws": (P, HY, P), "pw": (P, 4, P), "bs": (1, HY * P),
          "inv": (P, 4, T), "lora": (P, 1024), "bias": (HEADS_A, P, 384)}


def lay_out(v):
    def tiles(vec):
        return np.ascontiguousarray(vec.reshape(-1, P).T)

    def units(w, cols):
        w = w[:, cols].reshape(-1, UK, P, len(cols) // UN, UN)
        return w.transpose(3, 0, 2, 1, 4).reshape(-1, P, UK * UN)

    def cols_of(tile_list):
        return np.concatenate([np.arange(t * P, (t + 1) * P) for t in tile_list])

    def down(w, half):
        w = w[half * FF_HALF * P:(half + 1) * FF_HALF * P].reshape(11, 2, P, 4, 512)
        return w.transpose(3, 0, 2, 1, 4).reshape(-1, P, UK * UN)

    w_in = v["w_in"][0]
    order = list(range(4, 22)) + list(range(28, 34)) + list(range(22, 28)) + list(range(4))
    parts = [units(w_in, cols_of(order)), units(v["w_out"][0], np.arange(D))]
    up = v["ffn_w_up"][0]
    for half in range(2):
        ts_ = [t for j in range(half * FF_HALF, (half + 1) * FF_HALF) for t in (j, FF_TILES + j)]
        parts += [units(up, cols_of(ts_)), down(v["ffn_w_down"][0], half)]
    w2 = v["w_in_2"][0]
    AQ, AK, AV, AZ, BR, BK_, BV, BZ = (8 * i for i in range(8))
    lora = np.zeros((D, UN), np.float32)
    lora[:, 0:P] = w2[:, 64 * P:65 * P]
    parts.append(units(lora, np.arange(UN)))
    loop = [t for g in range(8) for t in (BR + g, BK_ + g, BV + g, BZ + g, AQ + g, AK + g, AV + g, AZ + g)]
    parts.append(units(w2, cols_of(loop)))
    parts.append(units(v["w_mem_kv_2"][0], np.arange(D)))
    CQ, CZ, GA = 65, 73, 81
    parts.append(units(w2, cols_of([t for h in range(4) for t in (CQ + 2 * h, CQ + 2 * h + 1, CZ + 2 * h,
                                                                  CZ + 2 * h + 1)])))
    ups = [v[n][0] for n in ("w_up_a_2", "w_up_b_2", "w_up_c_2")]
    for j in range(8):
        for m in range(3):
            t = GA + 16 * m + 2 * j
            parts.append(units(w2, cols_of([t, t + 1])))
            parts.append(units(ups[m], cols_of([2 * j, 2 * j + 1])))
    parts.append(units(v["w_o_2"][0], np.arange(D)))
    stream = np.concatenate(parts)

    par = np.zeros((P, NPAR), np.float32)

    def put(name, cols, at=0):
        par[:cols.shape[0], COL[name] + at:COL[name] + at + cols.shape[1]] = cols

    put("norm_mix", tiles(v["norm_mix"][0]))
    put("pool_b", tiles(v["pool_b"][0]))
    put("pool_scale", tiles(v["pool_scale"][0]))
    for k in range(3):
        put("hy_w", tiles(v["hy_short_w"][0][k]), 18 * k)
    put("hy_b", tiles(v["hy_short_b"][0]))
    put("hy_skip", tiles(v["hy_skip"][0]))
    put("gm_g", tiles(v["gm_ln_g"][0]))
    put("gm_b", tiles(v["gm_ln_b"][0]))
    put("norm_ffn", tiles(v["norm_ffn"][0]))
    ffn = np.stack([tiles(t) for t in (*v["ffn_conv_w"][0], v["ffn_conv_b"][0])], axis=-1)
    ffn = ffn.reshape(P, 2, FF_TILES, 4).transpose(0, 2, 1, 3).reshape(P, -1)
    put("ffn", ffn)
    put("norm_final", tiles(v["norm_final"]))
    put("norm_g", tiles(v["norm_g_2"][0]))
    put("mem_g", tiles(v["mem_norm_g_2"][0]))
    mu = v["b_mu_rkv_2"][0]
    rows = [mu[0], mu[1], mu[2], v["b_k_k_2"][0], v["b_k_a_2"][0], v["b_r_k_2"][0].reshape(-1), v["b_ln_w_2"][0],
            v["b_ln_b_2"][0]]
    for k, r in enumerate(rows):
        par[:, COL["rwkv"] + k:COL["rwkv"] + 80:RW_COLS] = tiles(r)
    put("mu_wa", np.concatenate([v["b_mu_w_2"][0], v["b_mu_a_2"][0]])[:, None])
    put("w0", tiles(v["b_w0_2"][0]))
    put("a0", tiles(v["b_a0_2"][0]))
    for name, key in (("aq_g", "a_q_g_2"), ("ak_g", "a_k_g_2"), ("cq_g", "c_q_g_2"), ("ck_g", "c_k_g_2")):
        put(name, tiles(v[key][0]))
    for name, key in (("f_b1", "hy_filt_b1"), ("f_fr1", "hy_filt_freq1"), ("f_b2", "hy_filt_b2"),
                      ("f_fr2", "hy_filt_freq2")):
        put(name, v[key][0][:, None])

    dft, feat, decay, inv = hyena_tables()
    q, k = np.arange(T)[:, None], np.arange(T)[None, :]
    rel = v["a_rel_bias_2"][0][:, np.clip(q - k, -P, P) + P]
    bias = np.concatenate([rel[:, 0:P, 0:P], rel[:, P:T, :]], axis=2)
    out = {
        "units": stream,
        "xT": v["x"][0].T.reshape(KT, P, T).transpose(1, 0, 2),
        "memT": v["mem_2"][0].T.reshape(KT, P, T).transpose(1, 0, 2),
        "par": par, "con": const_tables(), "feat": feat, "fw1": v["hy_filt_w1"][0], "fw2": v["hy_filt_w2"][0],
        "fw3": v["hy_filt_w3"][0], "dft": dft, "decay": decay, "inv": inv,
        "ws": v["gm_w_s"][0].transpose(2, 0, 1), "pw": v["pool_w"][0].transpose(1, 0, 2),
        "bs": v["gm_b_s"][0].reshape(1, -1),
        "lora": np.concatenate([v["b_w2_2"][0], v["b_a2_2"][0]]),
        "bias": bias,
    }
    return {name: np.ascontiguousarray(t) for name, t in out.items()}


def kernel(**inputs):
    import concourse.bacc as bacc
    from concourse.bass_utils import run_bass_kernel_spmd

    arrays = lay_out({k: np.asarray(v) for k, v in inputs.items()})
    nc = bacc.Bacc("TRN2", target_bir_lowering=False, num_devices=1)
    aps = {}
    for name, shape in SHAPES.items():
        assert arrays[name].shape == shape, (name, arrays[name].shape, shape)
        aps[name] = nc.dram_tensor(f"in_{name}", shape, F32, kind="ExternalInput").ap()
    aps["out"] = nc.dram_tensor("out_y", (P, KT, T), F32, kind="ExternalOutput").ap()
    build(nc, aps)
    r = run_bass_kernel_spmd(nc, [{f"in_{name}": t for name, t in arrays.items()}], core_ids=[0])
    y = r.results[0]["out_y"]
    return np.ascontiguousarray(y.transpose(1, 0, 2).reshape(D, T).T)[None]
```

```python
from contextlib import ExitStack, contextmanager
from itertools import count

import numpy as np

import concourse.bass as bass
from concourse import mybir

ALU = mybir.AluOpType
ACT = mybir.ActivationFunctionType
F32 = mybir.dt.float32
F32R = mybir.dt.float32r
AX_X = mybir.AxisListType.X

P = 128
T = 256
D = 2048
KT = D // P
HY = 6
D_HY = HY * P
FF_TILES = 5632 // P
FF_HALF = FF_TILES // 2
CHUNK = 64
NCH = T // CHUNK
HEADS_A = 8
HEADS_C = 4
SUB = 8
NEG = -1e30
TWO_PI = 2.0 * np.pi
ROUND = float(1.5 * 2 ** 23)
PI_HI = 6.28125
PI_LO = float(np.float32(TWO_PI - PI_HI))
PI_CUT = 3.1415925

RING = 4
UK = 4
UN = 256

U_IN = 17 * 4
U_OUT = 8 * 4
U_UP = FF_HALF * 4
U_DOWN = 4 * 11
U_LORA = 4
U_RA = HEADS_A * 16
U_MEM = 8 * 4
U_C = HEADS_C * 8
U_MERGE = 8 * 18
UNITS = U_IN + U_OUT + 2 * (U_UP + U_DOWN) + U_LORA + U_RA + U_MEM + U_C + U_MERGE + U_OUT

PARAMS = [("norm_mix", 16), ("pool_b", 4), ("pool_scale", 4), ("hy_w", 54), ("hy_b", 18), ("hy_skip", 6),
          ("gm_g", 6), ("gm_b", 6), ("norm_ffn", 16), ("ffn", 8 * FF_TILES), ("norm_final", 16),
          ("norm_g", 16), ("mem_g", 16), ("rwkv", 80), ("mu_wa", 1), ("w0", 8), ("a0", 8), ("aq_g", 1),
          ("ak_g", 1), ("cq_g", 2), ("ck_g", 2), ("f_b1", 1), ("f_fr1", 1), ("f_b2", 1), ("f_fr2", 1)]
COL = {}
_at = 0
for _name, _n in PARAMS:
    COL[_name] = _at
    _at += _n
NPAR = _at
MU_R, MU_K, MU_V, K_K, K_A, R_K, LN_W, LN_B, RW_COLS = 0, 1, 2, 3, 4, 5, 6, 7, 10

CONSTS = [("ident", 128), ("upper", 128), ("upper_in", 128), ("lower_in", 128), ("lower_out", 128),
          ("upper_eq", 64), ("ones", 128), ("head_ones", 128), ("center", 128), ("eps6", 1), ("eps5", 1),
          ("eps_gn", 1)]
CC = {}
_at = 0
for _name, _n in CONSTS:
    CC[_name] = (_at, _n)
    _at += _n
NCONST = _at


def const_tables():
    r = np.arange(P)[:, None]
    c = np.arange(P)[None, :]
    same = (r // 64) == (c // 64)
    block = (r // SUB) == (c // SUB)
    eye = (r == c)
    parts = {
        "ident": eye, "upper": same & (r < c), "upper_in": block & (r < c), "lower_in": block & (r > c),
        "lower_out": same & (r > c) & ~block, "upper_eq": (r % 64) <= np.arange(64)[None, :],
        "ones": np.ones((P, P)), "head_ones": same, "center": eye - same / 64.0,
        "eps6": np.full((P, 1), 1e-6), "eps5": np.full((P, 1), 1e-5), "eps_gn": np.full((P, 1), 64e-5),
    }
    return np.concatenate([parts[n].astype(np.float32) for n, _ in CONSTS], axis=1)


def hyena_tables():
    f32 = np.float32
    t = np.arange(T)
    theta = 2.0 * np.pi / (2 * T) * (np.arange(T) + 0.5)
    ang = t[:, None] * theta[None, :]
    cos, sin = np.cos(ang), np.sin(ang)
    tables = np.stack([cos, sin, cos.T / T, sin.T / T]).astype(f32)
    tables = tables.reshape(4, 2, P, T).transpose(2, 0, 1, 3)
    tt = np.linspace(0.0, 1.0, T, dtype=f32)[:, None]
    w = (2.0 * np.pi * np.arange(T)[:, None] / T).astype(f32)
    f = np.linspace(1e-4, 15, 16, dtype=f32)[None, :]
    fw = (f * w).astype(np.float64)
    feat = np.concatenate([tt, np.cos(fw), -np.sin(fw)], axis=-1).astype(f32)
    lo = np.log(1e-2)
    deltas = np.linspace(lo / 1.5, lo / 0.3, D_HY, dtype=f32)
    decay = np.exp(-(tt * np.abs(deltas)[None, :]).astype(np.float64)).astype(f32)
    decay = decay.reshape(2, P, D_HY).transpose(1, 0, 2)
    inv = np.zeros((4, T), f32)
    for g, win in enumerate((2, 4, 8, 16)):
        a = np.maximum(t - win // 2, 0)
        b = np.minimum(t + win // 2 - 1, T - 1)
        inv[g] = 1.0 / (b - a + 1)
    return tables, feat.T, decay, np.broadcast_to(inv, (P, 4, T))


class Counts:

    def __init__(self, eng):
        self.eng = eng
        self.base = {}
        self.extra = {}

    def next(self, key, by=1):
        self.extra[key] = self.extra.get(key, 0) + by
        return self.now(key)

    def now(self, key):
        return self.base.get(key, 0) + self.extra.get(key, 0)

    @contextmanager
    def loop(self, n, per):
        base, extra = self.base, self.extra
        keys = set(base) | set(extra) | set(per)
        before = {k: base.get(k, 0) + extra.get(k, 0) for k in keys}
        self.base, self.extra = {}, {}
        with self.eng.Fori(0, n) as i:
            for k in keys:
                self.base[k] = before[k] + i * per[k] if k in per else before[k]
            yield i
            moved = {k: v for k, v in self.extra.items() if v}
            assert moved == per, f"one iteration moves {moved}"
        self.base = base
        self.extra = {k: extra.get(k, 0) + n * per.get(k, 0) for k in keys}


def build(nc, a):
    out_ap = a["out"]
    with ExitStack() as ctx:
        def sb(name, shape, dt=F32):
            return ctx.enter_context(nc.sbuf_tensor(name, shape, dt))

        def sem(name):
            return ctx.enter_context(nc.semaphore(name))

        banks = [ctx.enter_context(nc.psum_tensor(f"bank{i}", [P, 512], F32)) for i in range(8)]

        raw = [sb(f"raw{i}", [P, UK, UN]) for i in range(RING)]
        w_hi = [sb(f"w_hi{i}", [P, UK, UN], F32R) for i in range(RING)]
        w_lo = [sb(f"w_lo{i}", [P, UK, UN], F32R) for i in range(RING)]
        x = sb("x", [P, KT, T])
        h_hi = sb("h_hi", [P, KT, T], F32R)
        h_lo = sb("h_lo", [P, KT, T], F32R)
        par = sb("par", [P, NPAR])
        con = sb("con", [P, NCONST])
        arena_at = nc.sbuf_base
        arena_at = (arena_at + 31) // 32 * 32
        usable = nc.sbuf_usable_end - arena_at

        placed = {}

        def place(name, shape, at, dt=F32):
            size = 4 * int(np.prod(shape[1:]))
            assert at + size <= usable, (name, at + size, usable)
            placed[name] = at + size
            return nc.alloc_sbuf_tensor_at(name, shape, dt, offset=arena_at + at)

        K = 1024
        y_hi = place("y_hi", [P, KT, T], 0, F32R)
        y_lo = place("y_lo", [P, KT, T], 16 * K, F32R)
        scratch = place("scratch", [P, KT, T], 0)
        root = place("root", [P, T], 103 * K)
        x0 = place("x0", [P, HY, T], 32 * K)
        z1 = place("z1", [P, HY, T], 38 * K)
        zv = place("zv", [P, HY, T], 44 * K)
        k_re = place("k_re", [P, 2, D_HY], 50 * K)
        k_im = place("k_im", [P, 2, D_HY], 56 * K)
        dft = place("dft", [P, 4, 2, T], 62 * K)
        decay = place("decay", [P, 2, D_HY], 70 * K)
        f_fwd = place("f_fwd", [P, 2, D_HY], 76 * K)
        f_bwd = place("f_bwd", [P, 2, D_HY], 82 * K)
        f_sum = place("f_sum", [P, 2, D_HY], 88 * K)
        feat = place("feat", [33, T], 94 * K)
        fw1 = place("fw1", [33, 64], 95 * K)
        fw2 = place("fw2", [64, 64], 95 * K + 256)
        fh = [place(f"fh{i}", [64, T], (96 + i) * K) for i in range(4)]
        fw3 = place("fw3", [64, 2 * D_HY], 16 * K)
        gv = place("gv", [P, HY, T], 70 * K)
        gu = place("gu", [P, HY, T], 76 * K)
        gsq = place("gsq", [P, HY, T], 82 * K)
        gvt = place("gvt", [P, 2, D_HY], 82 * K)
        zt = place("zt", [P, 2, D_HY], 88 * K)
        ws = place("ws", [P, HY, P], 94 * K)
        pw = place("pw", [P, 4, P], 97 * K)
        bs = place("bs", [1, HY * P], 99 * K)
        prod = [place(f"prod{i}", [P, 384], (38 + 6) * K + 1536 * i) for i in range(4)]
        mix = place("mix", [P, 2, T], 44 * K)
        PW = 272
        pool_x = place("pool_x", [P, 4, PW], 50 * K)
        pool_a = place("pool_a", [P, 4, PW], 50 * K + 4352)
        pool_b = place("pool_b", [P, 4, PW], 50 * K + 2 * 4352)
        inv = place("inv", [P, 4, T], 64 * K)
        pool_d = place("pool_d", [P, 4, T], 32 * K)
        y_part = place("y_part", [P, 4, T], 88 * K)
        m_hi = place("m_hi", [P, FF_HALF, T], 0, F32R)
        m_lo = place("m_lo", [P, FF_HALF, T], 22 * K, F32R)
        scratch2 = place("scratch2", [P, KT, T], 46 * K)
        conv_o = place("conv_o", [P, 2, 2, T], 62 * K)
        conv_m = place("conv_m", [P, 2, T], 66 * K)
        root2 = place("root2", [P, T], 70 * K)
        yall = place("yall", [P, 24, T], 0)
        cum = place("cum", [P, 8, T], 24 * K)
        icl = place("icl", [P, 8, T], 32 * K)
        bd = {}
        at = 40 * K
        for n in ("a", "b", "k", "v", "Nt", "N", "No", "Kt", "Q", "F", "Vt", "At", "Bt", "Kk", "b1", "b2",
                  "b3", "AkV", "Y"):
            bd[n] = place("m_" + n, [P, NCH, P], at)
            at += 2 * K
        BK = place("m_BK", [P, 2, NCH, CHUNK], at)
        at += 2 * K
        small = {}
        for n, w in (("pr", 257), ("pk", 257), ("pv", 257), ("t0", 256), ("r", 256), ("k0", 256), ("v", 256),
                     ("k2", 256), ("kk", 256), ("sq", 256), ("rk", 256), ("bz", 256), ("ep", 260), ("en", 256),
                     ("rt", 256), ("bon", 256)):
            small[n] = place("s_" + n, [P, w], at)
            at += (4 * w + 31) // 32 * 32
        for i, n in ((0, "o"), (1, "gsq"), (2, "groot"), (0, "gk")):
            small[n] = place("s_" + n, [P, T], (16 + i) * K)
        prb = place("prb", [P, 384], 20 * K)
        av_t = place("av_t", [P, 2, P], 20 * K + 1536)
        avf = place("avf", [P, T], 21 * K + 1536)
        S = place("S", [P, 2, P], at)
        SA = place("SA", [P, 2, P], 19 * K)
        S_dec = place("S_dec", [P, P], at + 1024)
        at += 1536
        qk = place("qk", [P, 2, T], at)
        qr = place("qr", [P, 2, T], at + 2048)
        az = place("az", [P, T], at + 4096)
        bias_t = place("bias_t", [P, 384], at + 5120)
        stat = place("stat", [P, 16], at + 6656)
        prt = place("prt", [P, 384], at + 2048)
        lora = place("lora", [P, 1024], 40 * K)
        lx = place("lx", [P, 257], 44 * K)
        lt = place("lt", [P, T], 46 * K)
        ping = place("ping", [P, 8, T], 48 * K)
        cqs = place("cqs", [P, 8, T], 24 * K)
        czs = place("czs", [P, 8, T], 32 * K)
        memx = place("memx", [P, KT, T], 40 * K)
        mh_hi = place("mh_hi", [P, KT, T], 56 * K, F32R)
        mh_lo = place("mh_lo", [P, KT, T], 72 * K, F32R)
        scratch3 = place("scratch3", [P, KT, T], 88 * K)
        croot = place("croot", [P, T], 23 * K)
        csq = place("csq", [P, 2, T], 20 * K)
        mk = place("mk", [P, 8, T], 40 * K)
        mvt = place("mvt", [P, 2, 8 * P], 48 * K)
        cpair = place("cpair", [P, 2, T], 88 * K)
        cp = place("cp", [P, 2, T], 90 * K)
        msq = place("msq", [P, 2, T], 92 * K)
        mroot = place("mroot", [P, T], 94 * K)
        cstat = place("cstat", [P, 16], 95 * K)
        cpt = [place(f"cpt{h}", [P, 2, T], (96 + 2 * h) * K) for h in range(HEADS_C)]
        ya_hi = place("ya_hi", [P, 24, T], 24 * K, F32R)
        ya_lo = place("ya_lo", [P, 24, T], 48 * K, F32R)
        gate = place("gate", [P, 2, T], 72 * K)
        macc = place("macc", [P, 2, T], 74 * K)
        mtmp = place("mtmp", [P, 2, T], 76 * K)
        mg_hi = place("mg_hi", [P, KT, T], 78 * K, F32R)
        mg_lo = place("mg_lo", [P, KT, T], 0, F32R)
        obuf = place("obuf", [P, KT, T], 24 * K)

        landed = [sem(f"unit_landed{i}") for i in range(RING)]
        hi_done = sem("hi_done")
        split_done = sem("split_done")
        unit_used = sem("unit_used")
        bank_read = [sem(f"bank_read{i}") for i in range(4)]
        psum_for_dve = sem("psum_for_dve")
        psum_for_act = sem("psum_for_act")
        dve_for_pe = sem("dve_for_pe")
        act_for_pe = sem("act_for_pe")
        dve_for_act = sem("dve_for_act")
        act_for_dve = sem("act_for_dve")
        dve_step = sem("dve_step")
        x_in = sem("x_in")
        tab_in = sem("tab_in")
        filt_in = sem("filt_in")
        mixer_in = sem("mixer_in")
        inv_in = sem("inv_in")
        mem_in = sem("mem_in")
        lora_in = sem("lora_in")
        free_early = sem("free_early")
        free_inv = sem("free_inv")
        free_lora = sem("free_lora")
        free_mem = sem("free_mem")
        keys_ready = sem("keys_ready")
        head_sums = sem("head_sums")
        sums_read = sem("sums_read")
        qk_squared = sem("qk_squared")
        qk_sums = sem("qk_sums")
        bias_in = sem("bias_in")
        bias_used = sem("bias_used")
        hidden_ready = sem("hidden_ready")
        head_written = sem("head_written")
        merged_ready = sem("merged_ready")
        stored = sem("stored")

        PROJ = [banks[0], banks[1], banks[3], banks[4]]

        def p2(b):
            return PROJ[b][:, :].rearrange("p (s t) -> p s t", s=2)

        def col(name, i=0):
            return par[:, bass.ds(COL[name] + i, 1)]

        def con_(name):
            s, n = CC[name]
            return con[:, s:s + n]

        def b4(bank):
            return banks[bank][:, :].rearrange("p (c t) -> p c t", c=4)

        def bcast(ap2d, n):
            return ap2d.unsqueeze(1).broadcast_to([P, n, ap2d.shape[1]])

        final_fill = {}
        block = ctx.enter_context(nc.Block())

        @block.gpsimd
        def _(pool):
            for dst, src in ((feat[:, :], "feat"), (fw1[:, :], "fw1"), (fw2[:, :], "fw2"), (fw3[:, :], "fw3"),
                             (dft[:, :, :, :], "dft"), (decay[:, :, :], "decay")):
                pool.dma_start(dst, a[src]).then_inc(filt_in, 16)
            pool.wait_ge(free_early, 1)
            for dst, src in ((ws[:, :, :], "ws"), (pw[:, :, :], "pw"), (bs[:, :], "bs")):
                pool.dma_start(dst, a[src]).then_inc(mixer_in, 16)
            pool.wait_ge(free_inv, 1)
            pool.dma_start(inv[:, :, :], a["inv"]).then_inc(inv_in, 16)
            pool.wait_ge(free_lora, 1)
            pool.dma_start(lora[:, :], a["lora"]).then_inc(lora_in, 16)
            with pool.Fori(0, HEADS_A) as g:
                pool.wait_ge(bias_used, g + 1)
                pool.dma_start(bias_t[:, :], a["bias"][g]).then_inc(bias_in, 16)
            pool.wait_ge(free_mem, 1)
            pool.dma_start(memx[:, :, :], a["memT"]).then_inc(mem_in, 16)

        @block.tensor
        def _(pe):
            n = Counts(pe)
            slots = count()

            def mm(out, lhsT, rhs, start=True, stop=True):
                return pe.matmul(out, lhsT, rhs, start=start, stop=stop, skip_group_check=True)

            def unit(bank, k0, hi, lo, first, last, tiles=2, fresh=True):
                slot = next(slots) % RING
                pe.wait_ge(split_done, n.next("split"))
                o = p2(bank)
                for kk in range(UK):
                    for t in range(tiles):
                        wh = w_hi[slot][:, kk, t * P:(t + 1) * P]
                        wl = w_lo[slot][:, kk, t * P:(t + 1) * P]
                        rh, rl = hi[:, k0 + kk, :], lo[:, k0 + kk, :]
                        mm(o[:, t, :], wh, rh, first and kk == 0 and t == 0, False)
                        mm(o[:, t, :], wh, rl, False, False)
                        m = mm(o[:, t, :], wl, rh, False, last and kk == UK - 1 and t == tiles - 1)
                m.then_inc(unit_used, 1)

            def group(bank, hi, lo, k0=0, units=4, tiles=2, filled=True):
                if filled:
                    pe.wait_ge(bank_read[bank], n.now(("fill", bank)))
                n.next(("fill", bank))
                for u in range(units):
                    unit(bank, k0 + UK * u, hi, lo, u == 0, u == units - 1, tiles)

            def from_dve(k=1):
                pe.wait_ge(dve_for_pe, n.next("dve", k))

            def from_act(k=1):
                pe.wait_ge(act_for_pe, n.next("act", k))

            def norm_sums(src):
                for c in range(4):
                    from_act()
                    for t in range(4 * c, 4 * c + 4):
                        m = mm(banks[2][:, 0:T], con_("ones"), src[:, t, :], t == 0, t == KT - 1)
                m.then_inc(psum_for_act, 1)

            pe.wait_ge(tab_in, 32)
            norm_sums(scratch)
            from_dve()
            group(0, h_hi, h_lo, filled=False)
            pe.wait_ge(filt_in, 6 * 16)
            mm(banks[3][0:64, 0:T], fw1[:, :], feat[:, :]).then_inc(psum_for_dve, 1)
            group(1, h_hi, h_lo, filled=False)
            from_act()
            mm(banks[3][0:64, 0:T], fw2[:, :], fh[3][:, :]).then_inc(psum_for_dve, 1)
            group(0, h_hi, h_lo)
            from_act()
            for c in range(2):
                for q in range(4):
                    if c == 1:
                        from_dve()
                    mm(banks[3 + q][:, 0:384], fh[3][:, c * P:(c + 1) * P], fw3[:, q * 384:(q + 1) * 384])\
                        .then_inc(psum_for_dve, 1)
            group(1, h_hi, h_lo)
            from_dve(4)
            from_dve()
            for q, (tab, src) in enumerate(((0, f_sum), (1, f_bwd))):
                for f in range(2):
                    for c in range(2):
                        b = 3 + (4 * q + 2 * f + c) % 4
                        if q == 1:
                            from_act()
                        for k in range(2):
                            m = mm(banks[b][:, 0:384], dft[:, tab, k, f * P:(f + 1) * P],
                                   src[:, k, c * 384:(c + 1) * 384], k == 0, k == 1)
                        m.then_inc(psum_for_act, 1)
            from_act(4)
            for p in range(4, 9):
                group(p % 2, h_hi, h_lo)
            group(1, h_hi, h_lo)
            from_dve()
            for c in range(2):
                for half in range(2):
                    b = 3 + 2 * c + half
                    for j in range(3):
                        m = pe.transpose(banks[b][:, j * P:(j + 1) * P], z1[:, 3 * half + j, c * P:(c + 1) * P],
                                         con_("ident"))
                    m.then_inc(psum_for_act, 1)
            group(0, h_hi, h_lo)
            group(1, h_hi, h_lo)
            from_act(4)
            for i, (f, c) in enumerate(((0, 0), (0, 1), (1, 0), (1, 1))):
                if i >= 2:
                    from_dve()
                for part in range(2):
                    b = 3 + 2 * (i % 2) + part
                    for k in range(2):
                        m = mm(banks[b][:, 0:384], dft[:, part, k, f * P:(f + 1) * P],
                               zt[:, k, c * 384:(c + 1) * 384], k == 0, k == 1)
                m.then_inc(psum_for_dve, 1)
            group(0, h_hi, h_lo)
            from_dve(3)
            for j in range(HY):
                o = banks[3 + j // 2][:, (j % 2) * T:(j % 2 + 1) * T]
                for i, (src, tab, k) in enumerate(((k_re, 2, 0), (k_re, 2, 1), (k_im, 3, 0), (k_im, 3, 1))):
                    m = mm(o, src[:, k, j * P:(j + 1) * P], dft[:, tab, k, :], i == 0, i == 3)
                if j % 2:
                    m.then_inc(psum_for_dve, 1)
            from_act()
            for j in range(HY):
                m = mm(banks[6][:, 0:T], con_("ones"), gv[:, j, :], j == 0, j == HY - 1)
            m.then_inc(psum_for_dve, 1)
            group(1, h_hi, h_lo)
            from_act()
            for j in range(HY):
                m = mm(banks[7][:, 0:T], con_("ones"), gsq[:, j, :], j == 0, j == HY - 1)
            m.then_inc(psum_for_act, 1)
            group(0, h_hi, h_lo)
            from_dve()
            for e in range(HY):
                for c in range(2):
                    i = 2 * c + e % 2
                    m = pe.transpose(banks[3 + e // 2][:, i * P:(i + 1) * P], gv[:, e, c * P:(c + 1) * P],
                                     con_("ident"))
                if e % 2:
                    m.then_inc(psum_for_act, 1)
            group(1, h_hi, h_lo)
            pe.wait_ge(mixer_in, 3 * 16)
            from_act(3)
            for e in range(HY):
                for c in range(2):
                    o = banks[3 + e // 2][:, (e % 2) * T + c * P:(e % 2) * T + (c + 1) * P]
                    mm(o, gvt[:, c, e * P:(e + 1) * P], ws[:, e, :], True, False)
                    m = mm(o, con[0:1, CC["ones"][0]:CC["ones"][0] + P], bs[0:1, e * P:(e + 1) * P], False, True)
                if e % 2:
                    m.then_inc(psum_for_dve, 1)
            group(0, h_hi, h_lo)
            from_dve()
            for g in range(4):
                m = mm(banks[6 + g // 2][:, (g % 2) * T:(g % 2 + 1) * T], pw[:, g, :], pool_d[:, g, :])
            m.then_inc(psum_for_dve, 1)
            from_dve()
            with n.loop(4, {("fill", 0): 1, ("fill", 1): 1, "split": 8}):
                group(1, y_hi, y_lo)
                group(0, y_hi, y_lo)
            norm_sums(scratch2)
            from_dve()
            n.next(("fill", 2))
            n.next(("fill", 3))
            with n.loop(2, {("fill", 0): 13, ("fill", 1): 13, ("fill", 2): 2, ("fill", 3): 2,
                            "split": U_UP + U_DOWN, "hidden": FF_HALF}):
                with n.loop(FF_HALF // 2, {("fill", 0): 1, ("fill", 1): 1, "split": 8}):
                    group(1, h_hi, h_lo)
                    group(0, h_hi, h_lo)
                pe.wait_ge(hidden_ready, n.next("hidden", FF_HALF))
                for q in range(4):
                    pair = (0, 1) if q % 2 == 0 else (2, 3)
                    for b in pair:
                        pe.wait_ge(bank_read[b], n.now(("fill", b)))
                        n.next(("fill", b))
                    for u in range(11):
                        slot = next(slots) % RING
                        pe.wait_ge(split_done, n.next("split"))
                        wh4 = w_hi[slot][:, :, :].rearrange("p k n -> p (k n)").rearrange("p (k n) -> p k n", k=2)
                        wl4 = w_lo[slot][:, :, :].rearrange("p k n -> p (k n)").rearrange("p (k n) -> p k n", k=2)
                        for kk in range(2):
                            for t in range(4):
                                o = p2(pair[t // 2])[:, t % 2, :]
                                wh, wl = wh4[:, kk, t * P:(t + 1) * P], wl4[:, kk, t * P:(t + 1) * P]
                                rh, rl = m_hi[:, 2 * u + kk, :], m_lo[:, 2 * u + kk, :]
                                mm(o, wh, rh, u == 0 and kk == 0 and t % 2 == 0, False)
                                mm(o, wh, rl, False, False)
                                m = mm(o, wl, rh, False, u == 10 and kk == 1 and t % 2 == 1)
                        m.then_inc(unit_used, 1)
            norm_sums(scratch2)
            norm_sums(scratch2)
            from_dve()
            group(1, h_hi, h_lo, tiles=1)
            from_act()
            pe.wait_ge(lora_in, 16)
            for j in range(8):
                if j >= 2:
                    from_act()
                mm(banks[3 + j % 2][:, 0:T], lora[0:64, j * P:(j + 1) * P], lt[0:64, :])
                mm(banks[5 + j % 2][:, 0:T], lora[64:128, j * P:(j + 1) * P], lt[64:128, :])\
                    .then_inc(psum_for_act, 1)
            from_act(2)

            ident = con_("ident")

            def per_chunk(bank, lhs, rhs):
                o = b4(bank)
                for c in range(NCH):
                    m = mm(o[:, c, :], lhs[:, c, :], rhs[:, c, :])
                return m

            def turned(bank, src):
                o = b4(bank)
                for c in range(NCH):
                    m = pe.transpose(o[:, c, :], src[:, c, :], ident)
                return m

            def part(k, half=None, hi=h_hi, lo=h_lo, banks_of=(0, 1, 0, 1)):
                bank = banks_of[k // 4]
                if half != 1:
                    if k % 4 == 0:
                        pe.wait_ge(bank_read[bank], n.now(("fill", bank)))
                        n.next(("fill", bank))
                    pe.wait_ge(split_done, n.next("split"))
                    part.slot = next(slots) % RING
                slot = part.slot
                o = p2(bank)
                for kk in {None: range(4), 0: range(2), 1: range(2, 4)}[half]:
                    for t in range(2):
                        wh = w_hi[slot][:, kk, t * P:(t + 1) * P]
                        wl = w_lo[slot][:, kk, t * P:(t + 1) * P]
                        rh, rl = hi[:, (k % 4) * UK + kk, :], lo[:, (k % 4) * UK + kk, :]
                        mm(o[:, t, :], wh, rh, k % 4 == 0 and kk == 0 and t == 0, False)
                        mm(o[:, t, :], wh, rl, False, False)
                        m = mm(o[:, t, :], wl, rh, False, k % 4 == 3 and kk == 3 and t == 1)
                if half != 0:
                    m.then_inc(unit_used, 1)

            def heads(k, half=None):
                part(k, half)
                if k == 9 and half != 0:
                    pe.wait_ge(keys_ready, n.next("keys"))
                    mm(banks[7][:, 0:T], con_("head_ones"), small["sq"][:, :])
                    mm(banks[7][:, T:2 * T], con_("head_ones"), small["rk"][:, :]).then_inc(head_sums, 1)
                if k == 12:
                    pe.wait_ge(sums_read, n.next("sums"))
                    pe.wait_ge(qk_squared, n.next("qk"))
                    mm(banks[7][:, :], con_("ones"), qr[:, :, :].rearrange("p s t -> p (s t)")).then_inc(qk_sums, 1)

            def late(units):
                units(0)
                from_dve()
                a_, b_, k_, v_ = bd["a"], bd["b"], bd["k"], bd["v"]
                per_chunk(3, b_, a_).then_inc(psum_for_dve, 1)
                per_chunk(4, a_, b_).then_inc(psum_for_dve, 1)
                per_chunk(5, k_, a_).then_inc(psum_for_dve, 1)
                o6 = banks[6][:, :].rearrange("p (q c t) -> p q c t", q=2, c=NCH)
                for q, lhs in enumerate((b_, k_)):
                    for c in range(NCH):
                        m = mm(o6[:, q, c, :], lhs[:, c, :], small["rt"][:, c * CHUNK:(c + 1) * CHUNK])
                m.then_inc(psum_for_dve, 1)
                turned(2, v_).then_inc(psum_for_act, 1)
                from_act()
                for c in range(2):
                    m = pe.transpose(banks[7][:, c * P:(c + 1) * P], avf[:, c * P:(c + 1) * P], ident)
                m.then_inc(psum_for_act, 1)
                units(1)
                from_dve()
                per_chunk(3, bd["Nt"], bd["N"]).then_inc(psum_for_act, 1)
                per_chunk(4, bd["N"], bd["Nt"]).then_inc(psum_for_act, 1)
                from_dve()
                from_act()
                per_chunk(5, bd["Kt"], bd["Vt"]).then_inc(psum_for_act, 1)
                turned(6, a_).then_inc(psum_for_act, 1)
                turned(2, b_).then_inc(psum_for_act, 1)
                from_act()
                from_act(2)
                per_chunk(3, bd["b1"], bd["Q"]).then_inc(psum_for_dve, 1)
                per_chunk(4, bd["b2"], bd["b1"]).then_inc(psum_for_act, 1)
                mm(banks[7][:, 0:P], qk[:, 0, 0:P], qk[:, 1, 0:P])
                mm(banks[7][:, P:P + T], qk[:, 0, P:T], qk[:, 1, :]).then_inc(psum_for_dve, 1)
                units(2)
                from_act(3)
                turned(5, k_).then_inc(psum_for_act, 1)
                from_dve()
                from_act()
                per_chunk(3, bd["b3"], bd["Q"]).then_inc(psum_for_dve, 1)
                units(3)
                from_dve()
                from_act()
                per_chunk(3, bd["No"], bd["Q"]).then_inc(psum_for_dve, 1)
                per_chunk(4, bd["Q"], bd["No"]).then_inc(psum_for_act, 1)
                per_chunk(5, bd["Q"], bd["At"]).then_inc(psum_for_act, 1)
                per_chunk(6, bd["Q"], bd["AkV"]).then_inc(psum_for_act, 1)
                from_dve()
                from_act(1)
                per_chunk(3, bd["b2"], bd["b1"]).then_inc(psum_for_act, 1)
                per_chunk(4, bd["b1"], bd["b2"]).then_inc(psum_for_act, 1)
                units(4)
                from_act(2)
                from_act(2)
                per_chunk(3, bd["N"], bd["F"]).then_inc(psum_for_dve, 1)
                per_chunk(4, bd["Nt"], bd["N"]).then_inc(psum_for_act, 1)
                from_dve()
                for i, o in enumerate((0, P, 2 * P)):
                    m = pe.transpose(banks[7][:, i * P:(i + 1) * P], prb[:, o:o + P], ident)
                m.then_inc(psum_for_act, 1)
                units(5)
                from_act(1)
                from_dve()
                per_chunk(3, bd["b3"], bd["F"]).then_inc(psum_for_dve, 1)
                units(6)
                from_dve()
                per_chunk(5, bd["Y"], bd["F"]).then_inc(psum_for_act, 1)
                per_chunk(6, bd["F"], bd["Kt"]).then_inc(psum_for_act, 1)
                units(7, 0)
                from_act(3)

                def sa_of(c):
                    return SA[:, c % 2, :] if c else bd["b1"][:, 0, :]

                def state(c):
                    mm(banks[4][:, 0:P], bd["Bt"][:, c, :], sa_of(c), True, False)
                    mm(banks[4][:, 0:P], bd["Kk"][:, c, :], bd["Vt"][:, c, :], False, True)\
                        .then_inc(psum_for_dve, 1)

                def output(c):
                    cs = slice(c * CHUNK, (c + 1) * CHUNK)
                    mm(banks[3][:, cs], sa_of(c), BK[:, 0, c, :], True, False)
                    if c:
                        mm(banks[3][:, cs], S[:, c % 2, :], small["rt"][:, cs], False, False)
                    return mm(banks[3][:, cs], bd["Vt"][:, c, :], BK[:, 1, c, :], False, True)

                def solve(c):
                    from_dve()
                    mm(banks[2][:, 0:P], bd["b2"][:, c, :], S[:, c % 2, :]).then_inc(psum_for_dve, 1)

                state(0)
                output(0)
                mm(banks[5][:, 0:P], av_t[:, 0, :], prt[:, 0:P])
                mm(banks[5][:, P:T], av_t[:, 0, :], prt[:, P:T], True, False)
                mm(banks[5][:, P:T], av_t[:, 1, :], prt[:, T:T + P], False, True).then_inc(psum_for_dve, 1)
                units(7, 1)
                solve(1)
                units(8, 0)
                from_dve()
                state(1)
                output(1)
                units(8, 1)
                solve(2)
                units(9, 0)
                from_dve()
                state(2)
                output(2)
                units(9, 1)
                solve(3)
                units(10)
                from_dve()
                output(3).then_inc(psum_for_act, 1)
                units(11, 0)
                from_act()
                mm(banks[4][:, 0:T], con_("center"), small["o"][:, :]).then_inc(psum_for_act, 1)
                units(11, 1)
                from_act()
                mm(banks[6][:, 0:T], con_("head_ones"), small["gsq"][:, :]).then_inc(psum_for_act, 1)
                for k in range(12, 16):
                    units(k)

            late_counts = {"dve": 15, "act": 21}
            pair_counts = {("fill", 0): 2, ("fill", 1): 2, "split": 16, "keys": 1, "sums": 1, "qk": 1}
            for k in range(16):
                heads(k)
            with n.loop(HEADS_A - 1, late_counts | pair_counts):
                late(heads)
            late(part)

            def channel_sums(src, bank=7):
                for s in range(2):
                    m = mm(banks[bank][:, 0:T], con_("ones"), src[:, s, :], s == 0, s == 1)
                m.then_inc(psum_for_act, 1)

            for h in range(HEADS_C):
                part(4 * h)
                from_act()
                channel_sums(csq)
                for k in range(1, 4):
                    part(4 * h + k)
            norm_sums(scratch3)
            from_dve()
            for j in range(4):
                part(4 * j, None, mh_hi, mh_lo)
                if j:
                    from_act()
                    channel_sums(msq)
                for k in range(1, 4):
                    part(4 * j + k, None, mh_hi, mh_lo)
            for j in range(4):
                part(4 * j, None, mh_hi, mh_lo)
                if j == 0:
                    from_act()
                    channel_sums(msq)
                else:
                    pe.wait_ge(bank_read[(j - 1) % 2], n.now(("fill", (j - 1) % 2)))
                    for c in range(2):
                        for s in range(2):
                            m = pe.transpose(banks[6][:, (2 * c + s) * P:(2 * c + s + 1) * P],
                                             cpair[:, s, c * P:(c + 1) * P], ident)
                    m.then_inc(psum_for_act, 1)
                part(4 * j + 1, None, mh_hi, mh_lo)
                if j == 0:
                    from_dve()
                for q in range(2):
                    for s in range(2):
                        m = mm(banks[3][:, q * T:(q + 1) * T], cqs[:, 2 * j + s, q * P:(q + 1) * P],
                               mk[:, 2 * j + s, :], s == 0, s == 1)
                m.then_inc(psum_for_dve, 1)
                part(4 * j + 2, None, mh_hi, mh_lo)
                part(4 * j + 3, None, mh_hi, mh_lo)
                from_dve()
                for c in range(2):
                    for q in range(2):
                        m = pe.transpose(banks[4][:, (2 * c + q) * P:(2 * c + q + 1) * P],
                                         cp[:, q, c * P:(c + 1) * P], ident)
                m.then_inc(psum_for_act, 1)
                from_act(2 if j else 1)
            pe.wait_ge(bank_read[1], n.now(("fill", 1)))
            for c in range(2):
                for s in range(2):
                    m = pe.transpose(banks[6][:, (2 * c + s) * P:(2 * c + s + 1) * P],
                                     cpair[:, s, c * P:(c + 1) * P], ident)
            m.then_inc(psum_for_act, 1)
            from_act()
            for h in range(HEADS_C):
                o = banks[(3, 4, 5, 7)[h]]
                for s in range(2):
                    for c in range(2):
                        m = mm(o[:, s * T:(s + 1) * T], mvt[:, c, (2 * h + s) * P:(2 * h + s + 1) * P],
                               cpt[h][:, c, :], c == 0, c == 1)
                m.then_inc(psum_for_dve, 1)
            from_dve()
            with n.loop(4, {("fill", 0): 6, ("fill", 1): 6, "split": 36}):
                for j in range(2):
                    for m3 in range(3):
                        group(0, h_hi, h_lo)
                        group(1, ya_hi, ya_lo, k0=8 * m3, units=2)
            pe.wait_ge(merged_ready, 8)
            final_fill.update({b: n.now(("fill", b)) for b in (0, 1)})
            with n.loop(4, {("fill", 0): 1, ("fill", 1): 1, "split": 8}):
                group(0, mg_hi, mg_lo)
                group(1, mg_hi, mg_lo)
        @block.sync
        def _(sp):
            sp.dma_start(x[:, :, :], a["xT"]).then_inc(x_in, 16)
            sp.dma_start(par[:, :], a["par"]).then_inc(tab_in, 16)
            sp.dma_start(con[:, :], a["con"]).then_inc(tab_in, 16)
            for s in range(RING):
                sp.dma_start(raw[s][:, :, :], a["units"][s].rearrange("p (k n) -> p k n", k=UK))\
                    .then_inc(landed[s], 16)
            with sp.Fori(1, UNITS // RING) as i:
                for s in range(RING):
                    sp.wait_ge(split_done, i * RING + (s - RING + 1))
                    sp.dma_start(raw[s][:, :, :], a["units"][i * RING + s].rearrange("p (k n) -> p k n", k=UK))\
                        .then_inc(landed[s], 16)
            for j in range(8):
                sp.wait_ge(bank_read[j % 2], final_fill[j % 2] + j // 2 + 1)
                sp.dma_start(out_ap[:, 2 * j:2 * j + 2, :], obuf[:, 2 * j:2 * j + 2, :]).then_inc(stored, 16)
            sp.wait_ge(stored, 16 * 8)


        @block.scalar
        def _(act):
            n = Counts(act)
            slots = count()

            def send(ins, to):
                ins.then_inc(to, 1)

            def copy(out, in_, scale=1.0):
                return act.activation(out, in_, ACT.Copy, scale=scale)

            def split():
                slot = next(slots) % RING
                u = n.next("unit")
                act.wait_ge(landed[slot], n.next(("landed", slot), 16))
                if not isinstance(u, int) or u > RING:
                    act.wait_ge(unit_used, u - RING)
                copy(w_hi[slot][:, :, :], raw[slot][:, :, :]).then_inc(hi_done, 1)

            def split4(k=4):
                for _ in range(k):
                    split()

            def group_done():
                act.wait_ge(unit_used, n.now("unit") - RING)

            def psum(k=1):
                act.wait_ge(psum_for_act, n.next("psum", k))

            def from_dve(k=1):
                act.wait_ge(dve_for_act, n.next("dve", k))

            def to_pe(ins):
                ins.then_inc(act_for_pe, 1)

            def to_dve(ins):
                ins.then_inc(act_for_dve, 1)

            def norm(src, sq, hi, rt, split_it=True):
                for c in range(4):
                    cs = slice(4 * c, 4 * c + 4)
                    to_pe(act.activation(sq[:, cs, :], src[:, cs, :], ACT.Square))
                psum()
                to_dve(act.activation(rt[:, :], banks[2][:, 0:T], ACT.Sqrt, bias=con_("eps6"), scale=1.0 / D))
                if split_it:
                    for c in range(4):
                        cs = slice(4 * c, 4 * c + 4)
                        from_dve()
                        to_dve(copy(hi[:, cs, :], sq[:, cs, :]))

            act.wait_ge(x_in, 16)
            act.wait_ge(tab_in, 32)
            norm(x, scratch, h_hi, root)
            split4()

            def hyena(p):
                dst = (x0, z1, zv)[p // 3]
                j = 2 * (p % 3)
                b = p % 2
                group_done()
                n.next(("fill", b))
                for s in range(2):
                    m = act.activation(dst[:, j + s, :], p2(b)[:, s, :], ACT.Identity,
                                       bias=col("hy_b", 2 * p + s), scale=col("hy_w", 18 + 2 * p + s))
                to_dve(m)

            def sine():
                from_dve()
                to_pe(act.activation(fh[3][:, :], fh[2][:, :], ACT.Sin))

            split4()
            hyena(0)
            sine()
            split4()
            hyena(1)
            sine()
            split4()
            hyena(2)
            split4()
            hyena(3)
            for q, dst in enumerate((k_re, k_im)):
                for f in range(2):
                    for c in range(2):
                        psum()
                        to_pe(copy(dst[:, f, c * 384:(c + 1) * 384], banks[3 + (4 * q + 2 * f + c) % 4][:, 0:384]))
            for p in range(4, 9):
                split4()
                hyena(p)

            def gelu(p):
                dst = gv if p < 12 else gu
                j = 2 * (p % 3)
                group_done()
                n.next(("fill", p % 2))
                act.activation(dst[:, j:j + 2, :], p2(p % 2), ACT.Gelu_apprx_tanh).then_inc(bank_read[p % 2], 1)

            def y_half(tile, k, s):
                from_dve()
                to_dve(copy(y_hi[:, tile:tile + k, :], y_part[:, s:s + k, :]))

            split4()
            gelu(9)
            for c in range(2):
                for half in range(2):
                    psum()
                    to_pe(copy(zt[:, c, half * 384:(half + 1) * 384], banks[3 + 2 * c + half][:, 0:384]))
            split4()
            gelu(10)
            split4()
            group_done()
            n.next(("fill", 1))
            g11 = act.activation(gv[:, 4:6, :], p2(1), ACT.Gelu_apprx_tanh)
            g11.then_inc(bank_read[1], 1)
            split4()
            gelu(12)
            act.wait_ge(bank_read[0], n.now(("fill", 0)))
            act.activation(root[:, 0:1], gv[:, 5, 0:1], ACT.Copy).then_inc(act_for_pe, 1)
            for k in range(3):
                y_half(4 + 2 * k, 2, 2 * (k % 2))
            from_dve()
            to_pe(act.activation(gsq[:, :, :], gv[:, :, :], ACT.Square))
            split4()
            gelu(13)
            psum()
            to_dve(act.activation(root[:, :], banks[7][:, 0:T], ACT.Sqrt, bias=con_("eps5"), scale=1.0 / D_HY))
            split4()
            gelu(14)
            for k in range(3):
                psum()
                to_pe(copy(gvt[:, :, 2 * k * P:(2 * k + 2) * P],
                           banks[3 + k][:, :].rearrange("p (c t) -> p c t", c=2)))

            def pool_in(p, b):
                group_done()
                n.next(("fill", b))
                copy(pool_x[:, 2 * (p - 15):2 * (p - 15) + 2, 8:8 + T], p2(b)).then_inc(bank_read[b], 1)

            split4()
            pool_in(15, 1)
            for k in range(3):
                y_half(10 + 2 * k, 2, 2 * (k % 2))
            split4()
            pool_in(16, 0)
            y_half(0, 4, 0)

            with n.loop(4, dict({("landed", s): 32 for s in range(RING)}, unit=8, **{})) as i:
                split4(8)
            for b in (0, 1):
                n.next(("fill", b), 4)
                act.wait_ge(bank_read[b], n.now(("fill", b)))
            norm(x, scratch2, h_hi, root2)

            def land(k):
                return {("landed", s): 16 * k // RING for s in range(RING)}

            with n.loop(2, land(U_UP + U_DOWN) | {"unit": U_UP + U_DOWN, "dve": 2 * FF_HALF,
                                                  ("fill", 0): 13, ("fill", 1): 13}) as half:
                with n.loop(FF_HALF // 2, land(8) | {"unit": 8, "dve": 4, ("fill", 0): 1, ("fill", 1): 1}) as j:
                    for q, b in enumerate((1, 0)):
                        base = half * (8 * FF_HALF) + j * 16 + 8 * q
                        o = conv_o[:, q, :, :]
                        split4()
                        group_done()
                        n.next(("fill", b))
                        for s in range(2):
                            m = act.activation(o[:, s, :], p2(b)[:, s, :], ACT.Identity,
                                               bias=col("ffn", base + (4 * s + 3)),
                                               scale=col("ffn", base + (4 * s + 1)))
                        to_dve(m)
                        from_dve()
                        to_dve(act.activation(o[:, 0, :], o[:, 0, :], ACT.Silu))
                        from_dve()
                        to_dve(copy(m_hi[:, j * 2 + q, :], conv_m[:, q, :]))
                for q in range(4):
                    split4(11)
                    if q % 2 == 0:
                        n.next(("fill", 0))
                        n.next(("fill", 1))
            from_dve()
            norm(x, scratch2, None, root2, split_it=False)
            from_dve()
            norm(x, scratch2, h_hi, root2)
            split4()
            group_done()
            n.next(("fill", 1))
            copy(lx[:, 1:257], p2(1)[:, 0, :]).then_inc(bank_read[1], 1)
            from_dve()
            to_pe(act.activation(lt[0:64, :], lt[0:64, :], ACT.Tanh))
            for j in range(8):
                psum()
                act.activation(cum[:, j, :], banks[3 + j % 2][:, 0:T], ACT.Sigmoid, bias=col("w0", j))
                to_pe(act.activation(icl[:, j, :], banks[5 + j % 2][:, 0:T], ACT.Sigmoid, bias=col("a0", j)))
            act.activation(root2[:, 0:1], icl[:, 0, 0:1], ACT.Copy).then_inc(act_for_dve, 1)
            from_dve()

            def flat(t):
                return t[:, :, :].rearrange("p c t -> p (c t)")

            def keep(name, bank):
                psum()
                to_pe(copy(flat(bd[name]), banks[bank][:, :]))

            ep4 = small["ep"][:, :].rearrange("p (c t) -> p c t", c=NCH)
            def heads(k, g):
                split()
                if k % 4 == 3:
                    group_done()
                    n.next(("fill", (k // 4) % 2))
                if k == 3:
                    copy(small["pr"][:, 1:257], p2(0)[:, 0, :])
                    copy(small["pk"][:, 1:257], p2(0)[:, 1, :]).then_inc(bank_read[0], 1)
                if k == 7:
                    act.wait_ge(keys_ready, n.next("keys"))
                    copy(small["pv"][:, 1:257], p2(1)[:, 0, :])
                    to_dve(act.activation(small["k0"][:, :], p2(1)[:, 1, :], ACT.Tanh, scale=0.5))
                if k == 9:
                    from_dve()
                    to_dve(act.activation(small["sq"][:, :], small["sq"][:, :], ACT.Sqrt))
                if k == 11:
                    act.activation(qr[:, :, :], p2(0), ACT.Square).then_inc(qk_squared, 1)
                    copy(qk[:, :, :], p2(0)).then_inc(bank_read[0], 1)
                if k == 12:
                    act.wait_ge(qk_sums, n.next("qk"))
                    to_dve(act.activation(flat(qr), banks[7][:, :], ACT.Sqrt, bias=con_("eps6"), scale=1.0 / P))
                if k == 13:
                    from_dve()
                    cg_ = cum[:, bass.ds(g, 1), :].rearrange("p o t -> p (o t)")
                    act.activation(ep4[:, :, 1:65], cg_.rearrange("p (c t) -> p c t", c=NCH), ACT.Exp)
                    act.activation(small["en"][:, :], cg_, ACT.Exp, scale=-1.0)
                    for h in range(2):
                        hs = slice(64 * h, 64 * h + 64)
                        m = copy(bd["v"][hs, :, hs], small["v"][hs, :].rearrange("p (c t) -> p c t", c=NCH))
                    to_dve(m)
                if k == 15:
                    to_pe(copy(avf[:, :], p2(1)[:, 0, :]))
                    to_dve(act.activation(az[:, :], p2(1)[:, 1, :], ACT.Tanh, scale=0.5))

            def queries(k):
                split()
                if k % 4 == 3:
                    h, b = k // 4, (k // 4) % 2
                    group_done()
                    n.next(("fill", b))
                    copy(cqs[:, 2 * h:2 * h + 2, :], p2(b)).then_inc(bank_read[b], 1)

            def late(units):
                units(0)
                keep("Vt", 2)
                psum()
                to_pe(copy(flat(av_t), banks[7][:, 0:T]))
                units(1)
                keep("b1", 3)
                keep("b2", 4)
                keep("AkV", 5)
                keep("At", 6)
                keep("Bt", 2)
                keep("b3", 4)
                units(2)
                keep("Kk", 5)
                from_dve()
                act.activation(prb[:, 0:P], prb[:, 0:P], ACT.Exp, bias=stat[:, 2:3], accum_out=stat[:, 4:5])
                to_dve(act.activation(prb[:, P:3 * P], prb[:, P:3 * P], ACT.Exp, bias=stat[:, 3:4],
                                      accum_out=stat[:, 5:6]))
                units(3)
                keep("b1", 4)
                keep("Y", 5)
                keep("Kt", 6)
                keep("N", 3)
                keep("Nt", 4)
                units(4)
                keep("b3", 4)
                psum()
                to_pe(copy(prt[:, :], banks[7][:, 0:3 * P]))
                units(5)
                units(6)
                keep("b2", 5)
                keep("b1", 6)
                for k in range(7, 11):
                    units(k)
                psum()
                to_pe(copy(small["o"][:, :], banks[3][:, 0:T]))
                psum()
                to_pe(act.activation(small["gsq"][:, :], banks[4][:, 0:T], ACT.Square))
                units(11)
                psum()
                to_dve(act.activation(small["groot"][:, :], banks[6][:, 0:T], ACT.Sqrt, bias=con_("eps_gn"),
                                      scale=1.0 / 64))
                for k in range(12, 16):
                    units(k)

            ep4 = small["ep"][:, :].rearrange("p (c t) -> p c t", c=NCH)
            pair_counts = land(16) | {"unit": 16, ("fill", 0): 2, ("fill", 1): 2, "keys": 1, "qk": 1}
            for k in range(16):
                heads(k, 0)
            with n.loop(HEADS_A - 1, {"psum": 21, "dve": 3} | pair_counts) as i:
                late(lambda k: heads(k, i + 1))
            late(queries)
            for h in range(HEADS_C):
                act.wait_ge(bank_read[h % 2], n.now(("fill", h % 2)))
                to_pe(act.activation(csq[:, :, :], cqs[:, 2 * h:2 * h + 2, :], ACT.Square))
                split()
                psum()
                to_dve(act.activation(croot[:, :], banks[7][:, 0:T], ACT.Sqrt, bias=con_("eps6"),
                                      scale=1.0 / (2 * P)))
                split4(3)
                group_done()
                n.next(("fill", h % 2))
                from_dve()
                act.activation(czs[:, 2 * h:2 * h + 2, :], p2(h % 2), ACT.Silu).then_inc(bank_read[h % 2], 1)
            act.wait_ge(mem_in, 16)
            norm(memx, scratch3, mh_hi, croot)

            def key_root():
                psum()
                to_dve(act.activation(mroot[:, :], banks[7][:, 0:T], ACT.Sqrt, bias=con_("eps6"),
                                      scale=1.0 / (2 * P)))

            for j in range(4):
                split()
                if j:
                    key_root()
                    from_dve()
                split4(3)
                group_done()
                n.next(("fill", j % 2))
                to_pe(act.activation(msq[:, :, :], p2(j % 2), ACT.Square))
                copy(cpair[:, :, :], p2(j % 2)).then_inc(bank_read[j % 2], 1)
            for j in range(4):
                split()
                if j == 0:
                    key_root()
                    from_dve()
                else:
                    psum()
                    to_pe(copy(mvt[:, :, (j - 1) * 2 * P:j * 2 * P],
                               banks[6][:, :].rearrange("p (c t) -> p c t", c=2)))
                split()
                from_dve()
                for q in range(2):
                    m = act.activation(cp[:, q, :], banks[3][:, q * T:(q + 1) * T], ACT.Exp, scale=1.0 / 16,
                                       bias=cstat[:, 2 + q:3 + q], accum_out=cstat[:, 4 + q:5 + q])
                to_dve(m)
                split4(2)
                group_done()
                n.next(("fill", j % 2))
                copy(cpair[:, :, :], p2(j % 2)).then_inc(bank_read[j % 2], 1)
                psum()
                to_pe(copy(flat(cpt[j]), banks[4][:, :]))
            psum()
            to_pe(copy(mvt[:, :, 6 * P:8 * P], banks[6][:, :].rearrange("p (c t) -> p c t", c=2)))
            act.wait_ge(head_written, HEADS_C)
            for c in range(6):
                to_dve(copy(ya_hi[:, 4 * c:4 * c + 4, :], yall[:, 4 * c:4 * c + 4, :]))
            with n.loop(4, land(36) | {"unit": 36, "dve": 2, ("fill", 0): 6, ("fill", 1): 6}) as i:
                for j in range(2):
                    for m3 in range(3):
                        split4()
                        group_done()
                        act.wait_ge(bank_read[1], n.now(("fill", 1)))
                        n.next(("fill", 0))
                        act.activation(gate[:, :, :], p2(0), ACT.Tanh, scale=0.5).then_inc(bank_read[0], 1)
                        split4(2)
                        n.next(("fill", 1))
                    from_dve()
                    to_dve(copy(mg_hi[:, bass.ds(i * 4 + 2 * j, 2), :], macc[:, :, :], 0.5))
            with n.loop(7, land(4) | {"unit": 4}):
                split4()

        @block.vector
        def _(dve):
            n = Counts(dve)
            slots = count()

            def split():
                slot = next(slots) % RING
                dve.wait_ge(hi_done, n.next("unit"))
                dve.tensor_tensor(w_lo[slot][:, :, :], raw[slot][:, :, :], w_hi[slot][:, :, :].bitcast(F32),
                                  ALU.subtract).then_inc(split_done, 1)

            def split4(k=4):
                for _ in range(k):
                    split()

            def group_done():
                dve.wait_ge(unit_used, n.now("unit") - RING)

            def psum(k=1):
                dve.wait_ge(psum_for_dve, n.next("psum", k))

            def from_act(k=1):
                dve.wait_ge(act_for_dve, n.next("act", k))

            def step(ins):
                ins.then_inc(dve_step, 1)
                n.next("step")

            def settle():
                dve.wait_ge(dve_step, n.now("step"))

            def to_pe(ins):
                ins.then_inc(dve_for_pe, 1)
                n.next("to_pe")

            def settle_pe():
                dve.wait_ge(dve_for_pe, n.now("to_pe"))

            def to_act(ins):
                ins.then_inc(dve_for_act, 1)
                n.next("to_act")

            def settle_act():
                dve.wait_ge(dve_for_act, n.now("to_act"))

            def read(ins, b):
                ins.then_inc(bank_read[b], 1)

            def own_bank(b):
                dve.wait_ge(bank_read[b], n.now(("fill", b)))

            def tt(out, x_, y_, op):
                return dve.tensor_tensor(out, x_, y_, op)

            def stt(out, x_, s, y_, op0, op1):
                return dve.scalar_tensor_tensor(out, x_, s, y_, op0, op1)

            def ts(out, x_, s0, s1=None, op0=ALU.mult, op1=None):
                return dve.tensor_scalar(out, x_, s0, s1, op0) if op1 is None else \
                    dve.tensor_scalar(out, x_, s0, s1, op0, op1)

            def low(lo, f, hi):
                return tt(lo, f, hi.bitcast(F32), ALU.subtract)

            def norm(src, g, f, hi, lo, rt):
                from_act()
                step(dve.reciprocal(rt[:, :], rt[:, :]))
                settle()
                for t in range(KT):
                    m = stt(f[:, t, :], src[:, t, :], col(g, t), rt[:, :], ALU.mult, ALU.mult)
                    if hi is not None and t % 4 == 3:
                        to_act(m)
                if hi is None:
                    to_act(m)
                    settle_act()
                    return
                for c in range(4):
                    cs = slice(4 * c, 4 * c + 4)
                    from_act()
                    m = low(lo[:, cs, :], f[:, cs, :], hi[:, cs, :])
                to_pe(m)

            dve.wait_ge(x_in, 16)
            dve.wait_ge(tab_in, 32)
            norm(x, "norm_mix", scratch, h_hi, h_lo, root)
            split4()

            def taps(dst, b, w0, w2):
                o = p2(b)
                for s in range(2):
                    step(stt(dst[s][:, 1:T], o[:, s, 0:T - 1], w0[s], dst[s][:, 1:T], ALU.mult, ALU.add))
                settle()
                return [lambda s=s: stt(dst[s][:, 0:T - 1], o[:, s, 1:T], w2[s], dst[s][:, 0:T - 1], ALU.mult,
                                        ALU.add) for s in range(2)]

            def hyena(p):
                dst = (x0, z1, zv)[p // 3]
                j = 2 * (p % 3)
                b = p % 2
                from_act()
                n.next(("fill", b))
                last = taps([dst[:, j + s, :] for s in range(2)], b, [col("hy_w", 2 * p + s) for s in range(2)],
                            [col("hy_w", 36 + 2 * p + s) for s in range(2)])
                step(last[0]())
                read(last[1](), b)

            def sine(b_, fr):
                u, k, r = fh[0][:, :], fh[1][:, :], fh[2][:, :]
                psum()
                step(ts(u, banks[3][0:64, 0:T], col(b_)[0:64, :], col(fr)[0:64, :], ALU.add, ALU.mult))
                settle()
                step(ts(k, u, float(1.0 / TWO_PI), ROUND, ALU.mult, ALU.add))
                settle()
                step(ts(k, k, ROUND, None, ALU.subtract))
                settle()
                step(stt(r, k, -PI_HI, u, ALU.mult, ALU.add))
                settle()
                step(stt(r, k, -PI_LO, r, ALU.mult, ALU.add))
                settle()
                to_act(ts(r, r, PI_CUT, -PI_CUT, ALU.min, ALU.max))

            split4()
            hyena(0)
            dve.wait_ge(filt_in, 6 * 16)
            sine("f_b1", "f_fr1")
            split4()
            hyena(1)
            sine("f_b2", "f_fr2")
            split4()
            hyena(2)
            for c in range(2):
                for q in range(4):
                    psum()
                    dst = f_fwd if q < 2 else f_bwd
                    qs = slice((q % 2) * 384, (q % 2 + 1) * 384)
                    to_pe(tt(dst[:, c, qs], banks[3 + q][:, 0:384], decay[:, c, qs], ALU.mult))
            settle_pe()
            dve.memset(f_bwd[0:1, 0, :], 0.0).then_inc(free_early, 1)
            dve.wait_ge(free_early, 1)
            step(tt(f_sum[:, :, :], f_fwd[:, :, :], f_bwd[:, :, :], ALU.add))
            settle()
            to_pe(tt(f_bwd[:, :, :], f_fwd[:, :, :], f_bwd[:, :, :], ALU.subtract))
            for p in range(3, 9):
                split4()
                hyena(p)
            own_bank(0)
            own_bank(1)
            settle()
            to_pe(tt(z1[:, :, :], z1[:, :, :], zv[:, :, :], ALU.mult))
            for p in (9, 10, 11):
                split4()
                n.next(("fill", p % 2))
            for i, (f, c) in enumerate(((0, 0), (0, 1), (1, 0), (1, 1))):
                psum()
                zr, zi = (banks[3 + 2 * (i % 2) + k][:, 0:384] for k in range(2))
                cs = slice(c * 384, (c + 1) * 384)
                kr, ki = k_re[:, f, cs], k_im[:, f, cs]
                if i == 0:
                    settle_pe()
                step(tt(prod[0][:, :], zr, kr, ALU.mult))
                step(tt(prod[1][:, :], zi, ki, ALU.mult))
                step(tt(prod[2][:, :], zr, ki, ALU.mult))
                to_pe(tt(prod[3][:, :], zi, kr, ALU.mult))
                settle()
                settle_pe()
                step(tt(kr, prod[0][:, :], prod[1][:, :], ALU.subtract))
                if i < 3:
                    step(tt(ki, prod[2][:, :], prod[3][:, :], ALU.add))
                else:
                    to_pe(tt(ki, prod[2][:, :], prod[3][:, :], ALU.add))
                settle()
            settle_pe()
            split4()
            n.next(("fill", 0))

            def y_low(tile, k, s, last=None):
                from_act()
                m = low(y_lo[:, tile:tile + k, :], y_part[:, s:s + k, :], y_hi[:, tile:tile + k, :])
                (to_pe if last else step)(m)

            for k in range(3):
                psum()
                for s in range(2):
                    step(stt(mix[:, s, :], z1[:, 2 * k + s, :], col("hy_skip", 2 * k + s),
                             banks[3 + k][:, s * T:(s + 1) * T], ALU.mult, ALU.add))
                settle()
                s = 2 * (k % 2)
                to_act(tt(y_part[:, s:s + 2, :], mix[:, :, :], x0[:, 2 * k:2 * k + 2, :], ALU.mult))
                settle_act()
                y_low(4 + 2 * k, 2, s)
                settle()
            dve.memset(pool_x[:, :, 0:8], 0.0)
            dve.memset(pool_x[:, :, 8 + T:PW], 0.0).then_inc(free_inv, 1)
            psum()
            for j in range(HY):
                m = stt(gv[:, j, :], banks[6][:, 0:T], -1.0 / D_HY, gv[:, j, :], ALU.mult, ALU.add)
            to_act(m)
            settle_act()
            split4()
            n.next(("fill", 1))
            from_act()
            step(dve.reciprocal(root[:, :], root[:, :]))
            settle()
            step(tt(gv[:, :, :], gv[:, :, :], bcast(root[:, :], HY), ALU.mult))
            settle()
            for j in range(HY):
                m = ts(gv[:, j, :], gv[:, j, :], col("gm_g", j), col("gm_b", j), ALU.mult, ALU.add)
            to_pe(m)
            split4()
            n.next(("fill", 0))
            split4()
            n.next(("fill", 1))
            for k in range(3):
                psum()
                s = 2 * (k % 2)
                to_act(tt(y_part[:, s:s + 2, :], gu[:, 2 * k:2 * k + 2, :],
                          banks[3 + k][:, :].rearrange("p (s t) -> p s t", s=2), ALU.mult))
                settle_act()
                y_low(10 + 2 * k, 2, s)
                settle()
            split4()
            n.next(("fill", 0))
            own_bank(1)
            own_bank(0)
            dve.wait_ge(free_inv, 1)
            step(tt(pool_a[:, :, 1:PW], pool_x[:, :, 0:PW - 1], pool_x[:, :, 1:PW], ALU.add))
            settle()
            step(tt(pool_b[:, 1:4, 2:PW - 1], pool_a[:, 1:4, 1:PW - 2], pool_a[:, 1:4, 3:PW], ALU.add))
            settle()
            step(tt(pool_a[:, 2:4, 4:PW - 3], pool_b[:, 2:4, 2:PW - 5], pool_b[:, 2:4, 6:PW - 1], ALU.add))
            settle()
            step(tt(pool_b[:, 3:4, 8:PW - 7], pool_a[:, 3:4, 4:PW - 11], pool_a[:, 3:4, 12:PW - 3], ALU.add))
            settle()
            dve.wait_ge(inv_in, 16)
            for g in range(4):
                src = (pool_a, pool_b, pool_a, pool_b)[g]
                step(tt(pool_d[:, g, :], src[:, g, 8:8 + T], inv[:, g, :], ALU.mult))
            settle()
            to_pe(tt(pool_d[:, :, :], pool_d[:, :, :], pool_x[:, :, 8:8 + T], ALU.subtract))
            psum()
            for g in range(4):
                m = ts(y_part[:, g, :], banks[6 + g // 2][:, (g % 2) * T:(g % 2 + 1) * T], col("pool_b", g),
                       col("pool_scale", g), ALU.add, ALU.mult)
            to_act(m)
            settle_act()
            y_low(0, 4, 0, last=True)

            def residual(tile, b, out=None):
                group_done()
                n.next(("fill", b))
                t = x[:, bass.ds(tile, 2), :]
                dst = t if out is None else out[:, bass.ds(tile, 2), :]
                read(tt(dst, t, p2(b), ALU.add), b)

            with n.loop(4, {"unit": 8, ("fill", 0): 1, ("fill", 1): 1}) as i:
                for q, b in enumerate((1, 0)):
                    split4()
                    residual(i * 4 + 2 * q, b)
            own_bank(0)
            own_bank(1)
            norm(x, "norm_ffn", scratch2, h_hi, h_lo, root2)
            for b in (2, 3):
                n.next(("fill", b))
                dve.memset(conv_m[:, 0, 0:1], 0.0).then_inc(bank_read[b], 1)
                own_bank(b)
            with n.loop(2, {"unit": U_UP + U_DOWN, "act": 3 * FF_HALF, "to_act": 2 * FF_HALF, "step": 3 * FF_HALF // 1 - FF_HALF,
                            ("fill", 0): 13, ("fill", 1): 13, ("fill", 2): 2, ("fill", 3): 2}) as half:
                with n.loop(FF_HALF // 2, {"unit": 8, "act": 6, "to_act": 4, "step": 4, ("fill", 0): 1,
                                           ("fill", 1): 1}) as j:
                    for q, b in enumerate((1, 0)):
                        base = half * (8 * FF_HALF) + j * 16 + 8 * q
                        o = conv_o[:, q, :, :]
                        split4()
                        from_act()
                        n.next(("fill", b))
                        last = taps([o[:, s, :] for s in range(2)], b, [col("ffn", base + 4 * s) for s in range(2)],
                                    [col("ffn", base + (4 * s + 2)) for s in range(2)])
                        to_act(last[0]())
                        read(last[1](), b)
                        from_act()
                        own_bank(b)
                        to_act(tt(conv_m[:, q, :], o[:, 0, :], o[:, 1, :], ALU.mult))
                        settle_act()
                        from_act()
                        low(m_lo[:, j * 2 + q, :], conv_m[:, q, :], m_hi[:, j * 2 + q, :])\
                            .then_inc(hidden_ready, 1)
                for q in range(4):
                    split4(11)
                    group_done()
                    for s, b in enumerate((0, 1) if q % 2 == 0 else (2, 3)):
                        n.next(("fill", b))
                        t = x[:, 4 * q + 2 * s:4 * q + 2 * s + 2, :]
                        read(tt(t, t, p2(b), ALU.add), b)
                for b in range(4):
                    own_bank(b)
            to_act(dve.memset(lx[:, 0:1], 0.0))
            norm(x, "norm_final", x, None, None, root2)
            norm(x, "norm_g", scratch2, h_hi, h_lo, root2)
            dve.memset(lx[:, 0:1], 0.0).then_inc(free_lora, 1)
            dve.wait_ge(free_lora, 1)
            split4()
            n.next(("fill", 1))
            own_bank(1)
            step(tt(lt[:, :], lx[:, 0:T], lx[:, 1:T + 1], ALU.subtract))
            settle()
            to_act(stt(lt[:, :], lt[:, :], col("mu_wa"), lx[:, 1:T + 1], ALU.mult, ALU.add))
            from_act()
            step(ts(cum[:, :, :], cum[:, :, :], -float(np.exp(-0.5))))
            settle()
            a4, b4_ = (t[:, :, :].rearrange("p g (c t) -> p (g c) t", t=CHUNK) for t in (cum, ping))
            for k in range(6):
                s = 1 << k
                step(tt(b4_[:, :, s:CHUNK], a4[:, :, s:CHUNK], a4[:, :, 0:CHUNK - s], ALU.add))
                step(dve.tensor_copy(b4_[:, :, 0:s], a4[:, :, 0:s]))
                settle()
                a4, b4_ = b4_, a4
            for t in ("a", "b", "k", "v"):
                step(dve.memset(bd[t][:, :, :], 0.0))
            ep4 = small["ep"][:, :].rearrange("p (c t) -> p c t", c=NCH)
            step(dve.memset(ep4[:, :, 0:1], 1.0))
            for t in ("pr", "pk", "pv"):
                step(dve.memset(small[t][:, 0:1], 0.0))
            dve.memset(stat[:, 0:1], 0.0).then_inc(bias_used, 1)
            dve.wait_ge(bias_used, 1)
            settle()
            to_act(dve.memset(stat[:, 1:2], 0.0))
            settle_act()

            def c4(t):
                return t.rearrange("p (c t) -> p c t", c=NCH)

            def flat(t):
                return t[:, :, :].rearrange("p c t -> p (c t)")

            sm = small
            shift = lambda t: (sm[t][:, 0:T], sm[t][:, 1:T + 1])
            ident4 = bcast(con_("ident"), NCH)
            def heads(k, g):
                rw = lambda c: col("rwkv", g * RW_COLS + c)
                icl_g = icl[:, bass.ds(g, 1), :].rearrange("p o t -> p (o t)")
                split()
                if k % 4 == 3:
                    n.next(("fill", (k // 4) % 2))
                if k == 3:
                    own_bank(0)
                    prev, now = shift("pr")
                    step(tt(sm["t0"][:, :], prev, now, ALU.subtract))
                    prevk, nowk = shift("pk")
                    step(tt(sm["k2"][:, :], prevk, nowk, ALU.subtract))
                    settle()
                    step(stt(sm["r"][:, :], sm["t0"][:, :], rw(MU_R), now, ALU.mult, ALU.add))
                    step(stt(sm["k0"][:, :], sm["k2"][:, :], rw(MU_K), nowk, ALU.mult, ALU.add))
                    settle()
                    step(ts(sm["kk"][:, :], sm["k0"][:, :], rw(K_K)))
                    step(ts(sm["t0"][:, :], icl_g, 1.0, rw(K_A), ALU.subtract, ALU.mult))
                    settle()
                    step(tt(sm["sq"][:, :], sm["kk"][:, :], sm["kk"][:, :], ALU.mult))
                    step(stt(sm["k2"][:, :], sm["t0"][:, :], 1.0, sm["k0"][:, :], ALU.add, ALU.mult))
                    settle()
                    stt(sm["rk"][:, :], sm["r"][:, :], rw(R_K), sm["k2"][:, :], ALU.mult, ALU.mult)\
                        .then_inc(keys_ready, 1)
                    n.next("keys")
                if k == 7:
                    from_act()
                    prev, now = shift("pv")
                    step(tt(sm["t0"][:, :], prev, now, ALU.subtract))
                    read(stt(sm["k0"][:, :], sm["k0"][:, :], 1.0, p2(1)[:, 1, :], ALU.add, ALU.mult), 1)
                    settle()
                    step(stt(sm["v"][:, :], sm["t0"][:, :], rw(MU_V), now, ALU.mult, ALU.add))
                if k == 9:
                    dve.wait_ge(head_sums, n.next("sums"))
                    to_act(ts(sm["sq"][:, :], banks[7][:, 0:T], 1e-24, None, ALU.max))
                    settle()
                    tt(sm["rk"][:, :], banks[7][:, T:2 * T], sm["v"][:, :], ALU.mult).then_inc(sums_read, 1)
                if k == 10:
                    from_act()
                    step(dve.reciprocal(sm["sq"][:, :], sm["sq"][:, :]))
                    settle()
                    step(tt(sm["kk"][:, :], sm["kk"][:, :], sm["sq"][:, :], ALU.mult))
                    settle()
                    step(tt(sm["t0"][:, :], sm["kk"][:, :], icl_g, ALU.mult))
                if k == 12:
                    from_act()
                    step(dve.reciprocal(flat(qr), flat(qr)))
                    settle()
                    step(stt(qk[:, 0, :], qk[:, 0, :], col("aq_g"), qr[:, 0, :], ALU.mult, ALU.mult))
                    step(stt(qk[:, 1, :], qk[:, 1, :], col("ak_g"), qr[:, 1, :], ALU.mult, ALU.mult))
                if k == 13:
                    dve.wait_ge(sums_read, n.now("sums"))
                    settle()
                    step(dve.tensor_copy(sm["bon"][:, :], sm["rk"][:, :]))
                    to_act(dve.tensor_copy(sm["bz"][:, :], sm["k0"][:, :]))
                    from_act()
                    for h in range(2):
                        hp = slice(64 * h, 64 * h + 64)
                        step(stt(bd["a"][hp, :, hp], c4(sm["kk"][hp, :]), -1.0, ep4[hp, :, 0:CHUNK], ALU.mult,
                                 ALU.mult))
                        step(tt(bd["b"][hp, :, hp], c4(sm["t0"][hp, :]), c4(sm["en"][hp, :]), ALU.mult))
                        step(tt(bd["k"][hp, :, hp], c4(sm["k2"][hp, :]), c4(sm["en"][hp, :]), ALU.mult))
                    to_pe(tt(c4(sm["rt"][:, :]), c4(sm["r"][:, :]), ep4[:, :, 1:CHUNK + 1], ALU.mult))
                if k == 15:
                    from_act()
                    read(stt(az[:, :], az[:, :], 1.0, p2(1)[:, 1, :], ALU.add, ALU.mult), 1)

            def queries(k):
                split()
                if k % 4 == 3:
                    n.next(("fill", (k // 4) % 2))

            def y_tile(i):
                return yall[:, bass.ds(i, 1), :].rearrange("p o t -> p (o t)")

            def late(units, g):
                units(0)
                psum()
                step(tt(bd["Nt"][:, :, :], b4(3), bcast(con_("upper_in"), NCH), ALU.mult))
                psum()
                step(tt(bd["N"][:, :, :], b4(4), bcast(con_("lower_in"), NCH), ALU.mult))
                to_pe(tt(bd["No"][:, :, :], b4(4), bcast(con_("lower_out"), NCH), ALU.mult))
                psum()
                step(tt(bd["Kt"][:, :, :], b4(5), bcast(con_("upper"), NCH), ALU.mult))
                settle()
                step(tt(bd["Q"][:, :, :], bd["Nt"][:, :, :], ident4, ALU.add))
                psum()
                to_pe(tt(BK[:, :, :, :].rearrange("p q c t -> p (q c) t"),
                         banks[6][:, :].rearrange("p (q t) -> p q t", t=CHUNK), bcast(con_("upper_eq"), 8), ALU.mult))
                settle()
                units(1)
                psum()
                to_pe(tt(bd["Q"][:, :, :], bd["Q"][:, :, :], b4(3), ALU.add))
                psum()
                dve.wait_ge(bias_in, 16 * n.next("bias"))
                stt(prb[:, :], banks[7][:, 0:3 * P], float(P) ** -0.5, bias_t[:, :], ALU.mult, ALU.add)\
                    .then_inc(bias_used, 1)
                dve.wait_ge(bias_used, n.now("bias") + 1)
                step(dve.memset(prb[0:64, 64:P], NEG))
                step(dve.memset(prb[0:64, P + 192:3 * P], NEG))
                settle()
                step(dve.tensor_reduce(stat[:, 0:1], prb[:, 0:P], AX_X, ALU.max))
                step(dve.tensor_reduce(stat[:, 1:2], prb[:, P:3 * P], AX_X, ALU.max))
                settle()
                to_act(ts(stat[:, 2:4], stat[:, 0:2], -1.0))
                units(2)
                settle_pe()
                psum()
                to_pe(tt(bd["Q"][:, :, :], bd["Q"][:, :, :], b4(3), ALU.add))
                units(3)
                psum()
                step(dve.tensor_copy(bd["b2"][:, :, :], b4(3)))
                to_pe(tt(bd["F"][:, :, :], b4(3), ident4, ALU.add))
                from_act()
                step(dve.reciprocal(stat[:, 6:8], stat[:, 4:6]))
                settle()
                step(ts(prb[:, 0:P], prb[:, 0:P], stat[:, 6:7]))
                to_pe(ts(prb[:, P:3 * P], prb[:, P:3 * P], stat[:, 7:8]))
                settle_pe()
                units(4)
                psum()
                to_pe(tt(bd["F"][:, :, :], bd["F"][:, :, :], b4(3), ALU.add))
                units(5)
                settle_pe()
                psum()
                to_pe(tt(bd["F"][:, :, :], bd["F"][:, :, :], b4(3), ALU.add))
                units(6)

                def decay_of(c):
                    return ep4[:, c, CHUNK:CHUNK + 1]

                def solved(c):
                    if c < NCH - 1:
                        step(ts(S_dec[:, :], S[:, c % 2, :], decay_of(c)))
                    psum()
                    to_pe(tt(SA[:, c % 2, :], banks[2][:, 0:P], bd["b1"][:, c, :], ALU.add))
                    settle()

                def state(c):
                    psum()
                    to_pe(stt(S[:, (c + 1) % 2, :], banks[4][:, 0:P], decay_of(c), S_dec[:, :], ALU.mult, ALU.add))
                    settle_pe()

                psum()
                to_pe(ts(S[:, 1, :], banks[4][:, 0:P], decay_of(0)))
                settle_pe()
                psum()
                dve.wait_ge(bank_read[1], n.now(("fill", 1)))
                step(stt(y_tile(g), banks[5][:, 0:T], 0.5, az[:, :], ALU.mult, ALU.mult))
                units(7)
                solved(1)
                state(1)
                units(8)
                solved(2)
                state(2)
                units(9)
                solved(3)
                units(10)
                units(11)
                from_act()
                step(dve.reciprocal(sm["groot"][:, :], sm["groot"][:, :]))
                settle()
                step(tt(sm["gk"][:, :], banks[4][:, 0:T], sm["groot"][:, :], ALU.mult))
                settle()
                step(ts(sm["gk"][:, :], sm["gk"][:, :], col("rwkv", g * RW_COLS + LN_W),
                        col("rwkv", g * RW_COLS + LN_B), ALU.mult, ALU.add))
                settle()
                step(tt(sm["gk"][:, :], sm["gk"][:, :], sm["bon"][:, :], ALU.add))
                settle()
                step(stt(y_tile(g + 8), sm["gk"][:, :], 0.5, sm["bz"][:, :], ALU.mult, ALU.mult))
                for k in range(12, 16):
                    units(k)

            for k in range(16):
                heads(k, 0)
            with n.loop(HEADS_A - 1, {"unit": 16, "psum": 17, "act": 7, "step": 42, "to_pe": 15, "to_act": 3,
                                      ("fill", 0): 2, ("fill", 1): 2, "bias": 1, "keys": 1, "sums": 1}) as i:
                late(lambda k: heads(k, i + 1), i)
            late(queries, HEADS_A - 1)
            dve.memset(stat[:, 0:1], 0.0).then_inc(free_mem, 1)
            for h in range(HEADS_C):
                split()
                from_act()
                step(dve.reciprocal(croot[:, :], croot[:, :]))
                settle()
                for s in range(2):
                    q = cqs[:, 2 * h + s, :]
                    m = stt(q, q, col("cq_g", s), croot[:, :], ALU.mult, ALU.mult)
                    (step, to_act)[s](m)
                split4(3)
                n.next(("fill", h % 2))
            dve.wait_ge(mem_in, 16)
            norm(memx, "mem_g", scratch3, mh_hi, mh_lo, croot)
            settle_pe()

            def keys(j):
                from_act()
                step(dve.reciprocal(mroot[:, :], mroot[:, :]))
                settle()
                for s in range(2):
                    m = stt(mk[:, 2 * j + s, :], cpair[:, s, :], col("ck_g", s), mroot[:, :], ALU.mult, ALU.mult)
                    (step, to_act)[s](m)

            for j in range(4):
                split()
                if j:
                    keys(j - 1)
                split4(3)
                n.next(("fill", j % 2))
                own_bank(j % 2)
            for j in range(4):
                split()
                if j == 0:
                    keys(3)
                    settle_act()
                    to_pe(dve.memset(stat[:, 0:1], 0.0))
                split()
                psum()
                step(dve.tensor_reduce(cstat[:, 0:2], banks[3][:, :].rearrange("p (q t) -> p q t", q=2), AX_X,
                                       ALU.max))
                settle()
                to_act(ts(cstat[:, 2:4], cstat[:, 0:2], -1.0 / 16))
                from_act()
                step(dve.reciprocal(cstat[:, 6:8], cstat[:, 4:6]))
                settle()
                step(ts(cp[:, 0, :], cp[:, 0, :], cstat[:, 6:7]))
                to_pe(ts(cp[:, 1, :], cp[:, 1, :], cstat[:, 7:8]))
                split4(2)
                n.next(("fill", j % 2))
            for h in range(HEADS_C):
                psum()
                own_bank(h % 2)
                stt(yall[:, 16 + 2 * h:18 + 2 * h, :],
                    banks[(3, 4, 5, 7)[h]][:, :].rearrange("p (s t) -> p s t", s=2), 1.0,
                    czs[:, 2 * h:2 * h + 2, :], ALU.mult, ALU.mult).then_inc(head_written, 1)
            dve.wait_ge(head_written, HEADS_C)
            for c in range(6):
                from_act()
                cs = slice(4 * c, 4 * c + 4)
                m = low(ya_lo[:, cs, :], yall[:, cs, :], ya_hi[:, cs, :])
            to_pe(m)
            settle_pe()
            with n.loop(4, {"unit": 36, "act": 2, "to_act": 2, "step": 2, ("fill", 0): 6, ("fill", 1): 6,
                            "merged": 2}) as i:
                for j in range(2):
                    for m3 in range(3):
                        split4()
                        n.next(("fill", 0))
                        split4(2)
                        own_bank(0)
                        group_done()
                        n.next(("fill", 1))
                        dst = mtmp if m3 else macc
                        read(stt(dst[:, :, :], gate[:, :, :], 1.0, p2(1), ALU.add, ALU.mult), 1)
                        own_bank(1)
                        if m3:
                            (to_act if m3 == 2 else step)(tt(macc[:, :, :], macc[:, :, :], mtmp[:, :, :], ALU.add))
                            settle()
                    settle_act()
                    from_act()
                    hi = mg_hi[:, bass.ds(i * 4 + 2 * j, 2), :].bitcast(F32)
                    stt(mg_lo[:, bass.ds(i * 4 + 2 * j, 2), :], macc[:, :, :], 0.5, hi, ALU.mult, ALU.subtract)\
                        .then_inc(merged_ready, 1)
                    dve.wait_ge(merged_ready, n.next("merged"))
            with n.loop(3, {"unit": 8, ("fill", 0): 1, ("fill", 1): 1}) as i:
                for b in (0, 1):
                    split4()
                    residual(i * 4 + 2 * b, b, obuf)
            split4()
            residual(12, 0, obuf)
            dve.wait_ge(unit_used, UNITS)
            read(tt(obuf[:, 14:16, :], x[:, 14:16, :], p2(1), ALU.add), 1)


SHAPES = {"units": (UNITS, P, UK * UN), "xT": (P, KT, T), "memT": (P, KT, T), "par": (P, NPAR),
          "con": (P, NCONST), "feat": (33, T), "fw1": (33, 64), "fw2": (64, 64), "fw3": (64, 2 * D_HY),
          "dft": (P, 4, 2, T), "decay": (P, 2, D_HY), "ws": (P, HY, P), "pw": (P, 4, P), "bs": (1, HY * P),
          "inv": (P, 4, T), "lora": (P, 1024), "bias": (HEADS_A, P, 384)}


def lay_out(v):
    def tiles(vec):
        return np.ascontiguousarray(vec.reshape(-1, P).T)

    def units(w, cols):
        w = w[:, cols].reshape(-1, UK, P, len(cols) // UN, UN)
        return w.transpose(3, 0, 2, 1, 4).reshape(-1, P, UK * UN)

    def cols_of(tile_list):
        return np.concatenate([np.arange(t * P, (t + 1) * P) for t in tile_list])

    def down(w, half):
        w = w[half * FF_HALF * P:(half + 1) * FF_HALF * P].reshape(11, 2, P, 4, 512)
        return w.transpose(3, 0, 2, 1, 4).reshape(-1, P, UK * UN)

    w_in = v["w_in"][0]
    order = list(range(4, 22)) + list(range(28, 34)) + list(range(22, 28)) + list(range(4))
    parts = [units(w_in, cols_of(order)), units(v["w_out"][0], np.arange(D))]
    up = v["ffn_w_up"][0]
    for half in range(2):
        ts_ = [t for j in range(half * FF_HALF, (half + 1) * FF_HALF) for t in (j, FF_TILES + j)]
        parts += [units(up, cols_of(ts_)), down(v["ffn_w_down"][0], half)]
    w2 = v["w_in_2"][0]
    AQ, AK, AV, AZ, BR, BK_, BV, BZ = (8 * i for i in range(8))
    lora = np.zeros((D, UN), np.float32)
    lora[:, 0:P] = w2[:, 64 * P:65 * P]
    parts.append(units(lora, np.arange(UN)))
    loop = [t for g in range(8) for t in (BR + g, BK_ + g, BV + g, BZ + g, AQ + g, AK + g, AV + g, AZ + g)]
    parts.append(units(w2, cols_of(loop)))
    CQ, GA = 65, 81
    parts.append(units(w2, cols_of(range(CQ, CQ + 16))))
    parts.append(units(v["w_mem_kv_2"][0], np.arange(D)))
    ups = [v[n][0] for n in ("w_up_a_2", "w_up_b_2", "w_up_c_2")]
    for j in range(8):
        for m in range(3):
            t = GA + 16 * m + 2 * j
            parts.append(units(w2, cols_of([t, t + 1])))
            parts.append(units(ups[m], cols_of([2 * j, 2 * j + 1])))
    parts.append(units(v["w_o_2"][0], np.arange(D)))
    stream = np.concatenate(parts)

    par = np.zeros((P, NPAR), np.float32)

    def put(name, cols, at=0):
        par[:cols.shape[0], COL[name] + at:COL[name] + at + cols.shape[1]] = cols

    put("norm_mix", tiles(v["norm_mix"][0]))
    put("pool_b", tiles(v["pool_b"][0]))
    put("pool_scale", tiles(v["pool_scale"][0]))
    for k in range(3):
        put("hy_w", tiles(v["hy_short_w"][0][k]), 18 * k)
    put("hy_b", tiles(v["hy_short_b"][0]))
    put("hy_skip", tiles(v["hy_skip"][0]))
    put("gm_g", tiles(v["gm_ln_g"][0]))
    put("gm_b", tiles(v["gm_ln_b"][0]))
    put("norm_ffn", tiles(v["norm_ffn"][0]))
    ffn = np.stack([tiles(t) for t in (*v["ffn_conv_w"][0], v["ffn_conv_b"][0])], axis=-1)
    ffn = ffn.reshape(P, 2, FF_TILES, 4).transpose(0, 2, 1, 3).reshape(P, -1)
    put("ffn", ffn)
    put("norm_final", tiles(v["norm_final"]))
    put("norm_g", tiles(v["norm_g_2"][0]))
    put("mem_g", tiles(v["mem_norm_g_2"][0]))
    mu = v["b_mu_rkv_2"][0]
    rows = [mu[0], mu[1], mu[2], v["b_k_k_2"][0], v["b_k_a_2"][0], v["b_r_k_2"][0].reshape(-1), v["b_ln_w_2"][0],
            v["b_ln_b_2"][0]]
    for k, r in enumerate(rows):
        par[:, COL["rwkv"] + k:COL["rwkv"] + 80:RW_COLS] = tiles(r)
    put("mu_wa", np.concatenate([v["b_mu_w_2"][0], v["b_mu_a_2"][0]])[:, None])
    put("w0", tiles(v["b_w0_2"][0]))
    put("a0", tiles(v["b_a0_2"][0]))
    for name, key in (("aq_g", "a_q_g_2"), ("ak_g", "a_k_g_2"), ("cq_g", "c_q_g_2"), ("ck_g", "c_k_g_2")):
        put(name, tiles(v[key][0]))
    for name, key in (("f_b1", "hy_filt_b1"), ("f_fr1", "hy_filt_freq1"), ("f_b2", "hy_filt_b2"),
                      ("f_fr2", "hy_filt_freq2")):
        put(name, v[key][0][:, None])

    dft, feat, decay, inv = hyena_tables()
    q, k = np.arange(T)[:, None], np.arange(T)[None, :]
    rel = v["a_rel_bias_2"][0][:, np.clip(q - k, -P, P) + P]
    bias = np.concatenate([rel[:, 0:P, 0:P], rel[:, P:T, :]], axis=2)
    out = {
        "units": stream,
        "xT": v["x"][0].T.reshape(KT, P, T).transpose(1, 0, 2),
        "memT": v["mem_2"][0].T.reshape(KT, P, T).transpose(1, 0, 2),
        "par": par, "con": const_tables(), "feat": feat, "fw1": v["hy_filt_w1"][0], "fw2": v["hy_filt_w2"][0],
        "fw3": v["hy_filt_w3"][0], "dft": dft, "decay": decay, "inv": inv,
        "ws": v["gm_w_s"][0].transpose(2, 0, 1), "pw": v["pool_w"][0].transpose(1, 0, 2),
        "bs": v["gm_b_s"][0].reshape(1, -1),
        "lora": np.concatenate([v["b_w2_2"][0], v["b_a2_2"][0]]),
        "bias": bias,
    }
    return {name: np.ascontiguousarray(t) for name, t in out.items()}


def kernel(**inputs):
    import concourse.bacc as bacc
    from concourse.bass_utils import run_bass_kernel_spmd

    arrays = lay_out({k: np.asarray(v) for k, v in inputs.items()})
    nc = bacc.Bacc("TRN2", target_bir_lowering=False, num_devices=1)
    aps = {}
    for name, shape in SHAPES.items():
        assert arrays[name].shape == shape, (name, arrays[name].shape, shape)
        aps[name] = nc.dram_tensor(f"in_{name}", shape, F32, kind="ExternalInput").ap()
    aps["out"] = nc.dram_tensor("out_y", (P, KT, T), F32, kind="ExternalOutput").ap()
    build(nc, aps)
    r = run_bass_kernel_spmd(nc, [{f"in_{name}": t for name, t in arrays.items()}], core_ids=[0])
    y = r.results[0]["out_y"]
    return np.ascontiguousarray(y.transpose(1, 0, 2).reshape(D, T).T)[None]
```

```python
from contextlib import ExitStack, contextmanager
from itertools import count

import numpy as np

import concourse.bass as bass
from concourse import mybir

ALU = mybir.AluOpType
ACT = mybir.ActivationFunctionType
F32 = mybir.dt.float32
F32R = mybir.dt.float32r
AX_X = mybir.AxisListType.X

P = 128
T = 256
D = 2048
KT = D // P
HY = 6
D_HY = HY * P
FF_TILES = 5632 // P
FF_HALF = FF_TILES // 2
CHUNK = 64
NCH = T // CHUNK
HEADS_A = 8
HEADS_C = 4
SUB = 8
NEG = -1e30
TWO_PI = 2.0 * np.pi
ROUND = float(1.5 * 2 ** 23)
PI_HI = 6.28125
PI_LO = float(np.float32(TWO_PI - PI_HI))
PI_CUT = 3.1415925

RING = 4
UK = 4
UN = 256

U_IN = 17 * 4
U_OUT = 8 * 4
U_UP = FF_HALF * 4
U_DOWN = 4 * 11
U_LORA = 4
U_RA = HEADS_A * 16
U_MEM = 8 * 4
U_C = HEADS_C * 8
U_MERGE = 8 * 18
UNITS = U_IN + U_OUT + 2 * (U_UP + U_DOWN) + U_LORA + U_RA + U_MEM + U_C + U_MERGE + U_OUT

PARAMS = [("norm_mix", 16), ("pool_b", 4), ("pool_scale", 4), ("hy_w", 54), ("hy_b", 18), ("hy_skip", 6),
          ("gm_g", 6), ("gm_b", 6), ("norm_ffn", 16), ("ffn", 8 * FF_TILES), ("norm_final", 16),
          ("norm_g", 16), ("mem_g", 16), ("rwkv", 80), ("mu_wa", 1), ("w0", 8), ("a0", 8), ("aq_g", 1),
          ("ak_g", 1), ("cq_g", 2), ("ck_g", 2), ("f_b1", 1), ("f_fr1", 1), ("f_b2", 1), ("f_fr2", 1)]
COL = {}
_at = 0
for _name, _n in PARAMS:
    COL[_name] = _at
    _at += _n
NPAR = _at
MU_R, MU_K, MU_V, K_K, K_A, R_K, LN_W, LN_B, RW_COLS = 0, 1, 2, 3, 4, 5, 6, 7, 10

CONSTS = [("ident", 128), ("upper", 128), ("upper_in", 128), ("lower_in", 128), ("lower_out", 128),
          ("upper_eq", 64), ("ones", 128), ("head_ones", 128), ("center", 128), ("eps6", 1), ("eps5", 1),
          ("eps_gn", 1), ("eps12", 1)]
CC = {}
_at = 0
for _name, _n in CONSTS:
    CC[_name] = (_at, _n)
    _at += _n
NCONST = _at


def const_tables():
    r = np.arange(P)[:, None]
    c = np.arange(P)[None, :]
    same = (r // 64) == (c // 64)
    block = (r // SUB) == (c // SUB)
    eye = (r == c)
    parts = {
        "ident": eye, "upper": same & (r < c), "upper_in": block & (r < c), "lower_in": block & (r > c),
        "lower_out": same & (r > c) & ~block, "upper_eq": (r % 64) <= np.arange(64)[None, :],
        "ones": np.ones((P, P)), "head_ones": same, "center": eye - same / 64.0,
        "eps6": np.full((P, 1), 1e-6), "eps12": np.full((P, 1), 1e-12), "eps5": np.full((P, 1), 1e-5),
        "eps_gn": np.full((P, 1), 64e-5),
    }
    return np.concatenate([parts[n].astype(np.float32) for n, _ in CONSTS], axis=1)


def hyena_tables():
    f32 = np.float32
    t = np.arange(T)
    theta = 2.0 * np.pi / (2 * T) * (np.arange(T) + 0.5)
    ang = t[:, None] * theta[None, :]
    cos, sin = np.cos(ang), np.sin(ang)
    tables = np.stack([cos, sin, cos.T / T, sin.T / T]).astype(f32)
    tables = tables.reshape(4, 2, P, T).transpose(2, 0, 1, 3)
    tt = np.linspace(0.0, 1.0, T, dtype=f32)[:, None]
    w = (2.0 * np.pi * np.arange(T)[:, None] / T).astype(f32)
    f = np.linspace(1e-4, 15, 16, dtype=f32)[None, :]
    fw = (f * w).astype(np.float64)
    feat = np.concatenate([tt, np.cos(fw), -np.sin(fw)], axis=-1).astype(f32)
    lo = np.log(1e-2)
    deltas = np.linspace(lo / 1.5, lo / 0.3, D_HY, dtype=f32)
    decay = np.exp(-(tt * np.abs(deltas)[None, :]).astype(np.float64)).astype(f32)
    decay = decay.reshape(2, P, D_HY).transpose(1, 0, 2)
    inv = np.zeros((4, T), f32)
    for g, win in enumerate((2, 4, 8, 16)):
        a = np.maximum(t - win // 2, 0)
        b = np.minimum(t + win // 2 - 1, T - 1)
        inv[g] = 1.0 / (b - a + 1)
    return tables, feat.T, decay, np.broadcast_to(inv, (P, 4, T))


MEM_QUARTERS = ((0, 1), (2, 3), (), ())
MEM_SPLIT = ((), (), (0, 1), (2, 3))


class Counts:

    def __init__(self, eng):
        self.eng = eng
        self.base = {}
        self.extra = {}

    def next(self, key, by=1):
        self.extra[key] = self.extra.get(key, 0) + by
        return self.now(key)

    def now(self, key):
        return self.base.get(key, 0) + self.extra.get(key, 0)

    @contextmanager
    def loop(self, n, per):
        base, extra = self.base, self.extra
        keys = set(base) | set(extra) | set(per)
        before = {k: base.get(k, 0) + extra.get(k, 0) for k in keys}
        self.base, self.extra = {}, {}
        with self.eng.Fori(0, n) as i:
            for k in keys:
                self.base[k] = before[k] + i * per[k] if k in per else before[k]
            yield i
            moved = {k: v for k, v in self.extra.items() if v}
            assert moved == per, f"one iteration moves {moved}"
        self.base = base
        self.extra = {k: extra.get(k, 0) + n * per.get(k, 0) for k in keys}


def build(nc, a):
    out_ap = a["out"]
    with ExitStack() as ctx:
        def sb(name, shape, dt=F32):
            return ctx.enter_context(nc.sbuf_tensor(name, shape, dt))

        def sem(name):
            return ctx.enter_context(nc.semaphore(name))

        banks = [ctx.enter_context(nc.psum_tensor(f"bank{i}", [P, 512], F32)) for i in range(8)]

        raw = [sb(f"raw{i}", [P, UK, UN]) for i in range(RING)]
        w_hi = [sb(f"w_hi{i}", [P, UK, UN], F32R) for i in range(RING)]
        w_lo = [sb(f"w_lo{i}", [P, UK, UN], F32R) for i in range(RING)]
        x = sb("x", [P, KT, T])
        h_hi = sb("h_hi", [P, KT, T], F32R)
        h_lo = sb("h_lo", [P, KT, T], F32R)
        par = sb("par", [P, NPAR])
        con = sb("con", [P, NCONST])
        arena_at = nc.sbuf_base
        arena_at = (arena_at + 31) // 32 * 32
        usable = nc.sbuf_usable_end - arena_at

        placed = {}

        def place(name, shape, at, dt=F32):
            size = 4 * int(np.prod(shape[1:]))
            assert at + size <= usable, (name, at + size, usable)
            placed[name] = at + size
            return nc.alloc_sbuf_tensor_at(name, shape, dt, offset=arena_at + at)

        K = 1024
        spare = place("spare", [P, 8], 105 * K)
        y_hi = place("y_hi", [P, KT, T], 0, F32R)
        y_lo = place("y_lo", [P, KT, T], 16 * K, F32R)
        scratch = place("scratch", [P, KT, T], 0)
        root = place("root", [P, T], 103 * K)
        acc = place("acc", [P, 4, T], 99 * K)
        x0 = place("x0", [P, HY, T], 32 * K)
        z1 = place("z1", [P, HY, T], 38 * K)
        zv = place("zv", [P, HY, T], 44 * K)
        k_re = place("k_re", [P, 2, D_HY], 50 * K)
        k_im = place("k_im", [P, 2, D_HY], 56 * K)
        dft = place("dft", [P, 4, 2, T], 62 * K)
        decay = place("decay", [P, 2, D_HY], 70 * K)
        f_fwd = place("f_fwd", [P, 2, D_HY], 76 * K)
        f_bwd = place("f_bwd", [P, 2, D_HY], 82 * K)
        f_sum = place("f_sum", [P, 2, D_HY], 88 * K)
        feat = place("feat", [33, T], 94 * K)
        fw1 = place("fw1", [33, 64], 95 * K)
        fw2 = place("fw2", [64, 64], 95 * K + 256)
        fh = [place(f"fh{i}", [64, T], (96 + i) * K) for i in range(4)]
        fw3 = place("fw3", [64, 2 * D_HY], 16 * K)
        gv = place("gv", [P, HY, T], 70 * K)
        gu = place("gu", [P, HY, T], 76 * K)
        gsq = place("gsq", [P, HY, T], 82 * K)
        gvt = place("gvt", [P, 2, D_HY], 82 * K)
        zt = place("zt", [P, 2, D_HY], 88 * K)
        ws = place("ws", [P, HY, P], 94 * K)
        pw = place("pw", [P, 4, P], 97 * K)
        bs = place("bs", [1, HY * P], 99 * K)
        prod = [place(f"prod{i}", [P, 384], (38 + 6) * K + 1536 * i) for i in range(4)]
        mix = place("mix", [P, 2, T], 44 * K)
        PW = 272
        pool_x = place("pool_x", [P, 4, PW], 50 * K)
        pool_a = place("pool_a", [P, 4, PW], 50 * K + 4352)
        pool_b = place("pool_b", [P, 4, PW], 50 * K + 2 * 4352)
        inv = place("inv", [P, 4, T], 64 * K)
        pool_d = place("pool_d", [P, 4, T], 32 * K)
        y_part = place("y_part", [P, 4, T], 88 * K)
        m_hi = place("m_hi", [P, FF_HALF, T], 0, F32R)
        m_lo = place("m_lo", [P, FF_HALF, T], 22 * K, F32R)
        scratch2 = place("scratch2", [P, KT, T], 46 * K)
        conv_o = place("conv_o", [P, 2, 2, T], 62 * K)
        conv_m = place("conv_m", [P, 2, T], 66 * K)
        root2 = place("root2", [P, T], 70 * K)
        root3 = place("root3", [P, T], 71 * K)
        sq2 = place("sq2", [P, 2, T], 96 * K)
        acc_x = place("acc_x", [P, 2, T], 98 * K)
        acc_g = place("acc_g", [P, 2, T], 100 * K)
        gains = place("gains", [P, 2, KT], 102 * K)
        yall = place("yall", [P, 24, T], 0)
        cum = place("cum", [P, 8, T], 24 * K)
        icl = place("icl", [P, 8, T], 32 * K)
        bd = {}
        at = 40 * K
        for n in ("a", "b", "k", "v", "Nt", "N", "No", "Kt", "Q", "F", "Vt", "At", "Bt", "Kk", "b1", "b2",
                  "b3", "AkV", "Y"):
            bd[n] = place("m_" + n, [P, NCH, P], at)
            at += 2 * K
        BK = place("m_BK", [P, 2, NCH, CHUNK], at)
        at += 2 * K
        small = {}
        for n, w in (("pr", 257), ("pk", 257), ("pv", 257), ("t0", 256), ("r", 256), ("k0", 256), ("v", 256),
                     ("k2", 256), ("kk", 256), ("sq", 256), ("rk", 256), ("bz", 256), ("ep", 260), ("en", 256),
                     ("a_rt", 512)):
            small[n] = place("s_" + n, [P, w], at)
            at += (4 * w + 31) // 32 * 32
        for i, n in ((0, "o"), (1, "gsq"), (1, "groot"), (0, "gk"), (2, "bon")):
            small[n] = place("s_" + n, [P, T], (16 + i) * K)
        a_rt = small["a_rt"][:, :].rearrange("p (c q t) -> p c q t", c=NCH, q=2)
        prb = place("prb", [P, 384], 20 * K)
        av_t = place("av_t", [P, 2, P], 20 * K + 1536)
        avf = place("avf", [P, T], 21 * K + 1536)
        S = place("S", [P, 2, P], at)
        SA = place("SA", [P, 2, P], 19 * K)
        S_dec = place("S_dec", [P, P], at + 1024)
        at += 1536
        qk = place("qk", [P, 2, T], at)
        qr = place("qr", [P, 2, T], at + 2048)
        az = place("az", [P, T], at + 4096)
        bias_t = place("bias_t", [P, 384], at + 5120)
        stat = place("stat", [P, 16], at + 6656)
        prt = place("prt", [P, 384], at + 2048)
        lora = place("lora", [P, 1024], 40 * K)
        lx = place("lx", [P, 257], 44 * K)
        lt = place("lt", [P, T], 46 * K)
        ping = place("ping", [P, 8, T], 48 * K)
        cqs = place("cqs", [P, 8, T], 24 * K)
        czs = place("czs", [P, 8, T], 32 * K)
        memx = place("memx", [P, KT, T], 40 * K)
        mh_hi = place("mh_hi", [P, KT, T], 56 * K, F32R)
        mh_lo = place("mh_lo", [P, KT, T], 72 * K, F32R)
        scratch3 = place("scratch3", [P, KT, T], 88 * K)
        croot = place("croot", [P, T], 23 * K)
        memroot = place("memroot", [P, T], 22 * K)
        memacc = place("memacc", [P, 4, T], 16 * K)
        csq = place("csq", [P, 2, T], 20 * K)
        mk = place("mk", [P, 8, T], 40 * K)
        mvt = place("mvt", [P, 2, 8 * P], 48 * K)
        cpair = place("cpair", [P, 2, T], 88 * K)
        cp = place("cp", [P, 2, T], 90 * K)
        msq = place("msq", [P, 2, T], 92 * K)
        mroot = place("mroot", [P, T], 94 * K)
        cstat = place("cstat", [P, 16], 95 * K)
        cpt = [place(f"cpt{h}", [P, 2, T], (96 + 2 * h) * K) for h in range(HEADS_C)]
        ya_hi = place("ya_hi", [P, 24, T], 24 * K, F32R)
        ya_lo = place("ya_lo", [P, 24, T], 48 * K, F32R)
        gate = place("gate", [P, 2, T], 72 * K)
        macc = place("macc", [P, 2, T], 74 * K)
        mtmp = place("mtmp", [P, 2, T], 76 * K)
        mg_hi = place("mg_hi", [P, KT, T], 78 * K, F32R)
        mg_lo = place("mg_lo", [P, KT, T], 0, F32R)
        obuf = place("obuf", [P, KT, T], 24 * K)

        landed = [sem(f"unit_landed{i}") for i in range(RING)]
        hi_done = sem("hi_done")
        split_done = sem("split_done")
        unit_used = sem("unit_used")
        bank_read = [sem(f"bank_read{i}") for i in range(4)]
        psum_for_dve = sem("psum_for_dve")
        psum_for_act = sem("psum_for_act")
        dve_for_pe = sem("dve_for_pe")
        act_for_pe = sem("act_for_pe")
        dve_for_act = sem("dve_for_act")
        act_for_dve = sem("act_for_dve")
        dve_step = sem("dve_step")
        x_in = [sem(f"x_in{c}") for c in range(4)]
        tab_in = sem("tab_in")
        filt_in = sem("filt_in")
        tables_in = sem("tables_in")
        mixer_in = sem("mixer_in")
        inv_in = sem("inv_in")
        mem_in = [sem(f"mem_in{c}") for c in range(4)]
        lora_in = sem("lora_in")
        free_early = sem("free_early")
        free_inv = sem("free_inv")
        free_lora = sem("free_lora")
        free_mem = sem("free_mem")
        keys_ready = sem("keys_ready")
        head_sums = sem("head_sums")
        sums_read = sem("sums_read")
        qk_squared = sem("qk_squared")
        qk_sums = sem("qk_sums")
        bias_in = sem("bias_in")
        bias_used = sem("bias_used")
        hidden_ready = sem("hidden_ready")
        head_written = sem("head_written")
        merged_ready = sem("merged_ready")
        stored = sem("stored")

        PROJ = [banks[0], banks[1], banks[3], banks[4]]

        def p2(b):
            return PROJ[b][:, :].rearrange("p (s t) -> p s t", s=2)

        def col(name, i=0):
            return par[:, bass.ds(COL[name] + i, 1)]

        def con_(name):
            s, n = CC[name]
            return con[:, s:s + n]

        def b4(bank):
            return banks[bank][:, :].rearrange("p (c t) -> p c t", c=4)

        def bcast(ap2d, n):
            return ap2d.unsqueeze(1).broadcast_to([P, n, ap2d.shape[1]])

        final_fill = {}
        block = ctx.enter_context(nc.Block())

        @block.gpsimd
        def _(pool):
            for dst, src in ((feat[:, :], "feat"), (fw1[:, :], "fw1"), (fw2[:, :], "fw2")):
                pool.dma_start(dst, a[src]).then_inc(filt_in, 16)
            pool.wait_ge(landed[1], 16)
            for dst, src in ((fw3[:, :], "fw3"), (decay[:, :, :], "decay"), (dft[:, :, :, :], "dft")):
                pool.dma_start(dst, a[src]).then_inc(tables_in, 16)
            pool.wait_ge(free_early, 1)
            for dst, src in ((ws[:, :, :], "ws"), (pw[:, :, :], "pw"), (bs[:, :], "bs")):
                pool.dma_start(dst, a[src]).then_inc(mixer_in, 16)
            pool.wait_ge(free_inv, 1)
            pool.dma_start(inv[:, :, :], a["inv"]).then_inc(inv_in, 16)
            pool.wait_ge(free_lora, 1)
            pool.dma_start(lora[:, :], a["lora"]).then_inc(lora_in, 16)
            with pool.Fori(0, HEADS_A) as g:
                pool.wait_ge(bias_used, g + 1)
                pool.dma_start(bias_t[:, :], a["bias"][g]).then_inc(bias_in, 16)
            pool.wait_ge(free_mem, 1)
            for c in range(4):
                cs = slice(4 * c, 4 * c + 4)
                pool.dma_start(memx[:, cs, :], a["memT"][:, cs, :]).then_inc(mem_in[c], 16)

        @block.tensor
        def _(pe):
            n = Counts(pe)
            slots = count()

            def mm(out, lhsT, rhs, start=True, stop=True):
                return pe.matmul(out, lhsT, rhs, start=start, stop=stop, skip_group_check=True)

            def unit(bank, k0, hi, lo, first, last, tiles=2, fresh=True):
                slot = next(slots) % RING
                pe.wait_ge(split_done, n.next("split"))
                o = p2(bank)
                for kk in range(UK):
                    for t in range(tiles):
                        wh = w_hi[slot][:, kk, t * P:(t + 1) * P]
                        wl = w_lo[slot][:, kk, t * P:(t + 1) * P]
                        rh, rl = hi[:, k0 + kk, :], lo[:, k0 + kk, :]
                        mm(o[:, t, :], wh, rh, first and kk == 0 and t == 0, False)
                        mm(o[:, t, :], wh, rl, False, False)
                        m = mm(o[:, t, :], wl, rh, False, last and kk == UK - 1 and t == tiles - 1)
                m.then_inc(unit_used, 1)

            def group(bank, hi, lo, k0=0, units=4, tiles=2, filled=True, arriving=False, ready=None):
                if filled:
                    pe.wait_ge(bank_read[bank], n.now(("fill", bank)))
                n.next(("fill", bank))
                for u in range(units):
                    if arriving:
                        from_dve()
                    if ready:
                        pe.wait_ge(ready[0], ready[1][u])
                    unit(bank, k0 + UK * u, hi, lo, u == 0, u == units - 1, tiles)

            def from_dve(k=1):
                pe.wait_ge(dve_for_pe, n.next("dve", k))

            def from_act(k=1):
                pe.wait_ge(act_for_pe, n.next("act", k))

            def norm_sums(*accs, k=2):
                from_dve()
                for i, src in enumerate(accs):
                    for t in range(k):
                        m = mm(banks[2][:, i * T:(i + 1) * T], con_("ones"), src[:, t, :], t == 0, t == k - 1)
                m.then_inc(psum_for_act, 1)

            pe.wait_ge(tab_in, 32)
            norm_sums(acc)
            group(0, h_hi, h_lo, filled=False, arriving=True)
            pe.wait_ge(filt_in, 3 * 16)
            mm(banks[3][0:64, 0:T], fw1[:, :], feat[:, :]).then_inc(psum_for_dve, 1)
            group(1, h_hi, h_lo, filled=False)
            from_act()
            mm(banks[3][0:64, 0:T], fw2[:, :], fh[3][:, :]).then_inc(psum_for_dve, 1)
            group(0, h_hi, h_lo)
            from_act()
            pe.wait_ge(tables_in, 3 * 16)
            for c in range(2):
                for q in range(4):
                    if c == 1:
                        from_dve()
                    mm(banks[3 + q][:, 0:384], fh[3][:, c * P:(c + 1) * P], fw3[:, q * 384:(q + 1) * 384])\
                        .then_inc(psum_for_dve, 1)
            group(1, h_hi, h_lo)
            from_dve(4)
            from_dve()
            for q, (tab, src) in enumerate(((0, f_sum), (1, f_bwd))):
                for f in range(2):
                    for c in range(2):
                        b = 3 + (4 * q + 2 * f + c) % 4
                        if q == 1:
                            from_act()
                        for k in range(2):
                            m = mm(banks[b][:, 0:384], dft[:, tab, k, f * P:(f + 1) * P],
                                   src[:, k, c * 384:(c + 1) * 384], k == 0, k == 1)
                        m.then_inc(psum_for_act, 1)
            from_act(4)
            for p in range(4, 9):
                group(p % 2, h_hi, h_lo)
            group(1, h_hi, h_lo)
            from_dve()
            for c in range(2):
                for half in range(2):
                    b = 3 + 2 * c + half
                    for j in range(3):
                        m = pe.transpose(banks[b][:, j * P:(j + 1) * P], z1[:, 3 * half + j, c * P:(c + 1) * P],
                                         con_("ident"))
                    m.then_inc(psum_for_act, 1)
            group(0, h_hi, h_lo)
            group(1, h_hi, h_lo)
            from_act(4)
            for i, (f, c) in enumerate(((0, 0), (0, 1), (1, 0), (1, 1))):
                if i >= 2:
                    from_dve()
                for part in range(2):
                    b = 3 + 2 * (i % 2) + part
                    for k in range(2):
                        m = mm(banks[b][:, 0:384], dft[:, part, k, f * P:(f + 1) * P],
                               zt[:, k, c * 384:(c + 1) * 384], k == 0, k == 1)
                m.then_inc(psum_for_dve, 1)
            group(0, h_hi, h_lo)
            from_dve(3)
            for j in range(HY):
                o = banks[3 + j // 2][:, (j % 2) * T:(j % 2 + 1) * T]
                for i, (src, tab, k) in enumerate(((k_re, 2, 0), (k_re, 2, 1), (k_im, 3, 0), (k_im, 3, 1))):
                    m = mm(o, src[:, k, j * P:(j + 1) * P], dft[:, tab, k, :], i == 0, i == 3)
                if j % 2:
                    m.then_inc(psum_for_dve, 1)
            from_act()
            for j in range(HY):
                m = mm(banks[6][:, 0:T], con_("ones"), gv[:, j, :], j == 0, j == HY - 1)
            m.then_inc(psum_for_dve, 1)
            group(1, h_hi, h_lo)
            from_act()
            for j in range(HY):
                m = mm(banks[7][:, 0:T], con_("ones"), gsq[:, j, :], j == 0, j == HY - 1)
            m.then_inc(psum_for_act, 1)
            group(0, h_hi, h_lo)
            from_dve()
            for e in range(HY):
                for c in range(2):
                    i = 2 * c + e % 2
                    m = pe.transpose(banks[3 + e // 2][:, i * P:(i + 1) * P], gv[:, e, c * P:(c + 1) * P],
                                     con_("ident"))
                if e % 2:
                    m.then_inc(psum_for_act, 1)
            group(1, h_hi, h_lo)
            pe.wait_ge(mixer_in, 3 * 16)
            from_act(3)
            for e in range(HY):
                for c in range(2):
                    o = banks[3 + e // 2][:, (e % 2) * T + c * P:(e % 2) * T + (c + 1) * P]
                    mm(o, gvt[:, c, e * P:(e + 1) * P], ws[:, e, :], True, False)
                    m = mm(o, con[0:1, CC["ones"][0]:CC["ones"][0] + P], bs[0:1, e * P:(e + 1) * P], False, True)
                if e % 2:
                    m.then_inc(psum_for_dve, 1)
            from_dve()
            for g in range(4):
                m = mm(banks[6 + g // 2][:, (g % 2) * T:(g % 2 + 1) * T], pw[:, g, :], pool_d[:, g, :])
            m.then_inc(psum_for_dve, 1)
            group(0, h_hi, h_lo)
            most, rest = n.next("dve"), n.next("dve")
            with n.loop(4, {("fill", 0): 1, ("fill", 1): 1, "split": 8}):
                group(1, y_hi, y_lo, ready=(dve_for_pe, (most, most, most, rest)))
                group(0, y_hi, y_lo)
            norm_sums(acc_x)
            quarters = [n.next("dve") for _ in range(4)]
            n.next(("fill", 2))
            n.next(("fill", 3))
            with n.loop(2, {("fill", 0): 13, ("fill", 1): 13, ("fill", 2): 2, ("fill", 3): 2,
                            "split": U_UP + U_DOWN, "hidden": FF_HALF}):
                with n.loop(FF_HALF // 2, {("fill", 0): 1, ("fill", 1): 1, "split": 8}):
                    for b in (1, 0):
                        group(b, h_hi, h_lo, ready=(dve_for_pe, quarters) if b else None)
                for q in range(4):
                    pair = (1, 0) if q % 2 else (2, 3)
                    for b in pair:
                        pe.wait_ge(bank_read[b], n.now(("fill", b)))
                        n.next(("fill", b))
                    for u in range(11):
                        slot = next(slots) % RING
                        if q == 0:
                            pe.wait_ge(hidden_ready, n.next("hidden", 2))
                        pe.wait_ge(split_done, n.next("split"))
                        wh4 = w_hi[slot][:, :, :].rearrange("p k n -> p (k n)").rearrange("p (k n) -> p k n", k=2)
                        wl4 = w_lo[slot][:, :, :].rearrange("p k n -> p (k n)").rearrange("p (k n) -> p k n", k=2)
                        for kk in range(2):
                            for t in range(4):
                                o = p2(pair[t // 2])[:, t % 2, :]
                                wh, wl = wh4[:, kk, t * P:(t + 1) * P], wl4[:, kk, t * P:(t + 1) * P]
                                rh, rl = m_hi[:, 2 * u + kk, :], m_lo[:, 2 * u + kk, :]
                                mm(o, wh, rh, u == 0 and kk == 0 and t % 2 == 0, False)
                                mm(o, wh, rl, False, False)
                                m = mm(o, wl, rh, False, u == 10 and kk == 1 and t % 2 == 1)
                        m.then_inc(unit_used, 1)
            norm_sums(acc_x, acc_g)
            group(1, h_hi, h_lo, tiles=1, arriving=True)

            ident = con_("ident")

            def per_chunk(bank, lhs, rhs):
                o = b4(bank)
                for c in range(NCH):
                    m = mm(o[:, c, :], lhs[:, c, :], rhs[:, c, :])
                return m

            def turned(bank, src):
                o = b4(bank)
                for c in range(NCH):
                    m = pe.transpose(o[:, c, :], src[:, c, :], ident)
                return m

            part_slot = []

            def part(k, half=None, hi=h_hi, lo=h_lo, banks_of=(0, 1, 0, 1)):
                bank = banks_of[k // 4]
                if half != 1:
                    if k % 4 == 0:
                        pe.wait_ge(bank_read[bank], n.now(("fill", bank)))
                        n.next(("fill", bank))
                    pe.wait_ge(split_done, n.next("split"))
                    part_slot.append(next(slots) % RING)
                slot = part_slot[-1]
                o = p2(bank)
                for kk in {None: range(4), 0: range(2), 1: range(2, 4)}[half]:
                    for t in range(2):
                        wh = w_hi[slot][:, kk, t * P:(t + 1) * P]
                        wl = w_lo[slot][:, kk, t * P:(t + 1) * P]
                        rh, rl = hi[:, (k % 4) * UK + kk, :], lo[:, (k % 4) * UK + kk, :]
                        mm(o[:, t, :], wh, rh, k % 4 == 0 and kk == 0 and t == 0, False)
                        mm(o[:, t, :], wh, rl, False, False)
                        m = mm(o[:, t, :], wl, rh, False, k % 4 == 3 and kk == 3 and t == 1)
                if half != 0:
                    m.then_inc(unit_used, 1)

            def heads(k, half=None):
                part(k, half)
                if k == 9 and half != 0:
                    pe.wait_ge(keys_ready, n.next("keys"))
                    mm(banks[7][:, 0:T], con_("head_ones"), small["sq"][:, :])
                    mm(banks[7][:, T:2 * T], con_("head_ones"), small["rk"][:, :]).then_inc(head_sums, 1)
                if k == 12:
                    pe.wait_ge(sums_read, n.next("sums"))
                    pe.wait_ge(qk_squared, n.next("qk"))
                    mm(banks[7][:, :], con_("ones"), qr[:, :, :].rearrange("p s t -> p (s t)")).then_inc(qk_sums, 1)

            def late(units):
                units(0)
                from_dve()
                a_, b_, k_, v_ = bd["a"], bd["b"], bd["k"], bd["v"]
                both = small["a_rt"][:, :].rearrange("p (c t) -> p c t", c=NCH)
                per_chunk(3, b_, both).then_inc(psum_for_dve, 1)
                per_chunk(4, a_, b_).then_inc(psum_for_dve, 1)
                per_chunk(5, k_, both).then_inc(psum_for_dve, 1)
                turned(2, v_).then_inc(psum_for_act, 1)
                from_act()
                for c in range(2):
                    m = pe.transpose(banks[7][:, c * P:(c + 1) * P], avf[:, c * P:(c + 1) * P], ident)
                m.then_inc(psum_for_act, 1)
                units(1)
                from_dve()
                per_chunk(3, bd["Nt"], bd["N"]).then_inc(psum_for_act, 1)
                per_chunk(4, bd["N"], bd["Nt"]).then_inc(psum_for_act, 1)
                from_dve()
                from_act()
                per_chunk(5, bd["Kt"], bd["Vt"]).then_inc(psum_for_act, 1)
                turned(6, a_).then_inc(psum_for_act, 1)
                turned(2, b_).then_inc(psum_for_act, 1)
                from_act()
                from_act(2)
                per_chunk(3, bd["b1"], bd["Q"]).then_inc(psum_for_dve, 1)
                per_chunk(4, bd["b2"], bd["b1"]).then_inc(psum_for_act, 1)
                from_dve()
                mm(banks[7][:, 0:P], qk[:, 0, 0:P], qk[:, 1, 0:P])
                mm(banks[7][:, P:P + T], qk[:, 0, P:T], qk[:, 1, :]).then_inc(psum_for_dve, 1)
                units(2)
                from_act(3)
                turned(5, k_).then_inc(psum_for_act, 1)
                from_dve()
                from_act()
                per_chunk(3, bd["b3"], bd["Q"]).then_inc(psum_for_dve, 1)
                units(3)
                from_dve()
                from_act()
                per_chunk(3, bd["No"], bd["Q"]).then_inc(psum_for_dve, 1)
                per_chunk(4, bd["Q"], bd["No"]).then_inc(psum_for_act, 1)
                per_chunk(5, bd["Q"], bd["At"]).then_inc(psum_for_act, 1)
                per_chunk(6, bd["Q"], bd["AkV"]).then_inc(psum_for_act, 1)
                units(4, 0)
                from_dve()
                from_act(1)
                per_chunk(3, bd["b2"], bd["b1"]).then_inc(psum_for_act, 1)
                per_chunk(4, bd["b1"], bd["b2"]).then_inc(psum_for_act, 1)
                units(4, 1)
                from_act(2)
                from_act(2)
                per_chunk(3, bd["N"], bd["F"]).then_inc(psum_for_dve, 1)
                per_chunk(4, bd["Nt"], bd["N"]).then_inc(psum_for_act, 1)
                from_dve()
                for i, o in enumerate((0, P, 2 * P)):
                    m = pe.transpose(banks[7][:, i * P:(i + 1) * P], prb[:, o:o + P], ident)
                m.then_inc(psum_for_act, 1)
                units(5)
                from_act(1)
                from_dve()
                per_chunk(3, bd["b3"], bd["F"]).then_inc(psum_for_dve, 1)
                units(6)
                from_dve()
                per_chunk(5, bd["Y"], bd["F"]).then_inc(psum_for_act, 1)
                per_chunk(6, bd["F"], bd["Kt"]).then_inc(psum_for_act, 1)
                units(7, 0)
                from_act(3)

                def sa_of(c):
                    return SA[:, c % 2, :] if c else bd["b1"][:, 0, :]

                def state(c):
                    mm(banks[4][:, 0:P], bd["Bt"][:, c, :], sa_of(c), True, False)
                    mm(banks[4][:, 0:P], bd["Kk"][:, c, :], bd["Vt"][:, c, :], False, True)\
                        .then_inc(psum_for_dve, 1)

                def output(c):
                    cs = slice(c * CHUNK, (c + 1) * CHUNK)
                    mm(banks[3][:, cs], sa_of(c), BK[:, 0, c, :], True, False)
                    if c:
                        mm(banks[3][:, cs], S[:, c % 2, :], a_rt[:, c, 1, :], False, False)
                    return mm(banks[3][:, cs], bd["Vt"][:, c, :], BK[:, 1, c, :], False, True)

                def solve(c):
                    from_dve()
                    mm(banks[2][:, 0:P], bd["b2"][:, c, :], S[:, c % 2, :]).then_inc(psum_for_dve, 1)

                state(0)
                output(0)
                mm(banks[5][:, 0:P], av_t[:, 0, :], prt[:, 0:P])
                mm(banks[5][:, P:T], av_t[:, 0, :], prt[:, P:T], True, False)
                mm(banks[5][:, P:T], av_t[:, 1, :], prt[:, T:T + P], False, True).then_inc(psum_for_dve, 1)
                units(7, 1)
                solve(1)
                units(8, 0)
                from_dve()
                state(1)
                output(1)
                units(8, 1)
                solve(2)
                units(9, 0)
                from_dve()
                state(2)
                output(2)
                units(9, 1)
                solve(3)
                units(10)
                from_dve()
                output(3).then_inc(psum_for_act, 1)
                units(11, 0)
                from_act()
                mm(banks[4][:, 0:T], con_("center"), small["o"][:, :]).then_inc(psum_for_act, 1)
                units(11, 1)
                from_act()
                mm(banks[6][:, 0:T], con_("head_ones"), small["gsq"][:, :]).then_inc(psum_for_act, 1)
                for k in range(12, 16):
                    units(k)

            late_counts = {"dve": 16, "act": 21}
            pair_counts = {("fill", 0): 2, ("fill", 1): 2, "split": 16, "keys": 1, "sums": 1, "qk": 1}
            for k in range(16):
                heads(k)
                if k == 1:
                    from_act()
                    pe.wait_ge(lora_in, 16)
                if 1 <= k <= 4:
                    for j in (2 * k - 2, 2 * k - 1):
                        if j >= 2:
                            from_act()
                        mm(banks[3 + j % 2][:, 0:T], lora[0:64, j * P:(j + 1) * P], lt[0:64, :])
                        mm(banks[5 + j % 2][:, 0:T], lora[64:128, j * P:(j + 1) * P], lt[64:128, :])\
                            .then_inc(psum_for_act, 1)
                if k == 4:
                    from_act(2)
            with n.loop(HEADS_A - 1, late_counts | pair_counts):
                late(heads)
            late(part)

            def channel_sums(src, bank=7):
                for s in range(2):
                    m = mm(banks[bank][:, 0:T], con_("ones"), src[:, s, :], s == 0, s == 1)
                m.then_inc(psum_for_act, 1)

            for h in range(HEADS_C):
                part(4 * h)
                part(4 * h + 1)
                from_act()
                channel_sums(csq)
                if h == 2:
                    norm_sums(memacc)
                for k in range(2, 4):
                    part(4 * h + k)
            for j in range(4):
                if j == 0:
                    from_dve()
                part(4 * j, None, mh_hi, mh_lo)
                for k in range(1, 4):
                    if j == 0:
                        from_dve()
                    part(4 * j + k, None, mh_hi, mh_lo)
                    if j and k == 1:
                        from_act()
                        channel_sums(msq)
            for j in range(4):
                part(4 * j, None, mh_hi, mh_lo)
                if j:
                    from_act(2 if j > 1 else 1)
                if j == 0:
                    from_act()
                    channel_sums(msq)
                else:
                    pe.wait_ge(bank_read[(j - 1) % 2], n.now(("fill", (j - 1) % 2)))
                    for c in range(2):
                        for s in range(2):
                            m = pe.transpose(banks[6][:, (2 * c + s) * P:(2 * c + s + 1) * P],
                                             cpair[:, s, c * P:(c + 1) * P], ident)
                    m.then_inc(psum_for_act, 1)
                part(4 * j + 1, None, mh_hi, mh_lo)
                if j == 0:
                    part(2, None, mh_hi, mh_lo)
                    from_dve()
                for q in range(2):
                    for s in range(2):
                        m = mm(banks[3][:, q * T:(q + 1) * T], cqs[:, 2 * j + s, q * P:(q + 1) * P],
                               mk[:, 2 * j + s, :], s == 0, s == 1)
                m.then_inc(psum_for_dve, 1)
                if j:
                    part(4 * j + 2, None, mh_hi, mh_lo)
                part(4 * j + 3, None, mh_hi, mh_lo)
                from_dve()
                for c in range(2):
                    for q in range(2):
                        m = pe.transpose(banks[4][:, (2 * c + q) * P:(2 * c + q + 1) * P],
                                         cp[:, q, c * P:(c + 1) * P], ident)
                m.then_inc(psum_for_act, 1)
            from_act(2)
            pe.wait_ge(bank_read[1], n.now(("fill", 1)))
            for c in range(2):
                for s in range(2):
                    m = pe.transpose(banks[6][:, (2 * c + s) * P:(2 * c + s + 1) * P],
                                     cpair[:, s, c * P:(c + 1) * P], ident)
            m.then_inc(psum_for_act, 1)
            from_act()
            for h in range(HEADS_C):
                o = banks[(3, 4, 5, 7)[h]]
                for s in range(2):
                    for c in range(2):
                        m = mm(o[:, s * T:(s + 1) * T], mvt[:, c, (2 * h + s) * P:(2 * h + s + 1) * P],
                               cpt[h][:, c, :], c == 0, c == 1)
                m.then_inc(psum_for_dve, 1)
            y_split = n.next("dve")
            with n.loop(4, {("fill", 0): 6, ("fill", 1): 6, "split": 36}):
                for j in range(2):
                    for m3 in range(3):
                        group(0, h_hi, h_lo)
                        group(1, ya_hi, ya_lo, k0=8 * m3, units=2,
                              ready=None if j or m3 else (dve_for_pe, (y_split, y_split)))
            final_fill.update({b: n.now(("fill", b)) for b in (0, 1)})
            with n.loop(4, {("fill", 0): 1, ("fill", 1): 1, "split": 8}):
                group(0, mg_hi, mg_lo, ready=(merged_ready, (6, 6, 6, 8)))
                group(1, mg_hi, mg_lo)

        @block.sync
        def _(sp):
            for c in range(4):
                cs = slice(4 * c, 4 * c + 4)
                sp.dma_start(x[:, cs, :], a["xT"][:, cs, :]).then_inc(x_in[c], 16)
            sp.dma_start(par[:, :], a["par"]).then_inc(tab_in, 16)
            sp.dma_start(con[:, :], a["con"]).then_inc(tab_in, 16)
            for s in range(RING):
                sp.dma_start(raw[s][:, :, :], a["units"][s].rearrange("p (k n) -> p k n", k=UK))\
                    .then_inc(landed[s], 16)
            with sp.Fori(1, UNITS // RING) as i:
                for s in range(RING):
                    sp.wait_ge(split_done, i * RING + (s - RING + 1))
                    sp.dma_start(raw[s][:, :, :], a["units"][i * RING + s].rearrange("p (k n) -> p k n", k=UK))\
                        .then_inc(landed[s], 16)
            for j in range(8):
                sp.wait_ge(bank_read[j % 2], final_fill[j % 2] + j // 2 + 1)
                sp.dma_start(out_ap[:, 2 * j:2 * j + 2, :], obuf[:, 2 * j:2 * j + 2, :]).then_inc(stored, 16)
            sp.wait_ge(stored, 16 * 8)


        @block.scalar
        def _(act):
            n = Counts(act)
            slots = count()

            def send(ins, to):
                ins.then_inc(to, 1)

            def copy(out, in_, scale=1.0):
                return act.activation(out, in_, ACT.Copy, scale=scale)

            def split():
                slot = next(slots) % RING
                u = n.next("unit")
                act.wait_ge(landed[slot], n.next(("landed", slot), 16))
                if not isinstance(u, int) or u > RING:
                    act.wait_ge(unit_used, u - RING)
                copy(w_hi[slot][:, :, :], raw[slot][:, :, :]).then_inc(hi_done, 1)

            def split4(k=4):
                for _ in range(k):
                    split()

            def group_done():
                act.wait_ge(unit_used, n.now("unit") - RING)

            def psum(k=1):
                act.wait_ge(psum_for_act, n.next("psum", k))

            def from_dve(k=1):
                act.wait_ge(dve_for_act, n.next("dve", k))

            def to_pe(ins):
                ins.then_inc(act_for_pe, 1)

            def to_dve(ins):
                ins.then_inc(act_for_dve, 1)

            def squares(src, sq, arrived):
                for c in range(4):
                    act.wait_ge(arrived[c], 16)
                    cs = slice(4 * c, 4 * c + 4)
                    to_dve(act.activation(sq[:, cs, :], src[:, cs, :], ACT.Square))

            def root_of_mean(dst, src):
                psum()
                to_dve(act.activation(dst, src, ACT.Sqrt, bias=con_("eps6"), scale=1.0 / D))

            def high_halves(f, hi, with_units=False, quarters=range(4)):
                for c in quarters:
                    if with_units:
                        split()
                    cs = slice(4 * c, 4 * c + 4)
                    from_dve()
                    to_dve(copy(hi[:, cs, :], f[:, cs, :]))

            squares(x, scratch, x_in)
            act.wait_ge(tab_in, 32)
            act.activation(spare[:, 0:1], con_("eps6"), ACT.Sqrt)
            root_of_mean(root[:, :], banks[2][:, 0:T])
            high_halves(scratch, h_hi, with_units=True)

            def hyena(p):
                dst = (x0, z1, zv)[p // 3]
                j = 2 * (p % 3)
                b = p % 2
                group_done()
                n.next(("fill", b))
                for s in range(2):
                    m = act.activation(dst[:, j + s, :], p2(b)[:, s, :], ACT.Identity,
                                       bias=col("hy_b", 2 * p + s), scale=col("hy_w", 18 + 2 * p + s))
                to_dve(m)

            def sine():
                from_dve()
                to_pe(act.activation(fh[3][:, :], fh[2][:, :], ACT.Sin))

            split4()
            hyena(0)
            sine()
            split4()
            hyena(1)
            sine()
            split4()
            hyena(2)
            split4()
            hyena(3)
            for q, dst in enumerate((k_re, k_im)):
                for f in range(2):
                    for c in range(2):
                        psum()
                        to_pe(copy(dst[:, f, c * 384:(c + 1) * 384], banks[3 + (4 * q + 2 * f + c) % 4][:, 0:384]))
            for p in range(4, 9):
                split4()
                hyena(p)

            def gelu(p):
                dst = gv if p < 12 else gu
                j = 2 * (9, 10, 11, 12, 15, 16).index(p) % 6
                group_done()
                n.next(("fill", p % 2))
                act.activation(dst[:, j:j + 2, :], p2(p % 2), ACT.Gelu_apprx_tanh).then_inc(bank_read[p % 2], 1)

            def y_half(tile, k, s):
                from_dve()
                to_dve(copy(y_hi[:, tile:tile + k, :], y_part[:, s:s + k, :]))

            split4()
            gelu(9)
            for c in range(2):
                for half in range(2):
                    psum()
                    to_pe(copy(zt[:, c, half * 384:(half + 1) * 384], banks[3 + 2 * c + half][:, 0:384]))
            split4()
            gelu(10)
            split4()
            group_done()
            n.next(("fill", 1))
            act.activation(gv[:, 4:6, :], p2(1), ACT.Gelu_apprx_tanh).then_inc(bank_read[1], 1)
            split4()
            gelu(12)
            act.wait_ge(bank_read[0], n.now(("fill", 0)))
            act.activation(root[:, 0:1], gv[:, 5, 0:1], ACT.Copy).then_inc(act_for_pe, 1)
            for k in range(3):
                y_half(4 + 2 * k, 2, 2 * (k % 2))
            from_dve()
            to_pe(act.activation(gsq[:, :, :], gv[:, :, :], ACT.Square))
            def pool_in(p, b):
                group_done()
                n.next(("fill", b))
                copy(pool_x[:, 2 * (p - 13):2 * (p - 13) + 2, 8:8 + T], p2(b)).then_inc(bank_read[b], 1)

            split4()
            pool_in(13, 1)
            psum()
            to_dve(act.activation(root[:, :], banks[7][:, 0:T], ACT.Sqrt, bias=con_("eps5"), scale=1.0 / D_HY))
            split4()
            pool_in(14, 0)
            for k in range(3):
                psum()
                to_pe(copy(gvt[:, :, 2 * k * P:(2 * k + 2) * P],
                           banks[3 + k][:, :].rearrange("p (c t) -> p c t", c=2)))
            split4()
            gelu(15)
            for k in range(2):
                y_half(10 + 2 * k, 2, 2 * (k % 2))
            y_half(0, 4, 0)
            split4()
            gelu(16)
            y_half(14, 2, 0)

            with n.loop(4, {("landed", s): 32 for s in range(RING)} | {"unit": 8}):
                split4(8)
            for b in (0, 1):
                n.next(("fill", b), 4)
                act.wait_ge(bank_read[b], n.now(("fill", b)))
            act.activation(spare[:, 0:1], con_("eps6"), ACT.Sqrt)
            root_of_mean(root2[:, :], banks[2][:, 0:T])
            high_halves(scratch2, h_hi)

            def land(k):
                return {("landed", s): 16 * k // RING for s in range(RING)}

            with n.loop(2, land(U_UP + U_DOWN) | {"unit": U_UP + U_DOWN, "dve": 2 * FF_HALF,
                                                  ("fill", 0): 13, ("fill", 1): 13}) as half:
                with n.loop(FF_HALF // 2, land(8) | {"unit": 8, "dve": 4, ("fill", 0): 1, ("fill", 1): 1}) as j:
                    for q, b in enumerate((1, 0)):
                        base = half * (8 * FF_HALF) + j * 16 + 8 * q
                        o = conv_o[:, q, :, :]
                        split4()
                        group_done()
                        n.next(("fill", b))
                        for s in range(2):
                            m = act.activation(o[:, s, :], p2(b)[:, s, :], ACT.Identity,
                                               bias=col("ffn", base + (4 * s + 3)),
                                               scale=col("ffn", base + (4 * s + 1)))
                        to_dve(m)
                        from_dve()
                        to_dve(act.activation(o[:, 0, :], o[:, 0, :], ACT.Silu))
                        from_dve()
                        to_dve(copy(m_hi[:, j * 2 + q, :], conv_m[:, q, :]))
                for q in range(4):
                    split4(11)
                    if q % 2:
                        n.next(("fill", 0))
                        n.next(("fill", 1))
            act.activation(spare[:, 0:1], con_("eps6"), ACT.Sqrt)
            root_of_mean(root2[:, :], banks[2][:, 0:T])
            from_dve()
            to_dve(act.activation(root3[:, :], root3[:, :], ACT.Sqrt, bias=con_("eps12"), scale=1.0 / D))
            high_halves(scratch2, h_hi)
            split4()
            group_done()
            n.next(("fill", 1))
            copy(lx[:, 1:257], p2(1)[:, 0, :]).then_inc(bank_read[1], 1)
            from_dve()
            to_pe(act.activation(lt[0:64, :], lt[0:64, :], ACT.Tanh))

            def flat(t):
                return t[:, :, :].rearrange("p c t -> p (c t)")

            def keep(name, bank):
                psum()
                to_pe(copy(flat(bd[name]), banks[bank][:, :]))

            ep4 = small["ep"][:, :].rearrange("p (c t) -> p c t", c=NCH)
            def heads(k, g):
                split()
                if k % 4 == 3:
                    group_done()
                    n.next(("fill", (k // 4) % 2))
                if k == 3:
                    copy(small["pr"][:, 1:257], p2(0)[:, 0, :])
                    copy(small["pk"][:, 1:257], p2(0)[:, 1, :]).then_inc(bank_read[0], 1)
                if k == 7:
                    act.wait_ge(keys_ready, n.next("keys"))
                    copy(small["pv"][:, 1:257], p2(1)[:, 0, :])
                    to_dve(act.activation(small["k0"][:, :], p2(1)[:, 1, :], ACT.Tanh, scale=0.5))
                if k == 9:
                    from_dve()
                    to_dve(act.activation(small["sq"][:, :], small["sq"][:, :], ACT.Sqrt))
                if k == 11:
                    act.activation(qr[:, :, :], p2(0), ACT.Square).then_inc(qk_squared, 1)
                    copy(qk[:, :, :], p2(0)).then_inc(bank_read[0], 1)
                if k == 12:
                    act.wait_ge(qk_sums, n.next("qk"))
                    to_dve(act.activation(flat(qr), banks[7][:, :], ACT.Sqrt, bias=con_("eps6"), scale=1.0 / P))
                if k == 13:
                    cg_ = cum[:, bass.ds(g, 1), :].rearrange("p o t -> p (o t)")
                    rate = float(np.exp(-0.5))
                    act.activation(ep4[:, :, 1:65], cg_.rearrange("p (c t) -> p c t", c=NCH), ACT.Exp, scale=-rate)
                    act.activation(small["en"][:, :], cg_, ACT.Exp, scale=rate)
                    for h in range(2):
                        hs = slice(64 * h, 64 * h + 64)
                        m = copy(bd["v"][hs, :, hs], small["v"][hs, :].rearrange("p (c t) -> p c t", c=NCH))
                    to_dve(m)
                if k == 15:
                    to_pe(copy(avf[:, :], p2(1)[:, 0, :]))
                    to_dve(act.activation(az[:, :], p2(1)[:, 1, :], ACT.Tanh, scale=0.5))

            def queries(k):
                split()
                if k % 4 == 3:
                    h, b = k // 4, (k // 4) % 2
                    group_done()
                    n.next(("fill", b))
                    copy(cqs[:, 2 * h:2 * h + 2, :], p2(b)).then_inc(bank_read[b], 1)

            def late(units):
                units(0)
                keep("Vt", 2)
                psum()
                to_pe(copy(flat(av_t), banks[7][:, 0:T]))
                units(1)
                keep("b1", 3)
                keep("b2", 4)
                keep("AkV", 5)
                keep("At", 6)
                keep("Bt", 2)
                keep("b3", 4)
                units(2)
                keep("Kk", 5)
                from_dve()
                act.activation(prb[:, 0:P], prb[:, 0:P], ACT.Exp, bias=stat[:, 2:3], accum_out=stat[:, 4:5])
                to_dve(act.activation(prb[:, P:3 * P], prb[:, P:3 * P], ACT.Exp, bias=stat[:, 3:4],
                                      accum_out=stat[:, 5:6]))
                units(3)
                keep("b1", 4)
                keep("Y", 5)
                keep("Kt", 6)
                keep("N", 3)
                keep("Nt", 4)
                units(4)
                keep("b3", 4)
                psum()
                to_pe(copy(prt[:, :], banks[7][:, 0:3 * P]))
                units(5)
                units(6)
                keep("b2", 5)
                keep("b1", 6)
                for k in range(7, 11):
                    units(k)
                from_dve()
                psum()
                to_pe(copy(small["o"][:, :], banks[3][:, 0:T]))
                psum()
                to_pe(act.activation(small["gsq"][:, :], banks[4][:, 0:T], ACT.Square))
                units(11)
                psum()
                to_dve(act.activation(small["groot"][:, :], banks[6][:, 0:T], ACT.Sqrt, bias=con_("eps_gn"),
                                      scale=1.0 / 64))
                for k in range(12, 16):
                    units(k)

            ep4 = small["ep"][:, :].rearrange("p (c t) -> p c t", c=NCH)
            pair_counts = land(16) | {"unit": 16, ("fill", 0): 2, ("fill", 1): 2, "keys": 1, "qk": 1}
            for k in range(16):
                if k == 13:
                    from_dve()
                heads(k, 0)
                if 1 <= k <= 4:
                    for j in (2 * k - 2, 2 * k - 1):
                        psum()
                        act.activation(cum[:, j, :], banks[3 + j % 2][:, 0:T], ACT.Sigmoid, bias=col("w0", j))
                        to_pe(act.activation(icl[:, j, :], banks[5 + j % 2][:, 0:T], ACT.Sigmoid,
                                             bias=col("a0", j)))
                if k == 4:
                    to_dve(copy(spare[:, 1:2], icl[:, 0, 0:1]))
            with n.loop(HEADS_A - 1, {"psum": 21, "dve": 3} | pair_counts) as i:
                late(lambda k: heads(k, i + 1))
            late(queries)
            def query_squares(h):
                act.wait_ge(bank_read[h % 2], n.now(("fill", h % 2)))
                to_pe(act.activation(csq[:, :, :], cqs[:, 2 * h:2 * h + 2, :], ACT.Square))

            query_squares(0)
            for h in range(HEADS_C):
                split()
                psum()
                to_dve(act.activation(croot[:, :], banks[7][:, 0:T], ACT.Sqrt, bias=con_("eps6"),
                                      scale=1.0 / (2 * P)))
                if h == 2:
                    root_of_mean(memroot[:, :], banks[2][:, 0:T])
                split4(3)
                for c in MEM_QUARTERS[h]:
                    act.wait_ge(mem_in[c], 16)
                    cs = slice(4 * c, 4 * c + 4)
                    to_dve(act.activation(scratch3[:, cs, :], memx[:, cs, :], ACT.Square))
                from_dve()
                if h < HEADS_C - 1:
                    query_squares(h + 1)
                if h >= 2:
                    high_halves(scratch3, mh_hi, quarters=MEM_SPLIT[h])
                group_done()
                n.next(("fill", h % 2))
                act.activation(czs[:, 2 * h:2 * h + 2, :], p2(h % 2), ACT.Silu).then_inc(bank_read[h % 2], 1)

            def key_root():
                psum()
                to_dve(act.activation(mroot[:, :], banks[7][:, 0:T], ACT.Sqrt, bias=con_("eps6"),
                                      scale=1.0 / (2 * P)))

            for j in range(4):
                split()
                if j:
                    key_root()
                    from_dve()
                split4(3)
                group_done()
                n.next(("fill", j % 2))
                to_pe(act.activation(msq[:, :, :], p2(j % 2), ACT.Square))
                copy(cpair[:, :, :], p2(j % 2)).then_inc(bank_read[j % 2], 1)
            for j in range(4):
                split()
                if j == 0:
                    key_root()
                    from_dve()
                else:
                    psum()
                    to_pe(copy(mvt[:, :, (j - 1) * 2 * P:j * 2 * P],
                               banks[6][:, :].rearrange("p (c t) -> p c t", c=2)))
                split()
                from_dve()
                for q in range(2):
                    m = act.activation(cp[:, q, :], banks[3][:, q * T:(q + 1) * T], ACT.Exp, scale=1.0 / 16,
                                       bias=cstat[:, 2 + q:3 + q], accum_out=cstat[:, 4 + q:5 + q])
                to_dve(m)
                split4(2)
                group_done()
                n.next(("fill", j % 2))
                copy(cpair[:, :, :], p2(j % 2)).then_inc(bank_read[j % 2], 1)
                psum()
                to_pe(copy(flat(cpt[j]), banks[4][:, :]))
            psum()
            to_pe(copy(mvt[:, :, 6 * P:8 * P], banks[6][:, :].rearrange("p (c t) -> p c t", c=2)))
            act.wait_ge(head_written, HEADS_C)
            for c in range(6):
                to_dve(copy(ya_hi[:, 4 * c:4 * c + 4, :], yall[:, 4 * c:4 * c + 4, :]))
            with n.loop(4, land(36) | {"unit": 36, "dve": 2, ("fill", 0): 6, ("fill", 1): 6}) as i:
                for j in range(2):
                    for m3 in range(3):
                        split4()
                        group_done()
                        act.wait_ge(bank_read[1], n.now(("fill", 1)))
                        n.next(("fill", 0))
                        act.activation(gate[:, :, :], p2(0), ACT.Tanh, scale=0.5).then_inc(bank_read[0], 1)
                        split4(2)
                        n.next(("fill", 1))
                    from_dve()
                    to_dve(copy(mg_hi[:, bass.ds(i * 4 + 2 * j, 2), :], macc[:, :, :], 0.5))
            with n.loop(7, land(4) | {"unit": 4}):
                split4()

        @block.vector
        def _(dve):
            n = Counts(dve)
            slots = count()

            def split():
                slot = next(slots) % RING
                dve.wait_ge(hi_done, n.next("unit"))
                dve.tensor_tensor(w_lo[slot][:, :, :], raw[slot][:, :, :], w_hi[slot][:, :, :].bitcast(F32),
                                  ALU.subtract).then_inc(split_done, 1)

            def split4(k=4):
                for _ in range(k):
                    split()

            def group_done():
                dve.wait_ge(unit_used, n.now("unit") - RING)

            def psum(k=1):
                dve.wait_ge(psum_for_dve, n.next("psum", k))

            def from_act(k=1):
                dve.wait_ge(act_for_dve, n.next("act", k))

            def step(ins):
                ins.then_inc(dve_step, 1)
                n.next("step")

            def settle():
                dve.wait_ge(dve_step, n.now("step"))

            def to_pe(ins):
                ins.then_inc(dve_for_pe, 1)
                n.next("to_pe")

            def settle_pe():
                dve.wait_ge(dve_for_pe, n.now("to_pe"))

            def to_act(ins):
                ins.then_inc(dve_for_act, 1)
                n.next("to_act")

            def settle_act():
                dve.wait_ge(dve_for_act, n.now("to_act"))

            def read(ins, b):
                ins.then_inc(bank_read[b], 1)

            def own_bank(b):
                dve.wait_ge(bank_read[b], n.now(("fill", b)))

            def tt(out, x_, y_, op):
                return dve.tensor_tensor(out, x_, y_, op)

            def stt(out, x_, s, y_, op0, op1):
                return dve.scalar_tensor_tensor(out, x_, s, y_, op0, op1)

            def ts(out, x_, s0, s1=None, op0=ALU.mult, op1=None):
                return dve.tensor_scalar(out, x_, s0, s1, op0) if op1 is None else \
                    dve.tensor_scalar(out, x_, s0, s1, op0, op1)

            def low(lo, f, hi):
                return tt(lo, f, hi.bitcast(F32), ALU.subtract)

            def sum_quarter(c, sq, dst):
                from_act()
                if c == 1:
                    step(tt(dst[:, :, :], sq[:, 0:4, :], sq[:, 4:8, :], ALU.add))
                elif c:
                    step(tt(dst[:, :, :], dst[:, :, :], sq[:, 4 * c:4 * c + 4, :], ALU.add))
                settle()
                if c == 3:
                    to_pe(tt(dst[:, 0:2, :], dst[:, 0:2, :], dst[:, 2:4, :], ALU.add))

            def normalised(src, gain, f, hi, lo, rt, with_units=False, quarters=range(4)):
                def scaled(c):
                    for t in range(4 * c, 4 * c + 4):
                        m = stt(f[:, t, :], src[:, t, :], gain(t), rt[:, :], ALU.mult, ALU.mult)
                    to_act(m)

                scaled(quarters[0])
                for c in quarters:
                    if c < quarters[-1]:
                        scaled(c + 1)
                    if with_units:
                        split()
                    cs = slice(4 * c, 4 * c + 4)
                    from_act()
                    to_pe(low(lo[:, cs, :], f[:, cs, :], hi[:, cs, :]))

            def inverted(rt):
                from_act()
                step(dve.reciprocal(rt[:, :], rt[:, :]))
                settle()

            def running(tile, first, last=False, gained=False):
                xs = x[:, bass.ds(tile, 2), :]
                dst = acc_x if first else sq2
                step(tt(dst[:, :, :], xs, xs, ALU.mult))
                settle()
                if not first:
                    (to_pe if last and not gained else step)(tt(acc_x[:, :, :], acc_x[:, :, :], sq2[:, :, :], ALU.add))
                if gained:
                    for s in range(2):
                        g2 = gains[:, 0, bass.ds(tile + s, 1)]
                        if first:
                            m = ts(acc_g[:, s, :], acc_x[:, s, :], g2)
                        else:
                            m = stt(acc_g[:, s, :], sq2[:, s, :], g2, acc_g[:, s, :], ALU.mult, ALU.add)
                        step(m)
                settle()

            for c in range(4):
                sum_quarter(c, scratch, acc)
            dve.wait_ge(tab_in, 32)
            inverted(root)
            normalised(x, lambda t: col("norm_mix", t), scratch, h_hi, h_lo, root, with_units=True)

            def taps(dst, b, w0, w2):
                o = p2(b)
                for s in range(2):
                    step(stt(dst[s][:, 1:T], o[:, s, 0:T - 1], w0[s], dst[s][:, 1:T], ALU.mult, ALU.add))
                settle()
                return [lambda s=s: stt(dst[s][:, 0:T - 1], o[:, s, 1:T], w2[s], dst[s][:, 0:T - 1], ALU.mult,
                                        ALU.add) for s in range(2)]

            def hyena(p):
                dst = (x0, z1, zv)[p // 3]
                j = 2 * (p % 3)
                b = p % 2
                from_act()
                n.next(("fill", b))
                last = taps([dst[:, j + s, :] for s in range(2)], b, [col("hy_w", 2 * p + s) for s in range(2)],
                            [col("hy_w", 36 + 2 * p + s) for s in range(2)])
                step(last[0]())
                read(last[1](), b)

            def sine(b_, fr):
                u, k, r = fh[0][:, :], fh[1][:, :], fh[2][:, :]
                psum()
                step(ts(u, banks[3][0:64, 0:T], col(b_)[0:64, :], col(fr)[0:64, :], ALU.add, ALU.mult))
                settle()
                step(ts(k, u, float(1.0 / TWO_PI), ROUND, ALU.mult, ALU.add))
                settle()
                step(ts(k, k, ROUND, None, ALU.subtract))
                settle()
                step(stt(r, k, -PI_HI, u, ALU.mult, ALU.add))
                settle()
                step(stt(r, k, -PI_LO, r, ALU.mult, ALU.add))
                settle()
                to_act(ts(r, r, PI_CUT, -PI_CUT, ALU.min, ALU.max))

            split4()
            hyena(0)
            sine("f_b1", "f_fr1")
            split4()
            hyena(1)
            sine("f_b2", "f_fr2")
            split4()
            hyena(2)
            dve.wait_ge(tables_in, 3 * 16)
            for c in range(2):
                for q in range(4):
                    psum()
                    dst = f_fwd if q < 2 else f_bwd
                    qs = slice((q % 2) * 384, (q % 2 + 1) * 384)
                    to_pe(tt(dst[:, c, qs], banks[3 + q][:, 0:384], decay[:, c, qs], ALU.mult))
            settle_pe()
            dve.memset(f_bwd[0:1, 0, :], 0.0).then_inc(free_early, 1)
            dve.wait_ge(free_early, 1)
            step(tt(f_sum[:, :, :], f_fwd[:, :, :], f_bwd[:, :, :], ALU.add))
            settle()
            to_pe(tt(f_bwd[:, :, :], f_fwd[:, :, :], f_bwd[:, :, :], ALU.subtract))
            for p in range(3, 9):
                split4()
                hyena(p)
            own_bank(0)
            own_bank(1)
            settle()
            to_pe(tt(z1[:, :, :], z1[:, :, :], zv[:, :, :], ALU.mult))
            for p in (9, 10, 11):
                split4()
                n.next(("fill", p % 2))
            for i, (f, c) in enumerate(((0, 0), (0, 1), (1, 0), (1, 1))):
                psum()
                zr, zi = (banks[3 + 2 * (i % 2) + k][:, 0:384] for k in range(2))
                cs = slice(c * 384, (c + 1) * 384)
                kr, ki = k_re[:, f, cs], k_im[:, f, cs]
                if i == 0:
                    settle_pe()
                step(tt(prod[0][:, :], zr, kr, ALU.mult))
                step(tt(prod[1][:, :], zi, ki, ALU.mult))
                step(tt(prod[2][:, :], zr, ki, ALU.mult))
                to_pe(tt(prod[3][:, :], zi, kr, ALU.mult))
                settle()
                settle_pe()
                step(tt(kr, prod[0][:, :], prod[1][:, :], ALU.subtract))
                if i < 3:
                    step(tt(ki, prod[2][:, :], prod[3][:, :], ALU.add))
                else:
                    to_pe(tt(ki, prod[2][:, :], prod[3][:, :], ALU.add))
                settle()
            settle_pe()
            split4()
            n.next(("fill", 0))

            def y_low(tile, k, s, last=None):
                from_act()
                m = low(y_lo[:, tile:tile + k, :], y_part[:, s:s + k, :], y_hi[:, tile:tile + k, :])
                (to_pe if last else step)(m)

            for k in range(3):
                psum()
                for s in range(2):
                    step(stt(mix[:, s, :], z1[:, 2 * k + s, :], col("hy_skip", 2 * k + s),
                             banks[3 + k][:, s * T:(s + 1) * T], ALU.mult, ALU.add))
                settle()
                s = 2 * (k % 2)
                to_act(tt(y_part[:, s:s + 2, :], mix[:, :, :], x0[:, 2 * k:2 * k + 2, :], ALU.mult))
                settle_act()
                y_low(4 + 2 * k, 2, s)
                settle()
            dve.memset(pool_x[:, :, 0:8], 0.0)
            dve.memset(pool_x[:, :, 8 + T:PW], 0.0).then_inc(free_inv, 1)
            psum()
            for j in range(HY):
                m = stt(gv[:, j, :], banks[6][:, 0:T], -1.0 / D_HY, gv[:, j, :], ALU.mult, ALU.add)
            to_act(m)
            settle_act()
            split4()
            n.next(("fill", 1))
            from_act()
            step(dve.reciprocal(root[:, :], root[:, :]))
            settle()
            step(tt(gv[:, :, :], gv[:, :, :], bcast(root[:, :], HY), ALU.mult))
            settle()
            for j in range(HY):
                m = ts(gv[:, j, :], gv[:, j, :], col("gm_g", j), col("gm_b", j), ALU.mult, ALU.add)
            to_pe(m)
            split4()
            n.next(("fill", 0))
            own_bank(1)
            own_bank(0)
            dve.wait_ge(free_inv, 1)
            step(tt(pool_a[:, :, 1:PW], pool_x[:, :, 0:PW - 1], pool_x[:, :, 1:PW], ALU.add))
            settle()
            step(tt(pool_b[:, 1:4, 2:PW - 1], pool_a[:, 1:4, 1:PW - 2], pool_a[:, 1:4, 3:PW], ALU.add))
            settle()
            step(tt(pool_a[:, 2:4, 4:PW - 3], pool_b[:, 2:4, 2:PW - 5], pool_b[:, 2:4, 6:PW - 1], ALU.add))
            settle()
            step(tt(pool_b[:, 3:4, 8:PW - 7], pool_a[:, 3:4, 4:PW - 11], pool_a[:, 3:4, 12:PW - 3], ALU.add))
            settle()
            dve.wait_ge(inv_in, 16)
            for g in range(4):
                src = (pool_a, pool_b, pool_a, pool_b)[g]
                step(tt(pool_d[:, g, :], src[:, g, 8:8 + T], inv[:, g, :], ALU.mult))
            settle()
            to_pe(tt(pool_d[:, :, :], pool_d[:, :, :], pool_x[:, :, 8:8 + T], ALU.subtract))
            split4()
            n.next(("fill", 1))

            def gated(k, last=None):
                s = 2 * (k % 2)
                to_act(tt(y_part[:, s:s + 2, :], gu[:, 2 * k:2 * k + 2, :],
                          banks[3 + k][:, :].rearrange("p (s t) -> p s t", s=2), ALU.mult))
                settle_act()
                y_low(10 + 2 * k, 2, s, last)
                settle()

            own_bank(1)
            for k in range(3):
                psum()
                if k < 2:
                    gated(k)
            psum()
            for g in range(4):
                m = ts(y_part[:, g, :], banks[6 + g // 2][:, (g % 2) * T:(g % 2 + 1) * T], col("pool_b", g),
                       col("pool_scale", g), ALU.add, ALU.mult)
            to_act(m)
            settle_act()
            y_low(0, 4, 0, last=True)
            settle_pe()
            split4()
            n.next(("fill", 0))
            own_bank(0)
            gated(2, last=True)

            def residual(tile, b, out=None):
                group_done()
                n.next(("fill", b))
                t = x[:, bass.ds(tile, 2), :]
                dst = t if out is None else out[:, bass.ds(tile, 2), :]
                read(tt(dst, t, p2(b), ALU.add), b)

            step(dve.memset(acc_x[:, :, :], 0.0))
            step(tt(gains[:, 0, :], par[:, COL["norm_final"]:COL["norm_final"] + KT],
                    par[:, COL["norm_final"]:COL["norm_final"] + KT], ALU.mult))
            step(tt(gains[:, 1, :], par[:, COL["norm_final"]:COL["norm_final"] + KT],
                    par[:, COL["norm_g"]:COL["norm_g"] + KT], ALU.mult))
            with n.loop(4, {"unit": 8, ("fill", 0): 1, ("fill", 1): 1, "step": 4}) as i:
                for q, b in enumerate((1, 0)):
                    split4()
                    residual(i * 4 + 2 * q, b)
                    own_bank(b)
                    running(i * 4 + 2 * q, False)
            to_pe(dve.memset(lx[:, 0:1], 0.0))
            inverted(root2)
            normalised(x, lambda t: col("norm_ffn", t), scratch2, h_hi, h_lo, root2)
            for b in (2, 3):
                n.next(("fill", b))
                dve.memset(conv_m[:, 0, 0:1], 0.0).then_inc(bank_read[b], 1)
                own_bank(b)
            with n.loop(2, {"unit": U_UP + U_DOWN, "act": 3 * FF_HALF, "to_act": 2 * FF_HALF, "step": 2 * FF_HALF + 31,
                            ("fill", 0): 13, ("fill", 1): 13, ("fill", 2): 2, ("fill", 3): 2}) as half:
                with n.loop(FF_HALF // 2, {"unit": 8, "act": 6, "to_act": 4, "step": 4, ("fill", 0): 1,
                                           ("fill", 1): 1}) as j:
                    for q, b in enumerate((1, 0)):
                        base = half * (8 * FF_HALF) + j * 16 + 8 * q
                        o = conv_o[:, q, :, :]
                        split4()
                        from_act()
                        n.next(("fill", b))
                        last = taps([o[:, s, :] for s in range(2)], b, [col("ffn", base + 4 * s) for s in range(2)],
                                    [col("ffn", base + (4 * s + 2)) for s in range(2)])
                        to_act(last[0]())
                        read(last[1](), b)
                        from_act()
                        own_bank(b)
                        to_act(tt(conv_m[:, q, :], o[:, 0, :], o[:, 1, :], ALU.mult))
                        settle_act()
                        from_act()
                        low(m_lo[:, j * 2 + q, :], conv_m[:, q, :], m_hi[:, j * 2 + q, :])\
                            .then_inc(hidden_ready, 1)
                for q in range(4):
                    split4(11)
                    group_done()
                    for s, b in enumerate((1, 0) if q % 2 else (2, 3)):
                        n.next(("fill", b))
                        t = x[:, 4 * q + 2 * s:4 * q + 2 * s + 2, :]
                        read(tt(t, t, p2(b), ALU.add), b)
                    for s, b in enumerate((1, 0) if q % 2 else (2, 3)):
                        own_bank(b)
                        running(4 * q + 2 * s, q == 0 and s == 0, gained=True)
            to_pe(dve.memset(lx[:, 0:1], 0.0))
            dve.memset(stat[:, 0:1], 0.0).then_inc(free_lora, 1)
            from_act()
            step(ts(root3[:, :], banks[2][:, 0:T], 1e-6))
            settle()
            to_act(tt(root3[:, :], root3[:, :], banks[2][:, T:2 * T], ALU.add))
            settle_act()
            inverted(root3)
            normalised(x, lambda t: gains[:, 1, t:t + 1], scratch2, h_hi, h_lo, root3)
            step(dve.reciprocal(root2[:, :], root2[:, :]))
            split4()
            n.next(("fill", 1))
            own_bank(1)
            step(tt(lt[:, :], lx[:, 0:T], lx[:, 1:T + 1], ALU.subtract))
            settle()
            to_act(stt(lt[:, :], lt[:, :], col("mu_wa"), lx[:, 1:T + 1], ALU.mult, ALU.add))
            settle_act()
            for t in ("pr", "pk", "pv"):
                step(dve.memset(small[t][:, 0:1], 0.0))
            dve.memset(stat[:, 0:1], 0.0).then_inc(bias_used, 1)
            dve.wait_ge(bias_used, 1)

            ep4 = small["ep"][:, :].rearrange("p (c t) -> p c t", c=NCH)

            def residual_normed(ts_):
                for t in ts_:
                    step(stt(x[:, t, :], x[:, t, :], col("norm_final", t), root2[:, :], ALU.mult, ALU.mult))

            a4, b4_ = (t[:, :, :].rearrange("p g (c t) -> p (g c) t", t=CHUNK) for t in (cum, ping))

            def prefix(k):
                src, dst = ((a4, b4_), (b4_, a4))[k % 2]
                s = 1 << k
                step(tt(dst[:, :, s:CHUNK], src[:, :, s:CHUNK], src[:, :, 0:CHUNK - s], ALU.add))
                step(dve.tensor_copy(dst[:, :, 0:s], src[:, :, 0:s]))
                settle()

            def c4(t):
                return t.rearrange("p (c t) -> p c t", c=NCH)

            def flat(t):
                return t[:, :, :].rearrange("p c t -> p (c t)")

            sm = small
            shift = lambda t: (sm[t][:, 0:T], sm[t][:, 1:T + 1])
            ident4 = bcast(con_("ident"), NCH)
            def heads(k, g):
                rw = lambda c: col("rwkv", g * RW_COLS + c)
                icl_g = icl[:, bass.ds(g, 1), :].rearrange("p o t -> p (o t)")
                split()
                if k % 4 == 3:
                    n.next(("fill", (k // 4) % 2))
                if k == 6:
                    own_bank(0)
                    prev, now = shift("pr")
                    step(tt(sm["t0"][:, :], prev, now, ALU.subtract))
                    prevk, nowk = shift("pk")
                    step(tt(sm["k2"][:, :], prevk, nowk, ALU.subtract))
                    settle()
                    step(stt(sm["r"][:, :], sm["t0"][:, :], rw(MU_R), now, ALU.mult, ALU.add))
                    step(stt(sm["k0"][:, :], sm["k2"][:, :], rw(MU_K), nowk, ALU.mult, ALU.add))
                    settle()
                    step(ts(sm["kk"][:, :], sm["k0"][:, :], rw(K_K)))
                    step(ts(sm["t0"][:, :], icl_g, 1.0, rw(K_A), ALU.subtract, ALU.mult))
                    settle()
                    step(tt(sm["sq"][:, :], sm["kk"][:, :], sm["kk"][:, :], ALU.mult))
                    step(stt(sm["k2"][:, :], sm["t0"][:, :], 1.0, sm["k0"][:, :], ALU.add, ALU.mult))
                    settle()
                    stt(sm["rk"][:, :], sm["r"][:, :], rw(R_K), sm["k2"][:, :], ALU.mult, ALU.mult)\
                        .then_inc(keys_ready, 1)
                    n.next("keys")
                if k == 8:
                    from_act()
                    prev, now = shift("pv")
                    step(tt(sm["t0"][:, :], prev, now, ALU.subtract))
                    read(stt(sm["k0"][:, :], sm["k0"][:, :], 1.0, p2(1)[:, 1, :], ALU.add, ALU.mult), 1)
                    settle()
                    step(stt(sm["v"][:, :], sm["t0"][:, :], rw(MU_V), now, ALU.mult, ALU.add))
                if k == 9:
                    dve.wait_ge(head_sums, n.next("sums"))
                    to_act(ts(sm["sq"][:, :], banks[7][:, 0:T], 1e-24, None, ALU.max))
                    settle()
                    tt(sm["rk"][:, :], banks[7][:, T:2 * T], sm["v"][:, :], ALU.mult).then_inc(sums_read, 1)
                if k == 10:
                    from_act()
                    step(dve.reciprocal(sm["sq"][:, :], sm["sq"][:, :]))
                    settle()
                    step(tt(sm["kk"][:, :], sm["kk"][:, :], sm["sq"][:, :], ALU.mult))
                    settle()
                    step(tt(sm["t0"][:, :], sm["kk"][:, :], icl_g, ALU.mult))
                if k == 13:
                    dve.wait_ge(sums_read, n.now("sums"))
                    settle()
                    step(dve.tensor_copy(sm["bon"][:, :], sm["rk"][:, :]))
                    step(dve.tensor_copy(sm["bz"][:, :], sm["k0"][:, :]))
                    from_act(2)
                    step(stt(a_rt[:, :, 0, :], c4(sm["kk"][:, :]), -1.0, ep4[:, :, 0:CHUNK], ALU.mult, ALU.mult))
                    settle()
                    for h in range(2):
                        hp = slice(64 * h, 64 * h + 64)
                        step(dve.tensor_copy(bd["a"][hp, :, hp], a_rt[hp, :, 0, :]))
                        step(tt(bd["b"][hp, :, hp], c4(sm["t0"][hp, :]), c4(sm["en"][hp, :]), ALU.mult))
                        step(tt(bd["k"][hp, :, hp], c4(sm["k2"][hp, :]), c4(sm["en"][hp, :]), ALU.mult))
                    to_pe(tt(a_rt[:, :, 1, :], c4(sm["r"][:, :]), ep4[:, :, 1:CHUNK + 1], ALU.mult))

            def queries(k):
                split()
                if k == 9:
                    dve.memset(stat[:, 9:10], 0.0).then_inc(free_mem, 1)
                if k % 4 == 3:
                    n.next(("fill", (k // 4) % 2))

            def y_tile(i):
                return yall[:, bass.ds(i, 1), :].rearrange("p o t -> p (o t)")

            def late(units, g):
                units(0)
                psum()

                def masked(name, bank):
                    for h in range(2):
                        hp = slice(64 * h, 64 * h + 64)
                        mask = con_({"Nt": "upper_in", "Kt": "upper"}[name])[hp, hp]
                        step(tt(bd[name][hp, :, hp], b4(bank)[hp, :, 0:CHUNK],
                                mask.unsqueeze(1).broadcast_to([64, NCH, CHUNK]), ALU.mult))

                masked("Nt", 3)
                step(tt(BK[:, 0, :, :], b4(3)[:, :, CHUNK:P], bcast(con_("upper_eq"), NCH), ALU.mult))
                psum()
                step(tt(bd["N"][:, :, :], b4(4), bcast(con_("lower_in"), NCH), ALU.mult))
                to_pe(tt(bd["No"][:, :, :], b4(4), bcast(con_("lower_out"), NCH), ALU.mult))
                psum()
                masked("Kt", 5)
                settle()
                step(tt(bd["Q"][:, :, :], bd["Nt"][:, :, :], ident4, ALU.add))
                to_pe(tt(BK[:, 1, :, :], b4(5)[:, :, CHUNK:P], bcast(con_("upper_eq"), NCH), ALU.mult))
                settle()
                from_act()
                read(stt(az[:, :], az[:, :], 1.0, p2(1)[:, 1, :], ALU.add, ALU.mult), 1)
                step(dve.reciprocal(flat(qr), flat(qr)))
                settle()
                step(stt(qk[:, 0, :], qk[:, 0, :], col("aq_g"), qr[:, 0, :], ALU.mult, ALU.mult))
                to_pe(stt(qk[:, 1, :], qk[:, 1, :], col("ak_g"), qr[:, 1, :], ALU.mult, ALU.mult))
                units(1)
                psum()
                to_pe(tt(bd["Q"][:, :, :], bd["Q"][:, :, :], b4(3), ALU.add))
                psum()
                dve.wait_ge(bias_in, 16 * n.next("bias"))
                stt(prb[:, :], banks[7][:, 0:3 * P], float(P) ** -0.5, bias_t[:, :], ALU.mult, ALU.add)\
                    .then_inc(bias_used, 1)
                dve.wait_ge(bias_used, n.now("bias") + 1)
                step(dve.memset(prb[0:64, 64:P], NEG))
                step(dve.memset(prb[0:64, P + 192:3 * P], NEG))
                settle()
                step(dve.tensor_reduce(stat[:, 0:1], prb[:, 0:P], AX_X, ALU.max))
                step(dve.tensor_reduce(stat[:, 1:2], prb[:, P:3 * P], AX_X, ALU.max))
                settle()
                to_act(ts(stat[:, 2:4], stat[:, 0:2], -1.0))
                units(2)
                settle_pe()
                psum()
                to_pe(tt(bd["Q"][:, :, :], bd["Q"][:, :, :], b4(3), ALU.add))
                units(3)
                psum()
                step(dve.tensor_copy(bd["b2"][:, :, :], b4(3)))
                to_pe(tt(bd["F"][:, :, :], b4(3), ident4, ALU.add))
                from_act()
                step(dve.reciprocal(stat[:, 6:8], stat[:, 4:6]))
                settle()
                step(ts(prb[:, 0:P], prb[:, 0:P], stat[:, 6:7]))
                to_pe(ts(prb[:, P:3 * P], prb[:, P:3 * P], stat[:, 7:8]))
                settle_pe()
                units(4)
                psum()
                to_pe(tt(bd["F"][:, :, :], bd["F"][:, :, :], b4(3), ALU.add))
                units(5)
                settle_pe()
                psum()
                to_pe(tt(bd["F"][:, :, :], bd["F"][:, :, :], b4(3), ALU.add))
                units(6)

                def decay_of(c):
                    return ep4[:, c, CHUNK:CHUNK + 1]

                def solved(c):
                    if c < NCH - 1:
                        step(ts(S_dec[:, :], S[:, c % 2, :], decay_of(c)))
                    psum()
                    to_pe(tt(SA[:, c % 2, :], banks[2][:, 0:P], bd["b1"][:, c, :], ALU.add))
                    settle()

                def state(c):
                    psum()
                    to_pe(stt(S[:, (c + 1) % 2, :], banks[4][:, 0:P], decay_of(c), S_dec[:, :], ALU.mult, ALU.add))
                    settle_pe()

                psum()
                to_pe(ts(S[:, 1, :], banks[4][:, 0:P], decay_of(0)))
                settle_pe()
                psum()
                dve.wait_ge(bank_read[1], n.now(("fill", 1)))
                step(stt(y_tile(g), banks[5][:, 0:T], 0.5, az[:, :], ALU.mult, ALU.mult))
                solved(1)
                state(1)
                units(7)
                solved(2)
                state(2)
                units(8)
                solved(3)
                units(9)
                settle()
                to_act(dve.memset(stat[:, 8:9], 0.0))
                units(10)
                units(11)
                from_act()
                step(dve.reciprocal(sm["groot"][:, :], sm["groot"][:, :]))
                settle()
                step(tt(sm["gk"][:, :], banks[4][:, 0:T], sm["groot"][:, :], ALU.mult))
                settle()
                step(ts(sm["gk"][:, :], sm["gk"][:, :], col("rwkv", g * RW_COLS + LN_W),
                        col("rwkv", g * RW_COLS + LN_B), ALU.mult, ALU.add))
                settle()
                step(tt(sm["gk"][:, :], sm["gk"][:, :], sm["bon"][:, :], ALU.add))
                settle()
                step(stt(y_tile(g + 8), sm["gk"][:, :], 0.5, sm["bz"][:, :], ALU.mult, ALU.mult))
                for k in range(12, 16):
                    units(k)

            for k in range(16):
                heads(k, 0)
                if k < 4:
                    residual_normed(range(4 * k, 4 * k + 4))
                    settle()
                if k == 4:
                    from_act()
                if 5 <= k <= 10:
                    prefix(k - 5)
                if k == 11:
                    for t in ("a", "b", "k", "Nt", "Kt"):
                        step(dve.memset(bd[t][:, :, :], 0.0))
                    step(dve.memset(ep4[:, :, 0:1], 1.0))
                    settle()
                    to_act(dve.memset(bd["v"][:, :, :], 0.0))
            with n.loop(HEADS_A - 1, {"unit": 16, "psum": 16, "act": 7, "step": 46, "to_pe": 16, "to_act": 3,
                                      ("fill", 0): 2, ("fill", 1): 2, "bias": 1, "keys": 1, "sums": 1}) as i:
                late(lambda k: heads(k, i + 1), i)
            late(queries, HEADS_A - 1)
            for h in range(HEADS_C):
                split()
                from_act()
                step(dve.reciprocal(croot[:, :], croot[:, :]))
                settle()
                for s in range(2):
                    q = cqs[:, 2 * h + s, :]
                    m = stt(q, q, col("cq_g", s), croot[:, :], ALU.mult, ALU.mult)
                    (step, to_act)[s](m)
                split4(3)
                for c in MEM_QUARTERS[h]:
                    sum_quarter(c, scratch3, memacc)
                if h == 2:
                    inverted(memroot)
                    for c in range(4):
                        dve.wait_ge(mem_in[c], 16)
                if h >= 2:
                    normalised(memx, lambda t: col("mem_g", t), scratch3, mh_hi, mh_lo, memroot,
                               quarters=MEM_SPLIT[h])
                n.next(("fill", h % 2))

            def keys(j):
                from_act()
                step(dve.reciprocal(mroot[:, :], mroot[:, :]))
                settle()
                for s in range(2):
                    m = stt(mk[:, 2 * j + s, :], cpair[:, s, :], col("ck_g", s), mroot[:, :], ALU.mult, ALU.mult)
                    (step, to_act)[s](m)

            for j in range(4):
                split()
                if j:
                    keys(j - 1)
                split4(3)
                n.next(("fill", j % 2))
                own_bank(j % 2)
            for j in range(4):
                split()
                if j == 0:
                    keys(3)
                    settle_act()
                    to_pe(dve.memset(stat[:, 0:1], 0.0))
                split()
                psum()
                step(dve.tensor_reduce(cstat[:, 0:2], banks[3][:, :].rearrange("p (q t) -> p q t", q=2), AX_X,
                                       ALU.max))
                settle()
                to_act(ts(cstat[:, 2:4], cstat[:, 0:2], -1.0 / 16))
                from_act()
                step(dve.reciprocal(cstat[:, 6:8], cstat[:, 4:6]))
                settle()
                step(ts(cp[:, 0, :], cp[:, 0, :], cstat[:, 6:7]))
                to_pe(ts(cp[:, 1, :], cp[:, 1, :], cstat[:, 7:8]))
                split4(2)
                n.next(("fill", j % 2))
            for h in range(HEADS_C):
                psum()
                own_bank(h % 2)
                stt(yall[:, 16 + 2 * h:18 + 2 * h, :],
                    banks[(3, 4, 5, 7)[h]][:, :].rearrange("p (s t) -> p s t", s=2), 1.0,
                    czs[:, 2 * h:2 * h + 2, :], ALU.mult, ALU.mult).then_inc(head_written, 1)
            dve.wait_ge(head_written, HEADS_C)
            for c in range(6):
                from_act()
                cs = slice(4 * c, 4 * c + 4)
                m = low(ya_lo[:, cs, :], yall[:, cs, :], ya_hi[:, cs, :])
            to_pe(m)
            settle_pe()
            with n.loop(4, {"unit": 36, "act": 2, "to_act": 2, "step": 2, ("fill", 0): 6, ("fill", 1): 6,
                            "merged": 2}) as i:
                for j in range(2):
                    for m3 in range(3):
                        split4()
                        n.next(("fill", 0))
                        split4(2)
                        own_bank(0)
                        group_done()
                        n.next(("fill", 1))
                        dst = mtmp if m3 else macc
                        read(stt(dst[:, :, :], gate[:, :, :], 1.0, p2(1), ALU.add, ALU.mult), 1)
                        own_bank(1)
                        if m3:
                            (to_act if m3 == 2 else step)(tt(macc[:, :, :], macc[:, :, :], mtmp[:, :, :], ALU.add))
                            settle()
                    settle_act()
                    from_act()
                    hi = mg_hi[:, bass.ds(i * 4 + 2 * j, 2), :].bitcast(F32)
                    stt(mg_lo[:, bass.ds(i * 4 + 2 * j, 2), :], macc[:, :, :], 0.5, hi, ALU.mult, ALU.subtract)\
                        .then_inc(merged_ready, 1)
                    dve.wait_ge(merged_ready, n.next("merged"))
            with n.loop(3, {"unit": 8, ("fill", 0): 1, ("fill", 1): 1}) as i:
                for b in (0, 1):
                    split4()
                    residual(i * 4 + 2 * b, b, obuf)
            split4()
            residual(12, 0, obuf)
            dve.wait_ge(unit_used, UNITS)
            read(tt(obuf[:, 14:16, :], x[:, 14:16, :], p2(1), ALU.add), 1)


SHAPES = {"units": (UNITS, P, UK * UN), "xT": (P, KT, T), "memT": (P, KT, T), "par": (P, NPAR),
          "con": (P, NCONST), "feat": (33, T), "fw1": (33, 64), "fw2": (64, 64), "fw3": (64, 2 * D_HY),
          "dft": (P, 4, 2, T), "decay": (P, 2, D_HY), "ws": (P, HY, P), "pw": (P, 4, P), "bs": (1, HY * P),
          "inv": (P, 4, T), "lora": (P, 1024), "bias": (HEADS_A, P, 384)}


def lay_out(v):
    def tiles(vec):
        return np.ascontiguousarray(vec.reshape(-1, P).T)

    def units(w, cols):
        w = w[:, cols].reshape(-1, UK, P, len(cols) // UN, UN)
        return w.transpose(3, 0, 2, 1, 4).reshape(-1, P, UK * UN)

    def cols_of(tile_list):
        return np.concatenate([np.arange(t * P, (t + 1) * P) for t in tile_list])

    def down(w, half):
        w = w[half * FF_HALF * P:(half + 1) * FF_HALF * P].reshape(11, 2, P, 4, 512)
        return w.transpose(3, 0, 2, 1, 4).reshape(-1, P, UK * UN)

    w_in = v["w_in"][0]
    order = list(range(4, 22)) + list(range(28, 34)) + [22, 23] + list(range(4)) + list(range(24, 28))
    parts = [units(w_in, cols_of(order)), units(v["w_out"][0], np.arange(D))]
    up = v["ffn_w_up"][0]
    for half in range(2):
        ts_ = [t for j in range(half * FF_HALF, (half + 1) * FF_HALF) for t in (j, FF_TILES + j)]
        parts += [units(up, cols_of(ts_)), down(v["ffn_w_down"][0], half)]
    w2 = v["w_in_2"][0]
    AQ, AK, AV, AZ, BR, BK_, BV, BZ = (8 * i for i in range(8))
    lora = np.zeros((D, UN), np.float32)
    lora[:, 0:P] = w2[:, 64 * P:65 * P]
    parts.append(units(lora, np.arange(UN)))
    loop = [t for g in range(8) for t in (BR + g, BK_ + g, BV + g, BZ + g, AQ + g, AK + g, AV + g, AZ + g)]
    parts.append(units(w2, cols_of(loop)))
    CQ, GA = 65, 81
    parts.append(units(w2, cols_of(range(CQ, CQ + 16))))
    parts.append(units(v["w_mem_kv_2"][0], np.arange(D)))
    ups = [v[n][0] for n in ("w_up_a_2", "w_up_b_2", "w_up_c_2")]
    for j in range(8):
        for m in range(3):
            t = GA + 16 * m + 2 * j
            parts.append(units(w2, cols_of([t, t + 1])))
            parts.append(units(ups[m], cols_of([2 * j, 2 * j + 1])))
    parts.append(units(v["w_o_2"][0], np.arange(D)))
    stream = np.concatenate(parts)

    par = np.zeros((P, NPAR), np.float32)

    def put(name, cols, at=0):
        par[:cols.shape[0], COL[name] + at:COL[name] + at + cols.shape[1]] = cols

    put("norm_mix", tiles(v["norm_mix"][0]))
    put("pool_b", tiles(v["pool_b"][0]))
    put("pool_scale", tiles(v["pool_scale"][0]))
    for k in range(3):
        put("hy_w", tiles(v["hy_short_w"][0][k]), 18 * k)
    put("hy_b", tiles(v["hy_short_b"][0]))
    put("hy_skip", tiles(v["hy_skip"][0]))
    put("gm_g", tiles(v["gm_ln_g"][0]))
    put("gm_b", tiles(v["gm_ln_b"][0]))
    put("norm_ffn", tiles(v["norm_ffn"][0]))
    ffn = np.stack([tiles(t) for t in (*v["ffn_conv_w"][0], v["ffn_conv_b"][0])], axis=-1)
    ffn = ffn.reshape(P, 2, FF_TILES, 4).transpose(0, 2, 1, 3).reshape(P, -1)
    put("ffn", ffn)
    put("norm_final", tiles(v["norm_final"]))
    put("norm_g", tiles(v["norm_g_2"][0]))
    put("mem_g", tiles(v["mem_norm_g_2"][0]))
    mu = v["b_mu_rkv_2"][0]
    rows = [mu[0], mu[1], mu[2], v["b_k_k_2"][0], v["b_k_a_2"][0], v["b_r_k_2"][0].reshape(-1), v["b_ln_w_2"][0],
            v["b_ln_b_2"][0]]
    for k, r in enumerate(rows):
        par[:, COL["rwkv"] + k:COL["rwkv"] + 80:RW_COLS] = tiles(r)
    put("mu_wa", np.concatenate([v["b_mu_w_2"][0], v["b_mu_a_2"][0]])[:, None])
    put("w0", tiles(v["b_w0_2"][0]))
    put("a0", tiles(v["b_a0_2"][0]))
    for name, key in (("aq_g", "a_q_g_2"), ("ak_g", "a_k_g_2"), ("cq_g", "c_q_g_2"), ("ck_g", "c_k_g_2")):
        put(name, tiles(v[key][0]))
    for name, key in (("f_b1", "hy_filt_b1"), ("f_fr1", "hy_filt_freq1"), ("f_b2", "hy_filt_b2"),
                      ("f_fr2", "hy_filt_freq2")):
        put(name, v[key][0][:, None])

    dft, feat, decay, inv = hyena_tables()
    q, k = np.arange(T)[:, None], np.arange(T)[None, :]
    rel = v["a_rel_bias_2"][0][:, np.clip(q - k, -P, P) + P]
    bias = np.concatenate([rel[:, 0:P, 0:P], rel[:, P:T, :]], axis=2)
    out = {
        "units": stream,
        "xT": v["x"][0].T.reshape(KT, P, T).transpose(1, 0, 2),
        "memT": v["mem_2"][0].T.reshape(KT, P, T).transpose(1, 0, 2),
        "par": par, "con": const_tables(), "feat": feat, "fw1": v["hy_filt_w1"][0], "fw2": v["hy_filt_w2"][0],
        "fw3": v["hy_filt_w3"][0], "dft": dft, "decay": decay, "inv": inv,
        "ws": v["gm_w_s"][0].transpose(2, 0, 1), "pw": v["pool_w"][0].transpose(1, 0, 2),
        "bs": v["gm_b_s"][0].reshape(1, -1),
        "lora": np.concatenate([v["b_w2_2"][0], v["b_a2_2"][0]]),
        "bias": bias,
    }
    return {name: np.ascontiguousarray(t) for name, t in out.items()}


def kernel(**inputs):
    import concourse.bacc as bacc
    from concourse.bass_utils import run_bass_kernel_spmd

    arrays = lay_out({k: np.asarray(v) for k, v in inputs.items()})
    nc = bacc.Bacc("TRN2", target_bir_lowering=False, num_devices=1)
    aps = {}
    for name, shape in SHAPES.items():
        assert arrays[name].shape == shape, (name, arrays[name].shape, shape)
        aps[name] = nc.dram_tensor(f"in_{name}", shape, F32, kind="ExternalInput").ap()
    aps["out"] = nc.dram_tensor("out_y", (P, KT, T), F32, kind="ExternalOutput").ap()
    build(nc, aps)
    r = run_bass_kernel_spmd(nc, [{f"in_{name}": t for name, t in arrays.items()}], core_ids=[0])
    y = r.results[0]["out_y"]
    return np.ascontiguousarray(y.transpose(1, 0, 2).reshape(D, T).T)[None]
```
